# Optimizing a Trainium2 kernel written in Bass

```python
import math
import jax, jax.numpy as jnp
from jax import lax
import numpy as np

D_MODEL = 1024
BATCH = 1
SEQ = 128
DEPTH = 2
DEC_BATCH = 1
DEC_SEQ = 256
PAST_LEN = 128

GRID_W = 64
N_MIXERS = 2
N_ATTN_LAYERS = (DEPTH + 1) // 2
N_FOURIER_LAYERS = DEPTH // 2
N_HEADS = 8
HEAD_DIM = 64
V_DIM = 2 * HEAD_DIM
Q_WIDTH = N_HEADS * 2 * HEAD_DIM
K_WIDTH = N_HEADS * 2 * HEAD_DIM
V_WIDTH = N_HEADS * V_DIM
QKV_WIDTH = Q_WIDTH + K_WIDTH + V_WIDTH
ROPE_BASE = 10000.0
Q_BLOCK = 128
N_FOURIER_GROUPS = 8
FOURIER_GROUP_DIM = D_MODEL // N_FOURIER_GROUPS
N_EXPERT_GROUPS = 4
EXPERTS_PER_GROUP = 8
N_EXPERTS = N_EXPERT_GROUPS * EXPERTS_PER_GROUP
D_EXPERT = 256
TOP_K_IN_GROUP = 2
N_MOD = 6
LN_EPS = 1e-5
DEEPNORM_ALPHA = (2.0 * DEPTH) ** 0.25
DEEPNORM_BETA = (8.0 * DEPTH) ** -0.25

kernel_name = "hybrid_diffattn_fnet_hmoe_diffusion_step"

def _layernorm(x):
    xf = x.astype(jnp.float32)
    mu = jnp.mean(xf, axis=-1, keepdims=True)
    var = jnp.mean(jnp.square(xf - mu), axis=-1, keepdims=True)
    return ((xf - mu) * lax.rsqrt(var + LN_EPS)).astype(x.dtype)

def _modulate(x, shift, scale):
    return _layernorm(x) * (1 + scale) + shift

def _post_norm(x, out, gain, bias):
    return _layernorm(DEEPNORM_ALPHA * x + out) * gain + bias

def _ada(cond, w_ada, b_ada):
    m = (jax.nn.silu(cond) @ w_ada + b_ada)[..., None, :]
    return jnp.split(m, N_MOD, axis=-1)

def _rope_2d_tables(n_rows):
    nf = HEAD_DIM // 4
    rows = jnp.repeat(jnp.arange(n_rows, dtype=jnp.float32), GRID_W)
    cols = jnp.tile(jnp.arange(GRID_W, dtype=jnp.float32), n_rows)
    inv = ROPE_BASE ** (-jnp.arange(nf, dtype=jnp.float32) / nf)
    ang = jnp.stack([rows[:, None] * inv, cols[:, None] * inv], axis=1)
    return jnp.cos(ang), jnp.sin(ang)

def _apply_rope_2d(x, cos, sin):
    shp = x.shape
    nf = HEAD_DIM // 4
    xa = x.reshape(shp[:-1] + (2, HEAD_DIM // 2))
    x1, x2 = xa[..., :nf], xa[..., nf:]
    c = cos[None, :, None, None].astype(x.dtype)
    s = sin[None, :, None, None].astype(x.dtype)
    out = jnp.concatenate([x1 * c - x2 * s, x1 * s + x2 * c], axis=-1)
    return out.reshape(shp)

def _diff_lambda(lq1, lk1, lq2, lk2, lam_init):
    e1 = jnp.exp(jnp.sum(lq1.astype(jnp.float32) * lk1.astype(jnp.float32)))
    e2 = jnp.exp(jnp.sum(lq2.astype(jnp.float32) * lk2.astype(jnp.float32)))
    return e1 - e2 + lam_init

def _qkv(h, w_qkv):
    b, s, _ = h.shape
    qkv = h @ w_qkv
    q = qkv[..., :Q_WIDTH].reshape(b, s, N_HEADS, 2, HEAD_DIM)
    k = qkv[..., Q_WIDTH:Q_WIDTH + K_WIDTH].reshape(b, s, N_HEADS, 2, HEAD_DIM)
    v = qkv[..., Q_WIDTH + K_WIDTH:].reshape(b, s, N_HEADS, V_DIM)
    return q, k, v

def _diff_attention(q, k, v, lam):
    b, sq = q.shape[:2]
    nb = sq // Q_BLOCK
    qb = q.reshape(b, nb, Q_BLOCK, N_HEADS, 2, HEAD_DIM).transpose(1, 0, 2, 3, 4, 5)
    scale = HEAD_DIM ** -0.5

    def block(qblk):
        s = jnp.einsum('bqhjd,bkhjd->jbhqk', qblk, k).astype(jnp.float32) * scale
        p = jax.nn.softmax(s, axis=-1)
        pd = (p[0] - lam * p[1]).astype(v.dtype)
        return jnp.einsum('bhqk,bkhv->bqhv', pd, v)

    out = lax.map(block, qb)
    return out.transpose(1, 0, 2, 3, 4).reshape(b, sq, N_HEADS, V_DIM)

def _attn_output(o, gain, lam_init, w_o):
    b, s = o.shape[:2]
    of = o.astype(jnp.float32)
    of = of * lax.rsqrt(jnp.mean(jnp.square(of), axis=-1, keepdims=True) + LN_EPS)
    o = of.astype(o.dtype) * gain * (1.0 - lam_init)
    return o.reshape(b, s, D_MODEL) @ w_o

def _fourier_mix(h, w_out):
    b, s, _ = h.shape
    hg = h.reshape(b, s, N_FOURIER_GROUPS, FOURIER_GROUP_DIM).astype(jnp.float32)
    f = jnp.fft.fft2(hg, axes=(1, 3), norm="ortho").real
    return f.reshape(b, s, D_MODEL).astype(h.dtype) @ w_out

def _hier_moe(h, w_rg, w_re, w_g, w_u, w_d):
    b, s, d = h.shape
    t = h.reshape(b * s, d)
    pg = jax.nn.softmax((t @ w_rg).astype(jnp.float32), axis=-1)
    g_prob, g_idx = lax.top_k(pg, 1)
    le = (t @ w_re).astype(jnp.float32).reshape(-1, N_EXPERT_GROUPS, EXPERTS_PER_GROUP)
    g_onehot = jax.nn.one_hot(g_idx[:, 0], N_EXPERT_GROUPS, dtype=jnp.float32)
    le_sel = jnp.einsum('nge,ng->ne', le, g_onehot)
    pe = jax.nn.softmax(le_sel, axis=-1)
    e_prob, e_idx = lax.top_k(pe, TOP_K_IN_GROUP)
    e_w = e_prob / jnp.sum(e_prob, axis=-1, keepdims=True) * g_prob
    e_global = g_idx * EXPERTS_PER_GROUP + e_idx
    combine = jnp.sum(jax.nn.one_hot(e_global, N_EXPERTS, dtype=jnp.float32) * e_w[..., None], axis=1)
    a = jnp.einsum('nd,edf->nef', t, w_g)
    u = jnp.einsum('nd,edf->nef', t, w_u)
    act = jax.nn.silu(a) * u * combine[..., None].astype(t.dtype)
    y = jnp.einsum('nef,efd->nd', act, w_d)
    return y.reshape(b, s, d)

def setup_inputs(seed: int = 0) -> dict:
    key = jax.random.key(seed)
    ks = jax.random.split(key, 24)
    f32 = jnp.float32
    d = D_MODEL

    def nrm(k, shape, scale):
        return jax.random.normal(k, shape, f32) * scale

    return {
        "x_prompt": nrm(ks[0], (BATCH, SEQ, d), 1.0),
        "x_sample": nrm(ks[1], (DEC_BATCH, DEC_SEQ, d), 1.0),
        "cache_k": nrm(ks[2], (DEC_BATCH, N_ATTN_LAYERS, PAST_LEN, N_HEADS, 2 * HEAD_DIM), 1.0),
        "cache_v": nrm(ks[3], (DEC_BATCH, N_ATTN_LAYERS, PAST_LEN, N_HEADS, V_DIM), 1.0),
        "c": nrm(ks[4], (DEC_BATCH, d), 1.0),
        "c_ctx": nrm(ks[5], (d,), 1.0),
        "w_ada": nrm(ks[6], (DEPTH, d, N_MOD * d), d ** -0.5),
        "b_ada": nrm(ks[7], (DEPTH, N_MOD * d), 0.02),
        "ln_gain": 1.0 + nrm(ks[8], (DEPTH, 2, d), 0.02),
        "ln_bias": nrm(ks[9], (DEPTH, 2, d), 0.02),
        "w_qkv": nrm(ks[10], (N_ATTN_LAYERS, d, QKV_WIDTH), d ** -0.5),
        "w_attn_out": nrm(ks[11], (N_ATTN_LAYERS, V_WIDTH, d), V_WIDTH ** -0.5 * DEEPNORM_BETA),
        "lambda_q1": nrm(ks[12], (N_ATTN_LAYERS, HEAD_DIM), 0.1),
        "lambda_k1": nrm(ks[13], (N_ATTN_LAYERS, HEAD_DIM), 0.1),
        "lambda_q2": nrm(ks[14], (N_ATTN_LAYERS, HEAD_DIM), 0.1),
        "lambda_k2": nrm(ks[15], (N_ATTN_LAYERS, HEAD_DIM), 0.1),
        "subln_gain": 1.0 + nrm(ks[16], (N_ATTN_LAYERS, V_DIM), 0.02),
        "w_fourier_out": nrm(ks[17], (N_FOURIER_LAYERS, d, d), d ** -0.5 * DEEPNORM_BETA),
        "w_router_group": nrm(ks[18], (DEPTH, d, N_EXPERT_GROUPS), d ** -0.5),
        "w_router_expert": nrm(ks[19], (DEPTH, d, N_EXPERTS), d ** -0.5),
        "w_expert_gate": nrm(ks[20], (DEPTH, N_EXPERTS, d, D_EXPERT), d ** -0.5),
        "w_expert_up": nrm(ks[21], (DEPTH, N_EXPERTS, d, D_EXPERT), d ** -0.5),
        "w_expert_down": nrm(ks[22], (DEPTH, N_EXPERTS, D_EXPERT, d), D_EXPERT ** -0.5 * DEEPNORM_BETA),
    }

def reference(x_prompt, x_sample, cache_k, cache_v, c, c_ctx, w_ada, b_ada, ln_gain, ln_bias,
              w_qkv, w_attn_out, lambda_q1, lambda_k1, lambda_q2, lambda_k2, subln_gain,
              w_fourier_out, w_router_group, w_router_expert, w_expert_gate, w_expert_up,
              w_expert_down):
    x = x_prompt
    bp, sp, _ = x.shape
    k_ctx_list, v_ctx_list = [], []
    for i in range(DEPTH):
        sh_a, sc_a, g_a, sh_f, sc_f, g_f = _ada(c_ctx, w_ada[i], b_ada[i])
        h = _modulate(x, sh_a, sc_a)
        if i % N_MIXERS == 0:
            a = i // N_MIXERS
            lam_init = 0.8 - 0.6 * math.exp(-0.3 * i)
            lam = _diff_lambda(lambda_q1[a], lambda_k1[a], lambda_q2[a], lambda_k2[a], lam_init)
            q, k, v = _qkv(h, w_qkv[a])
            k_ctx_list.append(k.reshape(bp, sp, N_HEADS, 2 * HEAD_DIM))
            v_ctx_list.append(v)
            o = _diff_attention(q, k, v, lam)
            out = _attn_output(o, subln_gain[a], lam_init, w_attn_out[a])
        else:
            out = _fourier_mix(h, w_fourier_out[i // N_MIXERS])
        x = _post_norm(x, g_a * out, ln_gain[i, 0], ln_bias[i, 0])
        h = _modulate(x, sh_f, sc_f)
        moe = _hier_moe(h, w_router_group[i], w_router_expert[i], w_expert_gate[i],
                        w_expert_up[i], w_expert_down[i])
        x = _post_norm(x, g_f * moe, ln_gain[i, 1], ln_bias[i, 1])
    y_prompt = x
    new_cache_k = jnp.stack(k_ctx_list, axis=1)
    new_cache_v = jnp.stack(v_ctx_list, axis=1)

    x = x_sample
    bs, n_lat, _ = x.shape
    n_rows = n_lat // GRID_W
    cos, sin = _rope_2d_tables(n_rows)
    n_ctx = cache_k.shape[2]
    for i in range(DEPTH):
        sh_a, sc_a, g_a, sh_f, sc_f, g_f = _ada(c, w_ada[i], b_ada[i])
        h = _modulate(x, sh_a, sc_a)
        if i % N_MIXERS == 0:
            a = i // N_MIXERS
            lam_init = 0.8 - 0.6 * math.exp(-0.3 * i)
            lam = _diff_lambda(lambda_q1[a], lambda_k1[a], lambda_q2[a], lambda_k2[a], lam_init)
            q, k, v = _qkv(h, w_qkv[a])
            q = _apply_rope_2d(q, cos, sin)
            k = _apply_rope_2d(k, cos, sin)
            k_ctx = cache_k[:, a].reshape(bs, n_ctx, N_HEADS, 2, HEAD_DIM)
            k_all = jnp.concatenate([k, k_ctx.astype(k.dtype)], axis=1)
            v_all = jnp.concatenate([v, cache_v[:, a].astype(v.dtype)], axis=1)
            o = _diff_attention(q, k_all, v_all, lam)
            out = _attn_output(o, subln_gain[a], lam_init, w_attn_out[a])
        else:
            out = _fourier_mix(h, w_fourier_out[i // N_MIXERS])
        x = _post_norm(x, g_a * out, ln_gain[i, 0], ln_bias[i, 0])
        h = _modulate(x, sh_f, sc_f)
        moe = _hier_moe(h, w_router_group[i], w_router_expert[i], w_expert_gate[i],
                        w_expert_up[i], w_expert_down[i])
        x = _post_norm(x, g_f * moe, ln_gain[i, 1], ln_bias[i, 1])
    y_sample = x
    return (y_prompt, y_sample, new_cache_k, new_cache_v)


_drawn_inputs = setup_inputs


def setup_inputs(seed=0):
    import zlib

    import numpy as np

    out = dict(_drawn_inputs(seed))
    spreads = {}
    factors = {'lambda_q1': 3.578, 'lambda_q2': 8.0, 'lambda_k2': 3.019, 'subln_gain': 5.857}
    for name, (base, spread) in spreads.items():
        noise = np.random.default_rng([zlib.crc32(name.encode()), seed]).standard_normal(out[name].shape)
        drawn = base * np.exp(spread * noise) if base else spread * noise
        out[name] = __import__('jax').numpy.asarray(drawn.astype(out[name].dtype))
    for name, factor in factors.items():
        out[name] = (out[name] * factor).astype(out[name].dtype)
    return out
```

```python
import math
from contextlib import ExitStack

import numpy as np

import concourse.bass as bass
from concourse import mybir

F32 = mybir.dt.float32
I32 = mybir.dt.int32
U32 = mybir.dt.uint32
ALU = mybir.AluOpType
ACT = mybir.ActivationFunctionType
AX = mybir.AxisListType.X

P = 128
D = 1024
KC = D // P
TILES = 3
TOK = TILES * P
HEADS = 8
HD = 64
NMOD = 6
GROUPS, PER_GROUP = 4, 8
EXPERTS = GROUPS * PER_GROUP
FE = 256
CAP = 64
PAIRS = EXPERTS // 2
PASSES = TOK // CAP
NLOG = GROUPS + EXPERTS
SLOTS = 4
SLOT = 6 * D
EPS = 1e-5
ALPHA = (2.0 * 2) ** 0.25
LAM_INIT = 0.8 - 0.6 * math.exp(0.0)
SCALE = HD ** -0.5
INVALID = 4096
ADA_UNITS = NMOD * D // 512
QK_W = 768
STEPS = 3 * HEADS

UNITS = [("ada", 0, u) for u in range(4)]
_rest = [("ada", 0, u) for u in range(4, ADA_UNITS)] + [("ada", 1, u) for u in range(4)]
for _u in range(4):
    UNITS += [("qkv", 0, _u)] + _rest[3 * _u:3 * _u + 3]
UNITS += [("out", 0, 0), ("out", 0, 1)]
MOE_BASE = [len(UNITS)]
UNITS += [("expert", 0, e) for e in range(EXPERTS)]
UNITS += [("ada", 1, u) for u in range(4, ADA_UNITS)] + [("out", 1, 0), ("out", 1, 1)]
MOE_BASE.append(len(UNITS))
UNITS += [("expert", 1, e) for e in range(EXPERTS)]
AT = {unit: n for n, unit in enumerate(UNITS)}
DMAS = {"ada": 1, "qkv": 3, "out": 1, "expert": 3}
LANDED = []
_sum = [0] * SLOTS
for _n, (_kind, _, _) in enumerate(UNITS):
    _sum[_n % SLOTS] += 16 * DMAS[_kind]
    LANDED.append(_sum[_n % SLOTS])

_C = {}
_at = 0
for _name, _w in (("ident", P), ("tri", P), ("ones", P), ("sel", 8 * P), ("cos", 2 * HD), ("sin", 2 * HD),
                  ("slotbase", EXPERTS), ("thresholds", PASSES - 1), ("descend", 8), ("octal", PAIRS)):
    _C[_name] = (_at, _at + _w)
    _at += _w
NCONST = _at
NDFT = 2 * P + 2 * P + 4 * 2 * P


def constants():
    c = np.zeros((P, NCONST), np.float64)

    def put(name, a):
        c[:, _C[name][0]:_C[name][1]] = np.asarray(a).reshape(np.asarray(a).shape[0], -1)

    put("ident", np.eye(P))
    put("tri", np.triu(np.ones((P, P)), 1))
    put("ones", np.ones((P, P)))
    sel = np.zeros((P, 4, 2, P))
    for j in range(4):
        for i in range(2):
            sel[32 * j + i, j, i, :] = 1.0
    put("sel", sel)
    nf = HD // 4
    inv = np.float32(10000.0) ** (-np.arange(nf, dtype=np.float32) / nf)
    tok = np.arange(2 * P)
    pos = np.stack([tok // 64, tok % 64], 1).astype(np.float32)
    ang = (pos[:, :, None] * inv.astype(np.float32)).astype(np.float32)
    cos, sin = np.cos(ang.astype(np.float64)), np.sin(ang.astype(np.float64))
    full_c = np.concatenate([cos, cos], -1).reshape(2, P, HD).transpose(1, 0, 2)
    full_s = np.concatenate([-sin, sin], -1).reshape(2, P, HD).transpose(1, 0, 2)
    put("cos", full_c)
    put("sin", full_s)
    e = np.arange(EXPERTS)
    put("slotbase", np.tile((e % 2) * (CAP * PAIRS) + e // 2, (P, 1)))
    put("thresholds", np.tile(CAP * np.arange(1, PASSES), (P, 1)))
    put("octal", np.tile(8.0 ** (np.arange(PAIRS) % 8), (P, 1)))
    put("descend", np.tile(8 - np.arange(8), (P, 1)))

    def dft(n, scale):
        a = 2 * np.pi * (np.outer(np.arange(n), np.arange(n)) % n) / n
        return np.cos(a) * scale, np.sin(a) * scale

    cc, sc = dft(P, 1.0)
    cp, sp = dft(P, 1.0 / P)
    cl, sl = dft(2 * P, (2 * P * P) ** -0.5)
    lat = np.stack([cl, -sl], 1).reshape(2, P, 2, 2 * P).transpose(1, 0, 2, 3)
    table = np.concatenate([cc, sc, cp, -sp, lat.reshape(P, -1)], 1)
    ids = np.arange(P)[:, None, None] + P * np.arange(TILES)[None, None, :] + TOK * np.arange(2)[None, :, None]
    empty = np.full((P, PASSES * PAIRS), INVALID)
    ints = np.concatenate([ids.reshape(P, -1), empty], 1)
    return {"k_rows": c.astype(np.float32), "k_dft": table.astype(np.float32), "k_ints": ints.astype(np.int32)}


class Memory:

    def __init__(self, nc, ctx):
        def sb(name, shape, dt=F32):
            return ctx.enter_context(nc.sbuf_tensor(name, shape, dt))

        self.ring = sb("ring", [P, SLOTS, SLOT])
        self.x = sb("x", [P, TILES, D])
        self.h = sb("h", [P, TILES, D])
        self.hT = sb("hT", [P, KC, TOK])
        self.m = sb("m", [P, 2, ADA_UNITS, P])
        self.rows = sb("k_rows_sb", [P, NCONST])
        self.ints = sb("k_ints_sb", [P, 6 + PASSES * PAIRS], I32)
        self.wr = sb("wr", [P, 2, KC, NLOG])
        self.cond = sb("cond", [2 * KC, P])
        self.silu = sb("silu", [P, KC, 32])
        self.col = sb("col", [P, 2, 2, 4, 2])
        self.lams = sb("lams", [P, 8])
        self.gain8 = sb("gain8", [P, P])
        self.stats = sb("stats", [P, TILES, 2, 6])
        self.mv = sb("mv", [P, TILES, 2])
        self.rstd = sb("rstd", [P, TILES])
        self.mx = sb("mx", [P, 2, 2])
        self.nb = sb("nb", [P, 2, 2])
        self.ssum = sb("ssum", [P, 2, 2])
        self.rsum = sb("rsum", [P, 2, 2])
        self.ratio = sb("ratio", [P, 2])
        self.sq = sb("sq", [P, P])
        self.ss = sb("ss", [P, TILES])
        self.rs_v = sb("rs_v", [P, TILES])
        self.rs_t = sb("rs_t", [P, TILES])
        self.rs_y = sb("rs_y", [P, TILES])
        self.w = sb("w", [P, 2, TILES])
        self.slot = sb("slot", [P, 6], I32)
        self.words_f = sb("words_f", [P, 2])
        self.words = sb("words", [P, 2], I32)
        self.table = sb("table", [P, 8 * PAIRS], I32)
        self.source = sb("source", [P, 8 * PAIRS], I32)
        self.gidx = sb("gidx", [P, 2], I32)
        self.sidx = sb("sidx", [P, 2], I32)
        K = 256
        self.arena = a = sb("arena", [P, 50 * K])

        def view(at, size):
            return a[:, int(at * K):int(at * K) + size]

        self.qkv = [view(9 * b, TILES * QK_W).rearrange("p (t n) -> p t n", t=TILES) for b in range(2)]
        self.qT = view(18, TOK)
        self.kT = view(19.5, TOK + P)
        self.rope_a = view(21.5, 512)
        self.rope_b = view(23.5, 512)
        self.ctxk = view(25.5, D)
        self.ctxv = view(29.5, D)
        self.p = [[view(33.5 + 3 * b + 1.5 * j, TOK) for j in range(2)] for b in range(2)]
        self.pdT = [view(39.5 + 1.5 * b, TOK) for b in range(2)]
        self.lam = view(33.5, 4 * HD).rearrange("p (n d) -> p n d", n=4)
        self.lamtmp = view(34.5, HD)
        at = [16 * K]

        def small(*shape):
            n = int(np.prod(shape))
            v = a[:, at[0]:at[0] + n]
            at[0] += n
            names = "abc"[:len(shape)]
            return v.rearrange(f"p ({' '.join(names)}) -> p {' '.join(names)}",
                               **dict(zip(names[1:], shape[1:]))) if len(shape) > 1 else v

        self.L = small(TILES, NLOG)
        self.r3 = small(16, TILES)
        self.r12 = [small(TILES, GROUPS) for _ in range(4)]
        self.r24 = [small(TILES, PER_GROUP) for _ in range(8)]
        self.r96 = small(TILES, GROUPS, PER_GROUP)
        self.M = [small(TILES, EXPERTS) for _ in range(2)]
        self.Msum = small(TILES, EXPERTS)
        self.Mt = small(2 * TILES, EXPERTS)
        self.r6 = small(5, 6)
        self.r30 = small(6, PASSES - 1)
        self.pairmax = small(PAIRS)
        self.r80 = small(PAIRS, PASSES - 1)
        self.further = small(PAIRS)
        self.table_f = small(PASSES * PAIRS)
        self.table_g = small(PASSES * PAIRS)
        self.tmp = view(0, TILES * D).rearrange("p (t n) -> p t n", t=TILES)
        self.U = view(0, TILES * KC * 2 * P).rearrange("p (t g n) -> p t g n", t=TILES, g=KC)
        self.dft = view(24, NDFT)
        self.gates = view(30, 2 * D).rearrange("p (i n) -> p i n", i=2)
        self.gb = view(38, 2 * D).rearrange("p (i n) -> p i n", i=2)
        self.G = [view(4 * b, D) for b in range(2)]
        self.GT = [view(8 + 4 * b, D).rearrange("p (c s) -> p c s", c=KC) for b in range(2)]
        self.sil = [view(16 + b, FE) for b in range(2)]
        self.act = [view(18 + b, FE) for b in range(2)]
        self.actT = [view(20 + b, 2 * P).rearrange("p (f s) -> p f s", f=2) for b in range(2)]
        self.O = [view(22 + 4 * b, D) for b in range(2)]
        self.Y = view(0, TILES * 2 * D).rearrange("p (t k n) -> p t k n", t=TILES, k=2)
        self.psum = ctx.enter_context(nc.psum_tensor("psum", [P, 8 * 512], F32))
        self.bank = [self.psum[:, 512 * b:512 * b + 512] for b in range(8)]
        self.fT = self.h[:, :, :].rearrange("p t n -> p (t n)").rearrange("p (k n) -> p k n", k=KC)

    def const(self, name):
        return self.rows[:, _C[name][0]:_C[name][1]]

    def unit(self, n):
        return self.ring[:, n % SLOTS, :]


def bc(ap, shape):
    return ap.to_broadcast(shape)


def build(nc, A):
    ctx = ExitStack()
    with ctx:
        mem = Memory(nc, ctx)
        bank = mem.bank
        ident = mem.const("ident")

        sems = {}

        def sem(name):
            if name not in sems:
                sems[name] = ctx.enter_context(nc.semaphore(name))
            return sems[name]

        h_dram = [nc.dram_tensor(f"h_scratch{l}", (TOK, D), F32).ap() for l in range(2)]
        y_dram = [nc.dram_tensor(f"y_scratch{l}", (2 * TOK, D), F32).ap() for l in range(2)]
        t_dram = [nc.dram_tensor(f"table_scratch{l}", (PASSES * PAIRS * P, 1), I32).ap() for l in range(2)]

        cond_in, rows_in, router_in, x_in, lam_in, ctx_in = (
            sem(n) for n in ("cond_in", "rows_in", "router_in", "x_in", "lam_in", "ctx_in"))
        bias_in, zeroed, table_clear = sem("bias_in"), sem("zeroed"), sem("table_clear")
        landed = [sem(f"slot_landed{i}") for i in range(SLOTS)]
        cond_ps, silu_done = sem("cond_ps"), sem("silu_done")
        ada_ps, ada_done = sem("ada_ps"), sem("ada_done")
        col_ps, col_done = sem("col_ps"), sem("col_done")
        norm_ready = sem("norm_ready")
        t8_ps, t8_act, t8_dve = sem("t8_ps"), sem("t8_act"), sem("t8_dve")
        qkv_ps, qkv_sb, rope_done = sem("qkv_ps"), sem("qkv_sb"), sem("rope_done")
        kv_stored = [sem(f"kv_stored{b}") for b in range(2)]
        qkT_ps, qT_sb, kT_sb = sem("qkT_ps"), sem("qT_sb"), sem("kT_sb")
        score_ps, nb_done, exp_done = sem("score_ps"), sem("nb_done"), sem("exp_done")
        pd_done, pdT_ps, pdT_sb, pv_ps, o_done = (sem(n) for n in ("pd_done", "pdT_ps", "pdT_sb", "pv_ps", "o_done"))
        lam_done, o_raw = sem("lam_done"), sem("o_raw")
        gate_ps, gate_sb = sem("gate_ps"), sem("gate_sb")
        proj_ps, proj_used = sem("proj_ps"), sem("proj_used")
        gb_in, gb_used = sem("gb_in"), sem("gb_used")
        rows_ps = sem("rows_ps")
        h_stored = [sem(f"h_stored{l}") for l in range(2)]
        logits_ps, route_in, route_out, pos_ps, msum_done = (
            sem(n) for n in ("logits_ps", "route_in", "route_out", "pos_ps", "msum_done"))
        slot_done, ids_out, table_in, source_done, words_done, mlp_end = (
            sem(n) for n in ("slot_done", "ids_out", "table_in", "source_done", "words_done", "mlp_end"))
        dft_in, chan_ps, chan_act, chan_dve = sem("dft_in"), sem("chan_ps"), sem("chan_act"), sem("chan_dve")
        four_ps, four_act, four_dve = sem("four_ps"), sem("four_act"), sem("four_dve")
        y_in = [sem(f"y_in{t}") for t in range(TILES)]
        x_done, out_done, lam_prod = sem("x_done"), sem("out_done"), sem("lam_prod")
        g_clear, turns = sem("g_clear"), sem("turns")
        dve_chain, act_chain, pool_chain = sem("dve_chain"), sem("act_chain"), sem("pool_chain")

        def moe_sems(tag):
            names = ("gidx", "gathered", "gt_ps", "gt_act", "gt_dve", "u_ps", "sil", "act", "at_ps", "at_sb", "d_ps",
                     "o_act", "o_dve", "scattered", "o_free")
            return {n: sem(f"{n}_{tag}") for n in names}

        main = [moe_sems(f"main{l}") for l in range(2)]
        extra = moe_sems("extra")

        def passes(eng, l, S, first, body, start=None):
            eng.wait_ge(words_done, l + 1)
            with eng.Fori(0, 2) as half:
                word = eng.value_load(mem.words[0:1, bass.ds(half, 1)], min_val=0, max_val=(1 << 24) - 1)
                with eng.Fori(0, PAIRS // 4) as it:
                    for b in range(2):
                        n = half * (PAIRS // 2) + it * 2 + b
                        first(n, b, half * (PAIRS // 4) + it)
                        times = eng.snap((word >> (it * 6 + 3 * b)) & 7, min_val=0, max_val=PASSES - 1)
                        with eng.If(times > 0):
                            with eng.Fori(0, times) as r:
                                body(n, b, r + 1, eng.snap(further[eng]))
                                eng.reg_add(further[eng], further[eng], 1)
                        if start is not None:
                            start(n, b)

        further = {}
        block = ctx.enter_context(nc.Block())

        T8_LN = [0, 3]
        T8_O = 1
        T8_ROUTE = [2, 4]

        def wait_unit(eng, n):
            eng.wait_ge(landed[n % SLOTS], LANDED[n])

        ADA_ORDER = [n for n, unit in enumerate(UNITS) if unit[0] == "ada"]

        def wait_used(eng, n):
            kind, l, u = UNITS[n]
            if kind == "ada":
                eng.wait_ge(ada_ps, ADA_ORDER.index(n) + 1)
            elif kind == "qkv":
                eng.wait_ge(qkv_ps, 6 * u + 6)
            elif kind == "out":
                eng.wait_ge(proj_ps, 6 * l + 3 * u + 3)
            elif u // 2 < PAIRS - 1:
                eng.wait_ge(main[l]["gt_ps"], u // 2 + 2)
            else:
                eng.wait_ge(mlp_end, l + 1)

        def wait_t8(eng, use):
            eng.wait_ge(t8_act, 4 * (use + 1))
            eng.wait_ge(t8_dve, 4 * (use + 1))

        @block.sync
        def _(sp):
            for i, src in enumerate((A["c_ctx"].rearrange("(k p) -> k p", p=P),
                                     A["c"].rearrange("b (k p) -> (b k) p", p=P))):
                sp.dma_start(mem.cond[KC * i:KC * i + KC, :], src).then_inc(cond_in, 16)
            sp.dma_start(mem.rows[:, :], A["k_rows"]).then_inc(rows_in, 16)

            def load_expert(slot, l, e, done):
                for part, name in enumerate(("w_expert_gate", "w_expert_up", "w_expert_down")):
                    sp.dma_start(mem.ring[:, slot, part * 2 * D:(part + 1) * 2 * D],
                                 A[name][l][bass.ds(e, 1)].rearrange("o (p k) n -> p (o k n)", p=P)
                                 ).then_inc(done, 16)

            def load(n):
                kind, l, u = UNITS[n]
                if n >= SLOTS:
                    wait_used(sp, n - SLOTS)
                dst, done = mem.unit(n), landed[n % SLOTS]
                if kind == "ada":
                    sp.dma_start(dst[:, 0:KC * 512].rearrange("p (k n) -> p k n", k=KC),
                                 A["w_ada"][l].rearrange("(k p) n -> p k n", p=P)[:, :, 512 * u:512 * u + 512]
                                 ).then_inc(done, 16)
                elif kind == "qkv":
                    w = A["w_qkv"][0].rearrange("(k p) n -> p k n", p=P)
                    for part in range(3):
                        sp.dma_start(dst.rearrange("p (k n) -> p k n", k=KC)[:, :, 256 * part:256 * part + 256],
                                     w[:, :, D * part + 256 * u:D * part + 256 * u + 256]).then_inc(done, 16)
                elif kind == "out":
                    w = A["w_attn_out"][0] if l == 0 else A["w_fourier_out"][0]
                    sp.dma_start(dst[:, 0:KC * 512].rearrange("p (k n) -> p k n", k=KC),
                                 w.rearrange("(k p) n -> p k n", p=P)[:, :, 512 * u:512 * u + 512]
                                 ).then_inc(done, 16)
                else:
                    load_expert(n % SLOTS, l, u, done)

            for n in range(2):
                load(n)
            for t in range(TILES):
                src = A["x_prompt"][0] if t == 0 else A["x_sample"][0][(t - 1) * P:t * P, :]
                sp.dma_start(mem.x[:, t, :], src).then_inc(x_in, 16)
            for n in range(2, MOE_BASE[0]):
                load(n)
            for l in range(2):
                base = MOE_BASE[l]
                for n in range(base, base + SLOTS):
                    load(n)
                with sp.Fori(1, PAIRS // 2) as it:
                    for q in range(SLOTS):
                        e = sp.snap(it * 4 + q)
                        n = sp.snap(it * 2 + q // 2)
                        sp.wait_ge(main[l]["gt_ps"], n)
                        load_expert((base + q) % SLOTS, l, e, landed[(base + q) % SLOTS])
                if l == 0:
                    for n in range(base + EXPERTS, MOE_BASE[1]):
                        load(n)

        @block.gpsimd
        def _(pool):
            chain = [0]

            def link(ins):
                chain[0] += 1
                ins.then_inc(pool_chain, 1)
                pool.wait_ge(pool_chain, chain[0])

            pool.memset(mem.silu[:, :, :], 0.0).then_inc(zeroed, 1)
            pool.memset(mem.m[:, :, :, :], 0.0).then_inc(zeroed, 1)
            pool.dma_start(mem.ints[:, :], A["k_ints"]).then_inc(lam_in, 16)
            pool.wait_ge(zeroed, 2)
            for l in range(2):
                for i in range(2):
                    for j in range(4):
                        pool.dma_start(mem.m[32 * j + i:32 * j + i + 1, l, :, :],
                                       A["b_ada"][l:l + 1].rearrange("o (u j n) -> o u j n", u=ADA_UNITS, j=4)[:, :, j, :]
                                       ).then_inc(bias_in, 16)
            for l in range(2):
                pool.dma_start(t_dram[l].rearrange("(p n) o -> p (n o)", p=P), A["k_ints"][:, 6:]).then_inc(table_clear, 16)
            for n, name in enumerate(("lambda_q1", "lambda_k1", "lambda_q2", "lambda_k2")):
                pool.dma_start(mem.lam[:, n, :], A[name][0].partition_broadcast(P)).then_inc(lam_in, 16)
            pool.dma_start(mem.gain8[:, :], A["subln_gain"][0].partition_broadcast(P)).then_inc(lam_in, 16)
            pool.dma_start(mem.ctxk, A["cache_k"][0, 0].rearrange("s h d -> s (h d)")).then_inc(ctx_in, 16)
            pool.dma_start(mem.ctxv, A["cache_v"][0, 0].rearrange("s h d -> s (h d)")).then_inc(ctx_in, 16)
            for l in range(2):
                pool.dma_start(mem.wr[:, l, :, 0:GROUPS], A["w_router_group"][l].rearrange("(k p) n -> p k n", p=P)
                               ).then_inc(router_in, 16)
                pool.dma_start(mem.wr[:, l, :, GROUPS:], A["w_router_expert"][l].rearrange("(k p) n -> p k n", p=P)
                               ).then_inc(router_in, 16)
            pool.wait_ge(rows_in, 16)

            cos = mem.const("cos").rearrange("p (t n) -> p t n", t=2)
            sin = mem.const("sin").rearrange("p (t n) -> p t n", t=2)
            for u in range(4):
                buf = mem.qkv[u % 2]
                for t in (1, 2):
                    pool.wait_ge(qkv_sb, 6 * u + 2 * t)
                    x8 = buf[:, t, 0:512].rearrange("p (g n) -> p g n", n=HD)
                    x4 = buf[:, t, 0:512].rearrange("p (g s n) -> p g s n", s=2, n=16)
                    b4 = mem.rope_b.rearrange("p (g s n) -> p g s n", s=2, n=16)
                    sg = sin[:, t - 1, :].rearrange("p (a s n) -> p a s n", a=2, s=2)
                    pool.tensor_tensor(mem.rope_a.rearrange("p (g n) -> p g n", n=HD), x8,
                                       bc(cos[:, t - 1, :].unsqueeze(1), [P, 8, HD]), ALU.mult)
                    for s in range(2):
                        last = pool.tensor_tensor(
                            b4[:, :, s, :].rearrange("p (g a) n -> p g a n", a=2),
                            x4[:, :, 1 - s, :].rearrange("p (g a) n -> p g a n", a=2),
                            bc(sg[:, :, s, :].unsqueeze(1), [P, 8, 2, 16]), ALU.mult)
                    link(last)
                    link(pool.tensor_tensor(buf[:, t, 0:512], mem.rope_a, mem.rope_b, ALU.add))
                pool.sem_inc(rope_done, 1)
                pool.wait_ge(qkv_sb, 6 * u + 6)
                pool.dma_start(A["new_cache_k"][0, 0].rearrange("s h d -> s (h d)")[:, 256 * u:256 * u + 256],
                               buf[:, 0, 256:512]).then_inc(kv_stored[u % 2], 16)
                pool.dma_start(A["new_cache_v"][0, 0].rearrange("s h d -> s (h d)")[:, 256 * u:256 * u + 256],
                               buf[:, 0, 512:768]).then_inc(kv_stored[u % 2], 16)

            def value(x):
                return x if isinstance(x, int) else pool.snap(x)

            further[pool] = pool.alloc_register("further")
            pool.reg_mov(further[pool], 0)
            row_bound = pool.snap(pool.to_reg(TOK - 1))
            out_bound = pool.snap(pool.to_reg(2 * TOK - 1))
            table_bound = pool.snap(pool.to_reg(PASSES * PAIRS * P - 1))

            def gather(S, l, col, n, b):
                pool.tensor_copy(mem.gidx[:, b:b + 1], mem.source[:, bass.ds(col, 1)]).then_inc(S["gidx"], 1)
                pool.tensor_copy(mem.sidx[:, b:b + 1], mem.table[:, bass.ds(col, 1)]).then_inc(S["gidx"], 1)
                pool.wait_ge(S["gidx"], value(2 * n + 2))
                pool.sem_inc(turns, 1)
                pool.indirect_dma_start(mem.G[b], None, h_dram[l],
                                        bass.IndirectOffsetOnAxis(ap=mem.gidx[:, b:b + 1].bitcast(U32), axis=0),
                                        bounds_check=row_bound, oob_is_err=False).then_inc(S["gathered"], 16)

            def scatter(S, l, n, b):
                n2, n16 = value(n + 2), value(16 * n + 16)
                pool.wait_ge(S["o_act"], n2)
                pool.wait_ge(S["o_dve"], n2)
                pool.sem_inc(turns, 1)
                pool.indirect_dma_start(y_dram[l],
                                        bass.IndirectOffsetOnAxis(ap=mem.sidx[:, b:b + 1].bitcast(U32), axis=0),
                                        mem.O[b], None, bounds_check=out_bound, oob_is_err=False
                                        ).then_inc(S["scattered"], 16)
                pool.wait_ge(S["scattered"], n16)

            for l in range(2):
                S = main[l]
                pool.wait_ge(lam_in, 16 * 6)
                pool.wait_ge(table_clear, 32)
                pool.wait_ge(slot_done, l + 1)
                for c in range(6):
                    pool.indirect_dma_start(t_dram[l],
                                            bass.IndirectOffsetOnAxis(ap=mem.slot[:, c:c + 1].bitcast(U32), axis=0),
                                            mem.ints[:, c:c + 1], None, bounds_check=table_bound,
                                            oob_is_err=False).then_inc(ids_out, 16)
                for b in range(2):
                    pool.memset(mem.G[b], 0.0).then_inc(g_clear, 1)
                pool.wait_ge(g_clear, 2 * (l + 1))
                pool.wait_ge(h_stored[l], 16 * TILES)
                pool.wait_ge(source_done, l + 1)
                pool.sem_inc(S["o_free"], 2)
                gather(S, l, 0, 0, 0)

                def first(n, b, it):
                    pool.wait_ge(S["gt_ps"], value(n + 1))
                    gather(S, l, n + 1, n + 1, 1 - b)
                    scatter(S, l, n, b)

                def body(n, b, r, k):
                    pool.sem_inc(extra["o_free"], 1)
                    gather(extra, l, r * PAIRS + n, k, b)
                    scatter(extra, l, k, b)

                def after(n, b):
                    pool.sem_inc(S["o_free"], 1)

                passes(pool, l, S, first, body, after)
            for b in range(2):
                pool.wait_ge(kv_stored[b], 64)

        @block.tensor
        def _(pe):
            count = {"ada": 0}

            def ada(n, to):
                wait_unit(pe, n)
                if count["ada"] >= 1:
                    pe.wait_ge(ada_done, count["ada"])
                w = mem.unit(n)[:, 0:KC * 512].rearrange("p (k n) -> p k n", k=KC)
                out = bank[to]
                for k in range(KC):
                    for j in range(4):
                        last = pe.matmul(out[32 * j:32 * j + 32, 0:P], mem.silu[:, k, :],
                                         w[:, k, P * j:P * j + P], start=(k == 0), stop=(k == KC - 1))
                last.then_inc(ada_ps, 1)
                count["ada"] += 1

            def columns(l):
                for u in range(4):
                    last = pe.transpose(bank[3][:, P * u:P * u + P], mem.m[:, l, u, :], ident)
                last.then_inc(col_ps, 1)

            def t8(src):
                for k in range(KC):
                    for t in range(TILES):
                        last = pe.transpose(bank[k][:, P * t:P * t + P], src[:, t, P * k:P * k + P], ident)
                    last.then_inc(t8_ps, 1)

            def spread(l, vec, i, banks):
                for half in range(2):
                    for j in range(4):
                        last = pe.matmul(banks[half][:, P * j:P * j + P],
                                         mem.const("sel")[:, P * (2 * j + i):P * (2 * j + i) + P],
                                         mem.m[:, l, 2 * vec + half, :], start=True, stop=True)
                return last

            def project(l, srcT, half):
                n = AT["out", l, half]
                wait_unit(pe, n)
                w = mem.unit(n)[:, 0:KC * 512].rearrange("p (k n) -> p k n", k=KC)
                for t in range(TILES):
                    for k in range(KC):
                        last = pe.matmul(bank[3 * half + t], srcT[:, k, P * t:P * t + P], w[:, k, :],
                                         start=(k == 0), stop=(k == KC - 1))
                    last.then_inc(proj_ps, 1)

            pe.wait_ge(cond_in, 32)
            pe.wait_ge(rows_in, 16)
            pe.transpose(bank[0][:, 0:2 * KC], mem.cond[:, :], mem.const("ident")[0:2 * KC, 0:2 * KC]).then_inc(cond_ps, 1)
            pe.wait_ge(silu_done, 2)
            for u in range(4):
                ada(AT["ada", 0, u], 3)
            pe.wait_ge(router_in, 64)
            pe.wait_ge(ada_done, 4)
            columns(0)
            pe.wait_ge(norm_ready, 3)
            pe.wait_ge(col_done, 1)
            t8(mem.h)

            def qkv_group(u, g):
                n = AT["qkv", 0, u]
                i = 6 * u + g
                t, half = (1, 2, 0)[g // 2], g % 2
                if g == 0:
                    wait_unit(pe, n)
                if i >= 2:
                    pe.wait_ge(qkv_sb, i - 1)
                w = mem.unit(n).rearrange("p (k n) -> p k n", k=KC)
                for k in range(KC):
                    last = pe.matmul(bank[i % 2][:, 0:384], mem.hT[:, k, P * t:P * t + P],
                                     w[:, k, 384 * half:384 * half + 384], start=(k == 0), stop=(k == KC - 1))
                last.then_inc(qkv_ps, 1)

            def head_transposes(head):
                w, hh = head // 2, head % 2
                buf = mem.qkv[w % 2]
                pe.wait_ge(rope_done, w + 1)
                pe.wait_ge(qkv_sb, 6 * w + 6)
                pe.wait_ge(ada_done, count["ada"])
                if head >= 1:
                    pe.wait_ge(qT_sb, head)
                    pe.wait_ge(kT_sb, head)
                for t in range(TILES):
                    pe.transpose(bank[3][:, P * t:P * t + P], buf[:, t, P * hh:P * hh + P], ident)
                for t in range(TILES):
                    pe.transpose(bank[4][:, P * t:P * t + P], buf[:, t, 256 + P * hh:256 + P * hh + P], ident)
                pe.transpose(bank[4][:, TOK:TOK + P], mem.ctxk[:, P * head:P * head + P], ident).then_inc(qkT_ps, 1)

            def scores(g):
                head, t = g // 3, g % 3
                pe.wait_ge(qT_sb, head + 1)
                pe.wait_ge(kT_sb, head + 1)
                if g >= 1:
                    pe.wait_ge(exp_done, 2 * g)
                lo, hi = (0, P) if t == 0 else (P, TOK + P)
                for j in range(2):
                    last = pe.matmul(bank[5 + j][:, 0:hi - lo], mem.qT[HD * j:HD * j + HD, P * t:P * t + P],
                                     mem.kT[HD * j:HD * j + HD, lo:hi], start=True, stop=True)
                last.then_inc(score_ps, 1)

            def pd_transposes(g):
                pe.wait_ge(pd_done, g + 1)
                if g >= 1:
                    pe.wait_ge(pdT_sb, g)
                for c in range(1 if g % 3 == 0 else 3):
                    last = pe.transpose(bank[7][:, P * c:P * c + P], mem.p[g % 2][0][:, P * c:P * c + P], ident)
                last.then_inc(pdT_ps, 1)

            def pv(g):
                head, t = g // 3, g % 3
                buf, vc = mem.qkv[(head // 2) % 2], 512 + P * (head % 2)
                pe.wait_ge(pdT_sb, g + 1)
                if g >= 1:
                    pe.wait_ge(o_raw, g)
                out = bank[2][:, 0:P]
                v = [buf[:, 0, vc:vc + P]] if t == 0 else [buf[:, 1, vc:vc + P], buf[:, 2, vc:vc + P],
                                                           mem.ctxv[:, P * head:P * head + P]]
                for c, rhs in enumerate(v):
                    last = pe.matmul(out, mem.pdT[g % 2][:, P * c:P * c + P], rhs, start=(c == 0),
                                     stop=(c == len(v) - 1))
                last.then_inc(pv_ps, 1)

            wait_t8(pe, T8_LN[0])
            pe.wait_ge(ctx_in, 32)
            for u in range(5):
                between = [AT["qkv", 0, u] + 1 + i for i in range(3)] if u < 4 else []
                for s in range(6):
                    g = 6 * (u - 1) + s
                    if u >= 1 and s % 3 == 0:
                        head_transposes(g // 3)
                    if u < 4:
                        qkv_group(u, s)
                    if u >= 1:
                        scores(g)
                    if g >= 1:
                        pd_transposes(g - 1)
                    if s % 2 == 1 and between:
                        ada(between[s // 2], 3)
                    if g >= 1:
                        pv(g - 1)
            pd_transposes(STEPS - 1)
            pv(STEPS - 1)
            pe.wait_ge(o_done, STEPS)
            pe.wait_ge(ada_done, 16)
            t8(mem.h)

            further[pe] = pe.alloc_register("further")
            pe.reg_mov(further[pe], 0)

            def gt(S, n, b):
                pe.wait_ge(S["gathered"], 16 * n + 16)
                for c in range(KC):
                    last = pe.transpose(bank[2 + c // 4][:, P * (c % 4):P * (c % 4) + P],
                                        mem.G[b].rearrange("p (d c) -> p c d", c=KC)[:, c, :], ident)
                last.then_inc(S["gt_ps"], 1)

            def gate_up(S, n, b, slots, landings):
                pe.wait_ge(S["gt_act"], n + 1)
                pe.wait_ge(S["gt_dve"], n + 1)
                for done, value in landings:
                    pe.wait_ge(done, value)
                for c in range(KC):
                    for e in range(2):
                        w = mem.ring[:, slots[e], 0:4 * D].rearrange("p (g k n) -> p g k n", g=2, k=KC)[:, :, c, :]
                        last = pe.matmul(bank[b][64 * e:64 * e + 64, :].rearrange("p (g n) -> p g n", g=2),
                                         mem.GT[b][:, c, 64 * e:64 * e + 64], w,
                                         start=(c == 0), stop=(c == KC - 1))
                last.then_inc(S["u_ps"], 1)

            def act_transposes(S, n, b):
                pe.wait_ge(S["act"], n + 1)
                for f in range(2):
                    last = pe.transpose(bank[4][:, P * f:P * f + P],
                                        mem.act[b].rearrange("p (d f) -> p f d", f=2)[:, f, :], ident)
                last.then_inc(S["at_ps"], 1)

            def down(S, n, b, slots):
                pe.wait_ge(S["at_sb"], n + 1)
                pe.wait_ge(S["o_act"], n + 1)
                pe.wait_ge(S["o_dve"], n + 1)
                for half in range(2):
                    for f in range(2):
                        for e in range(2):
                            w = mem.ring[:, slots[e], 4 * D:].rearrange("p (k n) -> p k n", k=2)
                            last = pe.matmul(bank[5 + half][64 * e:64 * e + 64, :],
                                             mem.actT[b][:, f, 64 * e:64 * e + 64],
                                             w[:, f, 512 * half:512 * half + 512], start=(f == 0), stop=(f == 1))
                last.then_inc(S["d_ps"], 1)

            def mlp(l):
                S, base = main[l], MOE_BASE[l]

                def first(n, b, it):
                    units = [base + 2 * b + e for e in range(2)]
                    slots = [x % SLOTS for x in units]
                    gt(S, n, b)
                    gate_up(S, n, b, slots, [(landed[x % SLOTS], 48 * it + LANDED[x]) for x in units])
                    act_transposes(S, n, b)
                    down(S, n, b, slots)

                def body(n, b, r, k):
                    slots = [(base + 2 * b + e) % SLOTS for e in range(2)]
                    gt(extra, k, b)
                    gate_up(extra, k, b, slots, [])
                    act_transposes(extra, k, b)
                    pe.wait_ge(S["o_act"], n + 2)
                    pe.wait_ge(S["o_dve"], n + 2)
                    down(extra, k, b, slots)

                passes(pe, l, S, first, body)
                pe.drain().then_inc(mlp_end, 1)

            def mixer_output(l, srcT):
                spread(l, 2, 0, (bank[6], bank[7])).then_inc(gate_ps, 1)
                project(l, srcT, 0)
                pe.wait_ge(gate_sb, 4 * l + 1)
                spread(l, 2, 1, (bank[6], bank[7])).then_inc(gate_ps, 1)
                project(l, srcT, 1)

            def expert_input(l):
                pe.wait_ge(proj_used, 6 * (l + 1))
                pe.wait_ge(gate_sb, 4 * l + 2)
                for i in range(2):
                    spread(l, 4, i, (bank[4 * i], bank[4 * i + 1]))
                    spread(l, 3, i, (bank[4 * i + 2], bank[4 * i + 3])).then_inc(rows_ps, 1)
                pe.wait_ge(norm_ready, 6 * (l + 1))
                t8(mem.h)
                wait_t8(pe, T8_ROUTE[l])
                for t in range(TILES):
                    for k in range(KC):
                        last = pe.matmul(bank[0][:, NLOG * t:NLOG * t + NLOG], mem.hT[:, k, P * t:P * t + P],
                                         mem.wr[:, l, k, :], start=(k == 0), stop=(k == KC - 1))
                last.then_inc(logits_ps, 1)
                for i in range(2):
                    spread(l, 5, i, (bank[4 + 2 * i], bank[5 + 2 * i])).then_inc(gate_ps, 1)
                pe.wait_ge(msum_done, l + 1)
                for t in range(TILES):
                    for s in range(t + 1):
                        last = pe.matmul(bank[1][:, EXPERTS * t:EXPERTS * t + EXPERTS],
                                         mem.const("tri" if s == t else "ones"), mem.Msum[:, s, :],
                                         start=(s == 0), stop=(s == t))
                for s in range(TILES):
                    last = pe.matmul(bank[1][:, EXPERTS * TILES:EXPERTS * (TILES + 1)], mem.const("ones"),
                                     mem.Msum[:, s, :], start=(s == 0), stop=(s == TILES - 1))
                last.then_inc(pos_ps, 1)
                pe.wait_ge(gate_sb, 4 * l + 4)

            wait_t8(pe, T8_O)
            mixer_output(0, mem.hT)
            expert_input(0)
            mlp(0)

            columns(1)
            pe.wait_ge(norm_ready, 9)
            pe.wait_ge(col_done, 2)
            t8(mem.h)
            wait_t8(pe, T8_LN[1])
            pe.wait_ge(dft_in, 16)
            for n in range(4 * TILES):
                t, gp = n // 4, n % 4
                if n >= 4:
                    pe.wait_ge(chan_act if n % 2 == 0 else chan_dve, (n - 4) // 2 + 1)
                for i in range(2):
                    last = pe.matmul(bank[(0, 1, 3, 4)[n % 4]][:, 256 * i:256 * i + 256],
                                     mem.hT[:, 2 * gp + i, P * t:P * t + P], mem.dft[:, 0:256], start=True, stop=True)
                last.then_inc(chan_ps, 1)
                if n < 8:
                    ada(AT["ada", 1, 4 + n], 7)
            pe.wait_ge(chan_act, 2 * TILES)
            pe.wait_ge(chan_dve, 2 * TILES)
            pos_p = mem.dft[:, 256:512].rearrange("p (s n) -> p s n", s=2)
            pos_l = mem.dft[:, 512:].rearrange("p (t s n) -> p t s n", t=2, s=2)
            for g in range(KC):
                out = bank[5 + g % 2]
                if g >= 2:
                    pe.wait_ge(four_act if g % 2 == 0 else four_dve, (g - 2) // 2 + 1)
                for s in range(2):
                    pe.matmul(out[:, 0:P], mem.U[:, 0, g, P * s:P * s + P], pos_p[:, s, :],
                              start=(s == 0), stop=(s == 1))
                for i, (t, s) in enumerate(((0, 0), (0, 1), (1, 0), (1, 1))):
                    last = pe.matmul(out[:, P:TOK], mem.U[:, 1 + t, g, P * s:P * s + P], pos_l[:, t, s, :],
                                     start=(i == 0), stop=(i == 3))
                last.then_inc(four_ps, 1)
            pe.wait_ge(four_act, KC // 2)
            pe.wait_ge(four_dve, KC // 2)
            pe.wait_ge(ada_done, 2 * ADA_UNITS)
            mixer_output(1, mem.fT)
            expert_input(1)
            mlp(1)

        @block.scalar
        def _(act):
            def t8_evict(use, l=None):
                for k in range(0, KC, 2):
                    act.wait_ge(t8_ps, KC * use + k + 1)
                    if l is None:
                        last = nc.scalar.copy(mem.hT[:, k, :], bank[k][:, 0:TOK])
                    else:
                        for i, (lo, hi) in enumerate(((0, P), (P, TOK))):
                            last = nc.scalar.activation(mem.hT[:, k, lo:hi], bank[k][:, lo:hi], ACT.Identity,
                                                        bias=mem.col[:, 0, k // 4, k % 4, i:i + 1],
                                                        scale=mem.col[:, 1, k // 4, k % 4, i:i + 1])
                    last.then_inc(t8_act, 1)

            def gate_evict(n, i, banks):
                act.wait_ge(gate_ps, n)
                nc.scalar.copy(mem.gates[:, i, :], mem.psum[:, 512 * banks:512 * banks + D]).then_inc(gate_sb, 1)

            def load_norm(idx):
                if idx >= 1:
                    act.wait_ge(gb_used, idx)
                for i, name in enumerate(("ln_gain", "ln_bias")):
                    act.dma_start(mem.gb[:, i, :], A[name][idx // 2, idx % 2].partition_broadcast(P)).then_inc(gb_in, 16)

            act.wait_ge(cond_ps, 1)
            act.wait_ge(zeroed, 2)
            for i in range(2):
                nc.scalar.activation(mem.silu[:, :, i], bank[0][:, KC * i:KC * i + KC], ACT.Silu).then_inc(silu_done, 1)
            act.wait_ge(lam_prod, 2)
            nc.scalar.activation(mem.lams[:, 2:4], mem.lams[:, 0:2], ACT.Exp).then_inc(lam_done, 1)
            act.wait_ge(col_done, 1)
            t8_evict(T8_LN[0], 0)

            for u in range(5):
                for s in range(6):
                    g = 6 * (u - 1) + s
                    if u >= 1 and s % 3 == 0:
                        act.wait_ge(qkT_ps, g // 3 + 1)
                        nc.scalar.copy(mem.qT, bank[3][:, 0:TOK]).then_inc(qT_sb, 1)
                    if u >= 1:
                        w = P if g % 3 == 0 else TOK
                        act.wait_ge(nb_done, g + 1)
                        for j in range(2):
                            nc.scalar.activation(mem.p[g % 2][j][:, 0:w], bank[5 + j][:, 0:w], ACT.Exp,
                                                 bias=mem.nb[:, g % 2, j:j + 1], scale=SCALE,
                                                 accum_out=mem.ssum[:, g % 2, j:j + 1]).then_inc(exp_done, 1)
                    if u < 4:
                        i = 6 * u + s
                        t, half = (1, 2, 0)[s // 2], s % 2
                        act.wait_ge(qkv_ps, i + 1)
                        if s == 0 and u >= 2:
                            act.wait_ge(pv_ps, 6 * (u - 1))
                            act.wait_ge(kv_stored[u % 2], 32)
                        nc.scalar.copy(mem.qkv[u % 2][:, t, 384 * half:384 * half + 384],
                                       bank[i % 2][:, 0:384]).then_inc(qkv_sb, 1)
            t8_evict(T8_O)

            def gt_evict(S, n, b):
                act.wait_ge(S["gt_ps"], n + 1)
                nc.scalar.copy(mem.GT[b][:, 0:4, :], bank[2].rearrange("p (c s) -> p c s", c=4)
                               ).then_inc(S["gt_act"], 1)

            def silu(S, n, b):
                act.wait_ge(S["u_ps"], n + 1)
                nc.scalar.activation(mem.sil[b], bank[b][:, 0:FE], ACT.Silu).then_inc(S["sil"], 1)

            def o_evict(S, n, b):
                act.wait_ge(S["d_ps"], n + 1)
                act.wait_ge(S["o_free"], n + 1)
                nc.scalar.copy(mem.O[b][:, 0:512], bank[5]).then_inc(S["o_act"], 1)

            further[act] = act.alloc_register("further")
            act.reg_mov(further[act], 0)
            act.sem_inc(extra["o_act"], 1)

            def expert_input(l):
                for t in range(TILES):
                    act.wait_ge(norm_ready, 6 * l + 4 + t)
                    act.dma_start(h_dram[l][P * t:P * t + P, :], mem.h[:, t, :]).then_inc(h_stored[l], 16)
                t8_evict(T8_ROUTE[l])
                act.wait_ge(route_in, 2 * l + 1)
                nc.scalar.activation(mem.r12[1], mem.r12[0], ACT.Exp).then_inc(route_out, 1)
                act.wait_ge(route_in, 2 * l + 2)
                nc.scalar.activation(mem.r3[:, 6], mem.r3[:, 5], ACT.Exp).then_inc(route_out, 1)
                for i in range(2):
                    gate_evict(4 * l + 3 + i, i, 4 + 2 * i)
                load_norm(2 * l + 1)
                act.wait_ge(ids_out, 96 * (l + 1))
                act.dma_start(mem.table[:, 0:PASSES * PAIRS].rearrange("p (r n) -> p r n", r=PASSES),
                              t_dram[l].rearrange("(r p n) o -> p r (n o)", r=PASSES, p=P)).then_inc(table_in, 16)

            def mlp(l):
                S = main[l]
                act.sem_inc(S["o_act"], 1)

                def first(n, b, it):
                    gt_evict(S, n, b)
                    silu(S, n, b)
                    o_evict(S, n, b)

                def body(n, b, r, k):
                    gt_evict(extra, k, b)
                    silu(extra, k, b)
                    o_evict(extra, k, b)

                passes(act, l, S, first, body)
                act.wait_ge(S["gathered"], 16 * (PAIRS + 1))
                act.wait_ge(S["o_free"], PAIRS + 2)
                for t in range(TILES):
                    act.dma_start(mem.Y[:, t, :, :], y_dram[l].rearrange("(k t p) n -> t p k n", k=2, p=P)[t]
                                  ).then_inc(y_in[t], 16)
                if l == 0:
                    act.dma_start(mem.dft, A["k_dft"]).then_inc(dft_in, 16)

            load_norm(0)
            gate_evict(1, 0, 6)
            gate_evict(2, 1, 6)
            expert_input(0)
            mlp(0)
            act.wait_ge(col_done, 2)
            t8_evict(T8_LN[1], 1)
            for n in range(0, 4 * TILES, 2):
                t, gp = n // 4, n % 4
                act.wait_ge(chan_ps, n + 1)
                nc.scalar.copy(mem.U[:, t, 2 * gp:2 * gp + 2, :],
                               bank[(0, 1, 3, 4)[n % 4]].rearrange("p (g n) -> p g n", g=2)).then_inc(chan_act, 1)
            for g in range(0, KC, 2):
                act.wait_ge(four_ps, g + 1)
                nc.scalar.copy(mem.fT[:, g, :], bank[5 + g % 2][:, 0:TOK]).then_inc(four_act, 1)
            load_norm(2)
            gate_evict(5, 0, 6)
            gate_evict(6, 1, 6)
            expert_input(1)
            mlp(1)
            for t in range(TILES):
                act.wait_ge(x_done, t + 1)
                dst = A["y_prompt"][0] if t == 0 else A["y_sample"][0][(t - 1) * P:t * P, :]
                act.dma_start(dst, mem.x[:, t, :]).then_inc(out_done, 16)
            act.wait_ge(out_done, 16 * TILES)

        @block.vector
        def _(dve):
            V = nc.vector
            chain = [0]
            ada_count = [0]

            def link(ins):
                chain[0] += 1
                ins.then_inc(dve_chain, 1)
                dve.wait_ge(dve_chain, chain[0])

            def inverse_sqrt(y):
                v, t = mem.rs_v[:, :], mem.rs_t[:, :]
                link(V.tensor_scalar(t.bitcast(I32), v.bitcast(I32), 1, None, ALU.logical_shift_right))
                link(V.tensor_scalar(y.bitcast(I32), t.bitcast(I32), -1.0, float(0x5F3759DF), ALU.mult, ALU.add))
                for _ in range(3):
                    link(V.tensor_tensor(t, y, y, ALU.mult))
                    link(V.scalar_tensor_tensor(out=t, in0=t, scalar=-0.5, in1=v, op0=ALU.mult, op1=ALU.mult))
                    link(V.scalar_tensor_tensor(out=y, in0=t, scalar=1.5, in1=y, op0=ALU.add, op1=ALU.mult))

            def normalise(src, dst, done=None):
                for t in range(TILES):
                    for i in range(2):
                        last = V.bn_stats(mem.stats[:, t, i, :], src[:, t, 512 * i:512 * i + 512])
                link(last)
                for t in range(TILES):
                    last = V.bn_aggr(mem.mv[:, t, :], mem.stats[:, t, :, :].rearrange("p i n -> p (i n)"))
                link(last)
                link(V.tensor_scalar(mem.rs_v[:, :], mem.mv[:, :, 1], EPS, None, ALU.add))
                inverse_sqrt(mem.rstd[:, :])
                for t in range(TILES):
                    last = V.tensor_scalar(dst[:, t, :], src[:, t, :], mem.mv[:, t, 0:1], mem.rstd[:, t:t + 1],
                                           ALU.subtract, ALU.mult)
                    if done is not None:
                        last.then_inc(done, 1)
                if done is None:
                    link(last)

            def ada_add(n):
                l, u = UNITS[n][1:]
                src = bank[7 if l == 1 and u >= 4 else 3][:, 0:P]
                ada_count[0] += 1
                dve.wait_ge(ada_ps, ada_count[0])
                V.tensor_tensor(mem.m[:, l, u, :], mem.m[:, l, u, :], src, ALU.add).then_inc(ada_done, 1)

            def columns(l):
                dve.wait_ge(col_ps, l + 1)
                link(V.tensor_copy(mem.col[:, :, :, :, :].rearrange("p s u j i -> p (s u j) i"),
                                   bank[3].rearrange("p (c r) -> p c r", r=32)[:, :, 0:2]))
                V.tensor_scalar(mem.col[:, 1], mem.col[:, 1], 1.0, None, ALU.add).then_inc(col_done, 1)

            def t8_evict(use, l=None):
                for k in range(1, KC, 2):
                    dve.wait_ge(t8_ps, KC * use + k + 1)
                    if l is None:
                        last = V.tensor_copy(mem.hT[:, k, :], bank[k][:, 0:TOK])
                    else:
                        for i, (lo, hi) in enumerate(((0, P), (P, TOK))):
                            last = V.tensor_scalar(mem.hT[:, k, lo:hi], bank[k][:, lo:hi],
                                                   mem.col[:, 1, k // 4, k % 4, i:i + 1],
                                                   mem.col[:, 0, k // 4, k % 4, i:i + 1], ALU.mult, ALU.add)
                    last.then_inc(t8_dve, 1)

            dve.wait_ge(lam_in, 16 * 6)
            for i in range(2):
                V.tensor_tensor_reduce(out=mem.lamtmp, in0=mem.lam[:, 2 * i, :], in1=mem.lam[:, 2 * i + 1, :],
                                       scale=1.0, scalar=0.0, op0=ALU.mult, op1=ALU.add,
                                       accum_out=mem.lams[:, i:i + 1]).then_inc(lam_prod, 1)
                dve.wait_ge(lam_prod, i + 1)
            link(V.tensor_scalar(mem.gain8[:, :], mem.gain8[:, :], 1.0 - LAM_INIT, None, ALU.mult))
            dve.wait_ge(lam_done, 1)
            link(V.tensor_tensor(mem.lams[:, 4:5], mem.lams[:, 3:4], mem.lams[:, 2:3], ALU.subtract))
            link(V.tensor_scalar(mem.lams[:, 5:6], mem.lams[:, 4:5], -LAM_INIT, None, ALU.add))
            neg_lam = mem.lams[:, 5:6]

            dve.wait_ge(x_in, 48)
            normalise(mem.x, mem.h, norm_ready)
            dve.wait_ge(bias_in, 16 * 16)
            for u in range(4):
                ada_add(AT["ada", 0, u])
            columns(0)
            dve.wait_ge(col_done, 1)
            t8_evict(T8_LN[0], 0)

            def maximum(g):
                w = P if g % 3 == 0 else TOK
                dve.wait_ge(score_ps, g + 1)
                for j in range(2):
                    last = V.reduce_max(mem.mx[:, g % 2, j:j + 1], bank[5 + j][:, 0:w], AX)
                link(last)
                V.tensor_scalar(mem.nb[:, g % 2, :], mem.mx[:, g % 2, :], -SCALE, None, ALU.mult).then_inc(nb_done, 1)

            def difference(g):
                w = P if g % 3 == 0 else TOK
                dve.wait_ge(exp_done, 2 * g + 2)
                link(V.reciprocal(mem.rsum[:, g % 2, :], mem.ssum[:, g % 2, :]))
                link(V.scalar_tensor_tensor(out=mem.ratio[:, g % 2:g % 2 + 1], in0=mem.rsum[:, g % 2, 1:2],
                                            scalar=mem.ssum[:, g % 2, 0:1], in1=neg_lam, op0=ALU.mult, op1=ALU.mult))
                p0, p1 = mem.p[g % 2]
                V.scalar_tensor_tensor(out=p0[:, 0:w], in0=p1[:, 0:w], scalar=mem.ratio[:, g % 2:g % 2 + 1],
                                       in1=p0[:, 0:w], op0=ALU.mult, op1=ALU.add).then_inc(pd_done, 1)

            def pdT_evict(g):
                w = P if g % 3 == 0 else TOK
                dve.wait_ge(pdT_ps, g + 1)
                V.tensor_copy(mem.pdT[g % 2][:, 0:w], bank[7][:, 0:w]).then_inc(pdT_sb, 1)

            def head_norm(g):
                head, t = g // 3, g % 3
                o = mem.h[:, t, P * head:P * head + P]
                dve.wait_ge(pv_ps, g + 1)
                V.tensor_scalar(o, bank[2][:, 0:P], mem.rsum[:, g % 2, 0:1], None, ALU.mult
                                ).then_inc(o_raw, 1)
                dve.wait_ge(o_raw, g + 1)
                link(V.tensor_tensor_reduce(out=mem.sq[:, :], in0=o, in1=o, scale=1.0 / P, scalar=0.0,
                                            op0=ALU.mult, op1=ALU.add, accum_out=mem.ss[:, t:t + 1]))
                if t == TILES - 1:
                    link(V.tensor_scalar(mem.rs_v[:, :], mem.ss[:, :], EPS, None, ALU.add))
                    inverse_sqrt(mem.rs_y[:, :])
                    for i in range(TILES):
                        oi = mem.h[:, i, P * head:P * head + P]
                        V.scalar_tensor_tensor(out=oi, in0=oi, scalar=mem.rs_y[:, i:i + 1], in1=mem.gain8[:, :],
                                               op0=ALU.mult, op1=ALU.mult).then_inc(o_done, 1)

            for u in range(5):
                between = [AT["qkv", 0, u] + 1 + i for i in range(3)] if u < 4 else []
                for s in range(6):
                    g = 6 * (u - 1) + s
                    if u >= 1:
                        if s % 3 == 0:
                            dve.wait_ge(qkT_ps, g // 3 + 1)
                            V.tensor_copy(mem.kT, bank[4]).then_inc(kT_sb, 1)
                        maximum(g)
                    if g >= 1:
                        pdT_evict(g - 1)
                    if u >= 1:
                        difference(g)
                    if s % 2 == 1 and between:
                        ada_add(between[s // 2])
                    if g >= 1:
                        head_norm(g - 1)
            pdT_evict(STEPS - 1)
            head_norm(STEPS - 1)
            t8_evict(T8_O)

            def post_norm(idx, done=None):
                normalise(mem.x, mem.x)
                dve.wait_ge(gb_in, 32 * (idx + 1))
                for t in range(TILES):
                    last = V.tensor_tensor(mem.x[:, t, :], mem.x[:, t, :], mem.gb[:, 0, :], ALU.mult)
                link(last)
                for t in range(TILES):
                    last = V.tensor_tensor(mem.x[:, t, :], mem.x[:, t, :], mem.gb[:, 1, :], ALU.add)
                    if done is not None:
                        last.then_inc(done, 1)
                if done is None:
                    last.then_inc(gb_used, 1)
                    dve.wait_ge(gb_used, idx + 1)

            def mixer_output(l):
                for half in range(2):
                    for t in range(TILES):
                        i = 0 if t == 0 else 1
                        dve.wait_ge(gate_sb, 4 * l + 1 + i)
                        dve.wait_ge(proj_ps, 6 * l + 3 * half + t + 1)
                        V.tensor_tensor(mem.tmp[:, t, 512 * half:512 * half + 512], bank[3 * half + t],
                                        mem.gates[:, i, 512 * half:512 * half + 512], ALU.mult).then_inc(proj_used, 1)
                dve.wait_ge(proj_used, 6 * (l + 1))
                for t in range(TILES):
                    last = V.scalar_tensor_tensor(out=mem.x[:, t, :], in0=mem.x[:, t, :], scalar=ALPHA,
                                                  in1=mem.tmp[:, t, :], op0=ALU.mult, op1=ALU.add)
                link(last)
                post_norm(2 * l)

            def first_true(dst, tmp, eq, n, top):
                shape = [P, TILES, n]
                w = mem.const("descend")[:, 8 - n:8].unsqueeze(1)
                link(V.tensor_tensor(tmp, eq, bc(w, shape), ALU.mult))
                link(V.tensor_reduce(top, tmp, AX, ALU.max))
                link(V.tensor_tensor(dst, tmp, bc(top.unsqueeze(2), shape), ALU.is_equal))

            def route(l):
                r3, r12, r24 = mem.r3, mem.r12, mem.r24
                s4, s8, s32 = [P, TILES, GROUPS], [P, TILES, PER_GROUP], [P, TILES, GROUPS, PER_GROUP]
                dve.wait_ge(logits_ps, l + 1)
                link(V.tensor_copy(mem.L.rearrange("p t n -> p (t n)"), bank[0][:, 0:TILES * NLOG]))
                lg = mem.L[:, :, 0:GROUPS]
                le = mem.L[:, :, GROUPS:].rearrange("p t (g e) -> p t g e", g=GROUPS)
                link(V.tensor_reduce(r3[:, 0], lg, AX, ALU.max))
                V.tensor_tensor(r12[0], lg, bc(r3[:, 0].unsqueeze(2), s4), ALU.subtract).then_inc(route_in, 1)
                link(V.tensor_tensor(r12[2], lg, bc(r3[:, 0].unsqueeze(2), s4), ALU.is_equal))
                first_true(r12[2], r12[3], r12[2], GROUPS, r3[:, 1])
                group = r12[2]
                link(V.tensor_tensor(mem.r96, le, bc(group.unsqueeze(3), s32), ALU.mult))
                link(V.tensor_reduce(r24[0], mem.r96.rearrange("p t g e -> p t e g"), AX, ALU.add))
                link(V.tensor_reduce(r3[:, 2], r24[0], AX, ALU.max))
                link(V.tensor_tensor(r24[1], r24[0], bc(r3[:, 2].unsqueeze(2), s8), ALU.is_equal))
                first_true(r24[2], r24[3], r24[1], PER_GROUP, r3[:, 3])
                link(V.scalar_tensor_tensor(out=r24[4], in0=r24[2], scalar=-3.0e38, in1=r24[0],
                                            op0=ALU.mult, op1=ALU.add))
                link(V.tensor_reduce(r3[:, 4], r24[4], AX, ALU.max))
                V.tensor_tensor(r3[:, 5], r3[:, 4], r3[:, 2], ALU.subtract).then_inc(route_in, 1)
                link(V.tensor_tensor(r24[5], r24[4], bc(r3[:, 4].unsqueeze(2), s8), ALU.is_equal))
                first_true(r24[6], r24[7], r24[5], PER_GROUP, r3[:, 7])
                for k, one in enumerate((r24[2], r24[6])):
                    for g in range(GROUPS):
                        last = V.tensor_tensor(mem.M[k][:, :, PER_GROUP * g:PER_GROUP * g + PER_GROUP], one,
                                               bc(group[:, :, g:g + 1], s8), ALU.mult)
                link(last)
                V.tensor_tensor(mem.Msum, mem.M[0], mem.M[1], ALU.add).then_inc(msum_done, 1)
                dve.wait_ge(route_out, 2 * l + 2)
                link(V.tensor_reduce(r3[:, 8], r12[1], AX, ALU.add))
                link(V.tensor_scalar(r3[:, 9], r3[:, 6], 1.0, None, ALU.add))
                link(V.tensor_tensor(r3[:, 10], r3[:, 8], r3[:, 9], ALU.mult))
                link(V.reciprocal(mem.w[:, 0, :], r3[:, 10]))
                link(V.tensor_tensor(mem.w[:, 1, :], mem.w[:, 0, :], r3[:, 6], ALU.mult))
                dve.wait_ge(pos_ps, l + 1)
                pos = bank[1][:, 0:TILES * EXPERTS]
                base = bc(mem.const("slotbase").unsqueeze(1), [P, TILES, EXPERTS])
                counts = bank[1][:, TILES * EXPERTS:(TILES + 1) * EXPERTS].rearrange("p (n e) -> p n e", e=2)
                link(V.tensor_reduce(mem.pairmax, counts, AX, ALU.max))
                s80 = [P, PAIRS, PASSES - 1]
                link(V.tensor_tensor(mem.r80, bc(mem.pairmax.unsqueeze(2), s80), bc(mem.const("thresholds").unsqueeze(1), s80),
                                     ALU.is_gt))
                link(V.tensor_reduce(mem.further, mem.r80, AX, ALU.add))
                link(V.tensor_tensor(mem.further, mem.further, mem.const("octal"), ALU.mult))
                link(V.tensor_reduce(mem.words_f[:, :], mem.further.rearrange("p (h n) -> p h n", h=2), AX, ALU.add))
                V.tensor_copy(mem.words[:, :], mem.words_f[:, :]).then_inc(words_done, 1)
                for i, what in enumerate((pos.rearrange("p (t e) -> p t e", t=TILES), base)):
                    for k in range(2):
                        last = V.tensor_tensor(mem.Mt[:, TILES * k:TILES * k + TILES, :], mem.M[k], what, ALU.mult)
                    link(last)
                    link(V.tensor_reduce(mem.r6[:, i], mem.Mt, AX, ALU.add))
                link(V.tensor_tensor(mem.r30, bc(mem.r6[:, 0].unsqueeze(2), [P, 6, PASSES - 1]),
                                     bc(mem.const("thresholds").unsqueeze(1), [P, 6, PASSES - 1]), ALU.is_ge))
                link(V.tensor_reduce(mem.r6[:, 2], mem.r30, AX, ALU.add))
                link(V.scalar_tensor_tensor(out=mem.r6[:, 3], in0=mem.r6[:, 0], scalar=float(PAIRS), in1=mem.r6[:, 1],
                                            op0=ALU.mult, op1=ALU.add))
                link(V.scalar_tensor_tensor(out=mem.r6[:, 4], in0=mem.r6[:, 2], scalar=float(PAIRS * CAP),
                                            in1=mem.r6[:, 3], op0=ALU.mult, op1=ALU.add))
                V.tensor_copy(mem.slot[:, :], mem.r6[:, 4]).then_inc(slot_done, 1)
                dve.wait_ge(table_in, 16 * (l + 1))
                link(V.tensor_copy(mem.table_f, mem.table[:, 0:PASSES * PAIRS]))
                link(V.tensor_scalar(mem.table_g, mem.table_f, float(TOK), float(TOK), ALU.is_ge, ALU.mult))
                link(V.tensor_tensor(mem.table_g, mem.table_f, mem.table_g, ALU.subtract))
                V.tensor_copy(mem.source[:, 0:PASSES * PAIRS], mem.table_g).then_inc(source_done, 1)

            def expert_input(l):
                normalise(mem.x, mem.h)
                for t in range(TILES):
                    i = 0 if t == 0 else 1
                    dve.wait_ge(rows_ps, 2 * l + 1 + i)
                    link(V.scalar_tensor_tensor(out=mem.h[:, t, :], in0=mem.psum[:, 2048 * i:2048 * i + D], scalar=1.0,
                                                in1=mem.h[:, t, :], op0=ALU.add, op1=ALU.mult))
                    V.tensor_tensor(mem.h[:, t, :], mem.h[:, t, :], mem.psum[:, 2048 * i + D:2048 * i + 2 * D], ALU.add
                                    ).then_inc(norm_ready, 1)
                t8_evict(T8_ROUTE[l])
                route(l)

            def gt_evict(S, n, b):
                dve.wait_ge(S["gt_ps"], n + 1)
                V.tensor_copy(mem.GT[b][:, 4:8, :], bank[3].rearrange("p (c s) -> p c s", c=4)
                              ).then_inc(S["gt_dve"], 1)

            def up_times(S, n, b):
                dve.wait_ge(S["sil"], n + 1)
                V.tensor_tensor(mem.act[b], mem.sil[b], bank[b][:, FE:2 * FE], ALU.mult).then_inc(S["act"], 1)

            def at_evict(S, n, b):
                dve.wait_ge(S["at_ps"], n + 1)
                V.tensor_copy(mem.actT[b], bank[4][:, 0:2 * P].rearrange("p (f s) -> p f s", f=2)
                              ).then_inc(S["at_sb"], 1)

            def o_evict(S, n, b):
                dve.wait_ge(S["d_ps"], n + 1)
                dve.wait_ge(S["o_free"], n + 1)
                V.tensor_copy(mem.O[b][:, 512:D], bank[6]).then_inc(S["o_dve"], 1)

            further[dve] = dve.alloc_register("further")
            dve.reg_mov(further[dve], 0)
            dve.sem_inc(extra["o_dve"], 1)

            def mlp(l):
                S = main[l]
                dve.sem_inc(S["o_dve"], 1)

                def work(S, n, b):
                    gt_evict(S, n, b)
                    up_times(S, n, b)
                    at_evict(S, n, b)
                    o_evict(S, n, b)

                passes(dve, l, S, lambda n, b, it: work(S, n, b), lambda n, b, r, k: work(extra, k, b))

            def combine(l):
                for t in range(TILES):
                    i = 0 if t == 0 else 1
                    dve.wait_ge(y_in[t], 16 * (l + 1))
                    y0, y1 = mem.Y[:, t, 0, :], mem.Y[:, t, 1, :]
                    link(V.tensor_scalar(y0, y0, mem.w[:, 0, t:t + 1], None, ALU.mult))
                    link(V.scalar_tensor_tensor(out=y0, in0=y1, scalar=mem.w[:, 1, t:t + 1], in1=y0,
                                                op0=ALU.mult, op1=ALU.add))
                    link(V.tensor_tensor(y0, y0, mem.gates[:, i, :], ALU.mult))
                    link(V.scalar_tensor_tensor(out=mem.x[:, t, :], in0=mem.x[:, t, :], scalar=ALPHA, in1=y0,
                                                op0=ALU.mult, op1=ALU.add))

            for b in range(2):
                dve.wait_ge(kv_stored[b], 64)
            mixer_output(0)
            expert_input(0)
            mlp(0)
            columns(1)
            combine(0)
            post_norm(1)
            normalise(mem.x, mem.h, norm_ready)
            dve.wait_ge(col_done, 2)
            t8_evict(T8_LN[1], 1)
            for n in range(1, 4 * TILES, 2):
                t, gp = n // 4, n % 4
                dve.wait_ge(chan_ps, n + 1)
                V.tensor_copy(mem.U[:, t, 2 * gp:2 * gp + 2, :],
                              bank[(0, 1, 3, 4)[n % 4]].rearrange("p (g n) -> p g n", g=2)).then_inc(chan_dve, 1)
                for i in range(n - 1, n + 1):
                    if i < 8:
                        ada_add(AT["ada", 1, 4 + i])
            for g in range(1, KC, 2):
                dve.wait_ge(four_ps, g + 1)
                V.tensor_copy(mem.fT[:, g, :], bank[5 + g % 2][:, 0:TOK]).then_inc(four_dve, 1)
            mixer_output(1)
            expert_input(1)
            mlp(1)
            combine(1)
            post_norm(3, x_done)


_INS = ["x_prompt", "x_sample", "cache_k", "cache_v", "c", "c_ctx", "w_ada", "b_ada", "ln_gain", "ln_bias", "w_qkv",
        "w_attn_out", "lambda_q1", "lambda_k1", "lambda_q2", "lambda_k2", "subln_gain", "w_fourier_out",
        "w_router_group", "w_router_expert", "w_expert_gate", "w_expert_up", "w_expert_down"]
_OUTS = [("y_prompt", (1, P, D)), ("y_sample", (1, 2 * P, D)), ("new_cache_k", (1, 1, P, HEADS, 2 * HD)),
         ("new_cache_v", (1, 1, P, HEADS, 2 * HD))]


def kernel(**inputs):
    import concourse.bacc as bacc
    from concourse.bass_utils import run_bass_kernel_spmd

    nc = bacc.Bacc("TRN2", target_bir_lowering=False, num_devices=1)
    arrays = {name: np.ascontiguousarray(inputs[name]) for name in _INS}
    arrays.update(constants())
    aps = {name: nc.dram_tensor(f"in_{name}", a.shape, mybir.dt.from_np(a.dtype), kind="ExternalInput").ap()
           for name, a in arrays.items()}
    for name, shape in _OUTS:
        aps[name] = nc.dram_tensor(f"out_{name}", shape, F32, kind="ExternalOutput").ap()
    build(nc, aps)
    r = run_bass_kernel_spmd(nc, [{f"in_{name}": a for name, a in arrays.items()}], core_ids=[0])
    return tuple(r.results[0][f"out_{name}"] for name, _ in _OUTS)
```

```python
import math
from contextlib import ExitStack

import numpy as np

import concourse.bass as bass
from concourse import mybir

F32 = mybir.dt.float32
I32 = mybir.dt.int32
U32 = mybir.dt.uint32
ALU = mybir.AluOpType
ACT = mybir.ActivationFunctionType
AX = mybir.AxisListType.X

P = 128
D = 1024
KC = D // P
TILES = 3
TOK = TILES * P
HEADS = 8
HD = 64
NMOD = 6
GROUPS, PER_GROUP = 4, 8
EXPERTS = GROUPS * PER_GROUP
FE = 256
CAP = 64
PAIRS = EXPERTS // 2
PASSES = TOK // CAP
NLOG = GROUPS + EXPERTS
SLOTS = 4
SLOT = 6 * D
EPS = 1e-5
ALPHA = (2.0 * 2) ** 0.25
LAM_INIT = 0.8 - 0.6 * math.exp(0.0)
SCALE = HD ** -0.5
INVALID = 4096
ADA_UNITS = NMOD * D // 512
QK_W = 768
STEPS = 3 * HEADS

UNITS = [("ada", 0, u) for u in range(4)]
_rest = [("ada", 0, u) for u in range(4, ADA_UNITS)] + [("ada", 1, u) for u in range(4)]
for _u in range(4):
    UNITS += [("qkv", 0, _u)] + _rest[3 * _u:3 * _u + 3]
UNITS += [("out", 0, 0), ("out", 0, 1)]
MOE_BASE = [len(UNITS)]
UNITS += [("expert", 0, e) for e in range(EXPERTS)]
UNITS += [("ada", 1, u) for u in range(4, ADA_UNITS)] + [("out", 1, 0), ("out", 1, 1)]
MOE_BASE.append(len(UNITS))
UNITS += [("expert", 1, e) for e in range(EXPERTS)]
AT = {unit: n for n, unit in enumerate(UNITS)}
DMAS = {"ada": 1, "qkv": 3, "out": 1, "expert": 2}
LANDED = []
_sum = [0] * SLOTS
for _n, (_kind, _, _) in enumerate(UNITS):
    _sum[_n % SLOTS] += 16 * DMAS[_kind]
    LANDED.append(_sum[_n % SLOTS])

_C = {}
_at = 0
for _name, _w in (("ident", P), ("tri", P), ("ones", P), ("sel", 8 * P), ("cos", 2 * HD), ("sin", 2 * HD),
                  ("slotbase", EXPERTS), ("thresholds", PASSES - 1), ("descend", 8), ("octal", PAIRS), ("rowcode", P)):
    _C[_name] = (_at, _at + _w)
    _at += _w
NCONST = _at
NDFT = 2 * P + 2 * P + 4 * 2 * P


def constants():
    c = np.zeros((P, NCONST), np.float64)

    def put(name, a):
        c[:, _C[name][0]:_C[name][1]] = np.asarray(a).reshape(np.asarray(a).shape[0], -1)

    put("ident", np.eye(P))
    put("tri", np.triu(np.ones((P, P)), 1))
    put("ones", np.ones((P, P)))
    sel = np.zeros((P, 4, 2, P))
    for j in range(4):
        for i in range(2):
            sel[32 * j + i, j, i, :] = 1.0
    put("sel", sel)
    nf = HD // 4
    inv = np.float32(10000.0) ** (-np.arange(nf, dtype=np.float32) / nf)
    tok = np.arange(2 * P)
    pos = np.stack([tok // 64, tok % 64], 1).astype(np.float32)
    ang = (pos[:, :, None] * inv.astype(np.float32)).astype(np.float32)
    cos, sin = np.cos(ang.astype(np.float64)), np.sin(ang.astype(np.float64))
    full_c = np.concatenate([cos, cos], -1).reshape(2, P, HD).transpose(1, 0, 2)
    full_s = np.concatenate([-sin, sin], -1).reshape(2, P, HD).transpose(1, 0, 2)
    put("cos", full_c)
    put("sin", full_s)
    e = np.arange(EXPERTS)
    put("slotbase", np.tile((e % 2) * (CAP * PAIRS) + e // 2, (P, 1)))
    put("thresholds", np.tile(CAP * np.arange(1, PASSES), (P, 1)))
    put("octal", np.tile(8.0 ** (np.arange(PAIRS) % 8), (P, 1)))
    put("rowcode", np.tile(PAIRS * np.arange(P), (P, 1)))
    put("descend", np.tile(8 - np.arange(8), (P, 1)))

    def dft(n, scale):
        a = 2 * np.pi * (np.outer(np.arange(n), np.arange(n)) % n) / n
        return np.cos(a) * scale, np.sin(a) * scale

    cc, sc = dft(P, 1.0)
    cp, sp = dft(P, 1.0 / P)
    cl, sl = dft(2 * P, (2 * P * P) ** -0.5)
    lat = np.stack([cl, -sl], 1).reshape(2, P, 2, 2 * P).transpose(1, 0, 2, 3)
    table = np.concatenate([cc, sc, cp, -sp, lat.reshape(P, -1)], 1)
    ids = np.arange(P)[:, None, None] + P * np.arange(TILES)[None, None, :] + TOK * np.arange(2)[None, :, None]
    empty = np.full((P, PASSES * PAIRS), INVALID)
    ints = np.concatenate([ids.reshape(P, -1), empty], 1)
    return {"k_rows": c.astype(np.float32), "k_dft": table.astype(np.float32), "k_ints": ints.astype(np.int32)}


class Memory:

    def __init__(self, nc, ctx):
        def sb(name, shape, dt=F32):
            return ctx.enter_context(nc.sbuf_tensor(name, shape, dt))

        self.ring = sb("ring", [P, SLOTS, SLOT])
        self.x = sb("x", [P, TILES, D])
        self.h = sb("h", [P, TILES, D])
        self.hT = sb("hT", [P, KC, TOK])
        self.m = sb("m", [P, 2, ADA_UNITS, P])
        self.rows = sb("k_rows_sb", [P, NCONST])
        self.ints = sb("k_ints_sb", [P, 6 + PASSES * PAIRS], I32)
        self.wr = sb("wr", [P, 2, KC, NLOG])
        self.cond = sb("cond", [2 * KC, P])
        self.silu = sb("silu", [P, KC, 32])
        self.col = sb("col", [P, 2, 2, 4, 2])
        self.lams = sb("lams", [P, 8])
        self.gain8 = sb("gain8", [P, P])
        self.stats = sb("stats", [P, TILES, 2, 6])
        self.mv = sb("mv", [P, TILES, 2])
        self.rstd = sb("rstd", [P, TILES])
        self.mx = sb("mx", [P, 2, 2])
        self.nb = sb("nb", [P, 2, 2])
        self.ssum = sb("ssum", [P, 2, 2])
        self.rsum = sb("rsum", [P, 2, 2])
        self.ratio = sb("ratio", [P, 2])
        self.sq = sb("sq", [P, P])
        self.ss = sb("ss", [P, TILES])
        self.rs_v = sb("rs_v", [P, TILES])
        self.rs_t = sb("rs_t", [P, TILES])
        self.rs_y = sb("rs_y", [P, TILES])
        self.w = sb("w", [P, 2, TILES])
        self.slot = sb("slot", [P, 6], I32)
        self.words_f = sb("words_f", [P, 2])
        self.words = sb("words", [P, 2], I32)
        self.table = sb("table", [P, 8 * PAIRS], I32)
        self.place = sb("place", [P, 6])
        self.place_x = sb("place_x", [P, 6])
        self.sidx = sb("sidx", [P, 2], I32)
        K = 256
        self.arena = a = sb("arena", [P, 50 * K])

        def view(at, size):
            return a[:, int(at * K):int(at * K) + size]

        self.qkv = [view(9 * b, TILES * QK_W).rearrange("p (t n) -> p t n", t=TILES) for b in range(2)]
        self.qT = view(18, TOK)
        self.kT = view(19.5, TOK + P)
        self.rope_a = view(21.5, 512)
        self.rope_b = view(23.5, 512)
        self.ctxk = view(25.5, D)
        self.ctxv = view(29.5, D)
        self.p = [[view(33.5 + 3 * b + 1.5 * j, TOK) for j in range(2)] for b in range(2)]
        self.pdT = [view(39.5 + 1.5 * b, TOK) for b in range(2)]
        self.lam = view(33.5, 4 * HD).rearrange("p (n d) -> p n d", n=4)
        self.lamtmp = view(34.5, HD)
        at = [16 * K]

        def small(*shape):
            n = int(np.prod(shape))
            v = a[:, at[0]:at[0] + n]
            at[0] += n
            names = "abc"[:len(shape)]
            return v.rearrange(f"p ({' '.join(names)}) -> p {' '.join(names)}",
                               **dict(zip(names[1:], shape[1:]))) if len(shape) > 1 else v

        self.L = small(TILES, NLOG)
        self.r3 = small(16, TILES)
        self.r12 = [small(TILES, GROUPS) for _ in range(4)]
        self.r24 = [small(TILES, PER_GROUP) for _ in range(8)]
        self.r96 = small(TILES, GROUPS, PER_GROUP)
        self.M = [small(TILES, EXPERTS) for _ in range(2)]
        self.Msum = small(TILES, EXPERTS)
        self.Mt = small(2 * TILES, EXPERTS)
        self.r6 = small(5, 6)
        self.r30 = small(6, PASSES - 1)
        self.pairmax = small(PAIRS)
        self.r80 = small(PAIRS, PASSES - 1)
        self.further = small(PAIRS)
        self.tmp = view(0, TILES * D).rearrange("p (t n) -> p t n", t=TILES)
        self.U = view(0, TILES * KC * 2 * P).rearrange("p (t g n) -> p t g n", t=TILES, g=KC)
        self.dft = view(24, NDFT)
        self.gates = view(30, 2 * D).rearrange("p (i n) -> p i n", i=2)
        self.gb = view(38, 2 * D).rearrange("p (i n) -> p i n", i=2)
        self.sel = view(0, TOK).rearrange("p (t s) -> p t s", t=TILES)
        self.GT = [view(8 + 4 * b, D).rearrange("p (c s) -> p c s", c=KC) for b in range(2)]
        self.sil = [view(16 + b, FE) for b in range(2)]
        self.act = [view(18 + b, FE) for b in range(2)]
        self.actT = [view(20 + b, 2 * P).rearrange("p (f s) -> p f s", f=2) for b in range(2)]
        self.O = [view(22 + 4 * b, D) for b in range(2)]
        self.Y = view(0, TILES * 2 * D).rearrange("p (t k n) -> p t k n", t=TILES, k=2)
        self.psum = ctx.enter_context(nc.psum_tensor("psum", [P, 8 * 512], F32))
        self.bank = [self.psum[:, 512 * b:512 * b + 512] for b in range(8)]
        self.fT = self.h[:, :, :].rearrange("p t n -> p (t n)").rearrange("p (k n) -> p k n", k=KC)

    def const(self, name):
        return self.rows[:, _C[name][0]:_C[name][1]]

    def unit(self, n):
        return self.ring[:, n % SLOTS, :]


def bc(ap, shape):
    return ap.to_broadcast(shape)


def build(nc, A):
    ctx = ExitStack()
    with ctx:
        mem = Memory(nc, ctx)
        bank = mem.bank
        ident = mem.const("ident")

        sems = {}

        def sem(name):
            if name not in sems:
                sems[name] = ctx.enter_context(nc.semaphore(name))
            return sems[name]

        y_dram = [nc.dram_tensor(f"y_scratch{l}", (2 * TOK, D), F32).ap() for l in range(2)]
        t_dram = [nc.dram_tensor(f"table_scratch{l}", (PASSES * PAIRS * P, 1), I32).ap() for l in range(2)]

        cond_in, rows_in, router_in, x_in, lam_in, ctx_in, ints_in = (
            sem(n) for n in ("cond_in", "rows_in", "router_in", "x_in", "lam_in", "ctx_in", "ints_in"))
        bias_in, zeroed, table_clear = sem("bias_in"), sem("zeroed"), sem("table_clear")
        landed = [sem(f"slot_landed{i}") for i in range(SLOTS)]
        down_landed = [sem(f"down_landed{i}") for i in range(SLOTS)]
        cond_ps, silu_done = sem("cond_ps"), sem("silu_done")
        ada_ps, ada_done = sem("ada_ps"), sem("ada_done")
        col_ps, col_done = sem("col_ps"), sem("col_done")
        norm_ready = sem("norm_ready")
        t8_ps, t8_act, t8_dve = sem("t8_ps"), sem("t8_act"), sem("t8_dve")
        qkv_ps, qkv_sb, rope_done = sem("qkv_ps"), sem("qkv_sb"), sem("rope_done")
        kv_stored = [sem(f"kv_stored{b}") for b in range(2)]
        qkT_ps, qT_sb, kT_sb = sem("qkT_ps"), sem("qT_sb"), sem("kT_sb")
        score_ps, nb_done, exp_done = sem("score_ps"), sem("nb_done"), sem("exp_done")
        pd_done, pdT_ps, pdT_sb, pv_ps, o_done = (sem(n) for n in ("pd_done", "pdT_ps", "pdT_sb", "pv_ps", "o_done"))
        lam_done, o_raw = sem("lam_done"), sem("o_raw")
        gate_ps, gate_sb = sem("gate_ps"), sem("gate_sb")
        proj_ps, proj_used = sem("proj_ps"), sem("proj_used")
        gb_in, gb_used = sem("gb_in"), sem("gb_used")
        rows_ps = sem("rows_ps")
        turn_ps, turn_lo, turn_hi = sem("turn_ps"), sem("turn_lo"), sem("turn_hi")
        y_scaled = sem("y_scaled")
        logits_ps, route_in, route_out, pos_ps, msum_done = (
            sem(n) for n in ("logits_ps", "route_in", "route_out", "pos_ps", "msum_done"))
        slot_done, ids_out, table_in, words_done, mlp_end = (
            sem(n) for n in ("slot_done", "ids_out", "table_in", "words_done", "mlp_end"))
        dft_in, chan_ps, chan_act, chan_dve = sem("dft_in"), sem("chan_ps"), sem("chan_act"), sem("chan_dve")
        four_ps, four_act, four_dve = sem("four_ps"), sem("four_act"), sem("four_dve")
        y_in = [sem(f"y_in{t}") for t in range(TILES)]
        x_done, out_done, lam_prod = sem("x_done"), sem("out_done"), sem("lam_prod")
        turns = sem("turns")
        gate_up_through, down_through = sem("gate_up_through"), sem("down_through")
        dve_chain, act_chain, pool_chain = sem("dve_chain"), sem("act_chain"), sem("pool_chain")

        def moe_sems(tag):
            names = ("place", "sel_first", "sel", "sidx", "gt_ps", "gt_act", "gt_dve", "u_ps", "sil", "act", "at_ps", "at_sb", "d_ps",
                     "o_act", "o_dve", "scattered", "o_free")
            return {n: sem(f"{n}_{tag}") for n in names}

        main = [moe_sems(f"main{l}") for l in range(2)]
        extra = moe_sems("extra")

        def passes(eng, l, S, first, body, start=None):
            eng.wait_ge(words_done, l + 1)
            with eng.Fori(0, 2) as half:
                word = eng.value_load(mem.words[0:1, bass.ds(half, 1)], min_val=0, max_val=(1 << 24) - 1)
                with eng.Fori(0, PAIRS // 4) as it:
                    for b in range(2):
                        n = half * (PAIRS // 2) + it * 2 + b
                        first(n, b, half * (PAIRS // 4) + it)
                        times = eng.snap((word >> (it * 6 + 3 * b)) & 7, min_val=0, max_val=PASSES - 1)
                        with eng.If(times > 0):
                            with eng.Fori(0, times) as r:
                                body(n, b, r + 1, eng.snap(further[eng]))
                                eng.reg_add(further[eng], further[eng], 1)
                        if start is not None:
                            start(n, b)

        further = {}
        block = ctx.enter_context(nc.Block())

        T8_LN, T8_O = 0, 1
        TURN_ROUTE, TURN_LN = [0, 2], 1

        def wait_unit(eng, n):
            eng.wait_ge(landed[n % SLOTS], LANDED[n])

        ADA_ORDER = [n for n, unit in enumerate(UNITS) if unit[0] == "ada"]

        def wait_used(eng, n):
            kind, l, u = UNITS[n]
            if kind == "ada":
                eng.wait_ge(ada_ps, ADA_ORDER.index(n) + 1)
            elif kind == "qkv":
                eng.wait_ge(qkv_ps, 6 * u + 6)
            elif kind == "out":
                eng.wait_ge(proj_ps, 6 * l + 3 * u + 3)
            elif u // 2 < PAIRS - 1:
                eng.wait_ge(main[l]["gt_ps"], u // 2 + 3)
            else:
                eng.wait_ge(mlp_end, l + 1)
                for t in range(TILES):
                    eng.wait_ge(y_in[t], 16 * (l + 1))

        def wait_turn(eng, use, t):
            eng.wait_ge(turn_lo, TILES * use + t + 1)
            eng.wait_ge(turn_hi, TILES * use + t + 1)

        def wait_t8(eng, use):
            eng.wait_ge(t8_act, 4 * (use + 1))
            eng.wait_ge(t8_dve, 4 * (use + 1))

        @block.sync
        def _(sp):
            sp.dma_start(mem.rows[:, :], A["k_rows"]).then_inc(rows_in, 16)

            def load_gate_up(slot, l, e):
                for part, name in enumerate(("w_expert_gate", "w_expert_up")):
                    sp.dma_start(mem.ring[:, slot, part * 2 * D:(part + 1) * 2 * D],
                                 A[name][l][bass.ds(e, 1)].rearrange("o (p k) n -> p (o k n)", p=P)
                                 ).then_inc(landed[slot], 16)

            def load_down(slot, l, e):
                sp.dma_start(mem.ring[:, slot, 4 * D:], A["w_expert_down"][l][bass.ds(e, 1)].rearrange(
                    "o (p k) n -> p (o k n)", p=P)).then_inc(down_landed[slot], 16)

            def load(n):
                kind, l, u = UNITS[n]
                if n >= SLOTS:
                    wait_used(sp, n - SLOTS)
                dst, done = mem.unit(n), landed[n % SLOTS]
                if kind == "ada":
                    sp.dma_start(dst[:, 0:KC * 512].rearrange("p (k n) -> p k n", k=KC),
                                 A["w_ada"][l].rearrange("(k p) n -> p k n", p=P)[:, :, 512 * u:512 * u + 512]
                                 ).then_inc(done, 16)
                elif kind == "qkv":
                    w = A["w_qkv"][0].rearrange("(k p) n -> p k n", p=P)
                    for part in range(3):
                        sp.dma_start(dst.rearrange("p (k n) -> p k n", k=KC)[:, :, 256 * part:256 * part + 256],
                                     w[:, :, D * part + 256 * u:D * part + 256 * u + 256]).then_inc(done, 16)
                elif kind == "out":
                    w = A["w_attn_out"][0] if l == 0 else A["w_fourier_out"][0]
                    sp.dma_start(dst[:, 0:KC * 512].rearrange("p (k n) -> p k n", k=KC),
                                 w.rearrange("(k p) n -> p k n", p=P)[:, :, 512 * u:512 * u + 512]
                                 ).then_inc(done, 16)
                else:
                    load_gate_up(n % SLOTS, l, u)
                    load_down(n % SLOTS, l, u)

            further[sp] = sp.alloc_register("further")
            sp.reg_mov(further[sp], 1)
            load(0)
            for t in range(TILES):
                src = A["x_prompt"][0] if t == 0 else A["x_sample"][0][(t - 1) * P:t * P, :]
                sp.dma_start(mem.x[:, t, :], src).then_inc(x_in, 16)
            for n in range(1, MOE_BASE[0]):
                load(n)
            for l in range(2):
                base = MOE_BASE[l]
                for n in range(base, base + SLOTS):
                    load(n)
                sp.wait_ge(words_done, l + 1)
                for half in range(2):
                    word = sp.value_load(mem.words[0:1, half:half + 1], min_val=0, max_val=(1 << 24) - 1)
                    with sp.Fori(0, PAIRS // 4 - half) as it:
                        for b in range(2):
                            n = half * (PAIRS // 2) + it * 2 + b
                            times = sp.snap((word >> (it * 6 + 3 * b)) & 7, min_val=0, max_val=PASSES - 1)
                            first_done = sp.snap(n + 1)
                            sp.reg_add(further[sp], further[sp], times)
                            all_done = sp.snap(further[sp])
                            slots = [(base + 2 * b + e) % SLOTS for e in range(2)]
                            experts = [sp.snap(2 * n + 4 + e) for e in range(2)]
                            sp.wait_ge(main[l]["u_ps"], first_done)
                            sp.wait_ge(gate_up_through, all_done)
                            for e in range(2):
                                load_gate_up(slots[e], l, experts[e])
                            sp.wait_ge(main[l]["d_ps"], first_done)
                            sp.wait_ge(down_through, all_done)
                            for e in range(2):
                                load_down(slots[e], l, experts[e])
                if l == 0:
                    for n in range(base + EXPERTS, MOE_BASE[1]):
                        load(n)

        @block.gpsimd
        def _(pool):
            chain = [0]

            def link(ins):
                chain[0] += 1
                ins.then_inc(pool_chain, 1)
                pool.wait_ge(pool_chain, chain[0])

            pool.memset(mem.silu[:, :, :], 0.0).then_inc(zeroed, 1)
            pool.memset(mem.m[:, :, :, :], 0.0).then_inc(zeroed, 1)
            pool.dma_start(mem.ints[:, :], A["k_ints"]).then_inc(ints_in, 16)
            for l in range(2):
                pool.dma_start(t_dram[l].rearrange("(p n) o -> p (n o)", p=P), A["k_ints"][:, 6:]).then_inc(table_clear, 16)
            pool.wait_ge(rows_in, 16)

            cos = mem.const("cos").rearrange("p (t n) -> p t n", t=2)
            sin = mem.const("sin").rearrange("p (t n) -> p t n", t=2)
            for u in range(4):
                buf = mem.qkv[u % 2]
                for t in (1, 2):
                    pool.wait_ge(qkv_sb, 6 * u + 2 * t)
                    x8 = buf[:, t, 0:512].rearrange("p (g n) -> p g n", n=HD)
                    x4 = buf[:, t, 0:512].rearrange("p (g s n) -> p g s n", s=2, n=16)
                    b4 = mem.rope_b.rearrange("p (g s n) -> p g s n", s=2, n=16)
                    sg = sin[:, t - 1, :].rearrange("p (a s n) -> p a s n", a=2, s=2)
                    pool.tensor_tensor(mem.rope_a.rearrange("p (g n) -> p g n", n=HD), x8,
                                       bc(cos[:, t - 1, :].unsqueeze(1), [P, 8, HD]), ALU.mult)
                    for s in range(2):
                        last = pool.tensor_tensor(
                            b4[:, :, s, :].rearrange("p (g a) n -> p g a n", a=2),
                            x4[:, :, 1 - s, :].rearrange("p (g a) n -> p g a n", a=2),
                            bc(sg[:, :, s, :].unsqueeze(1), [P, 8, 2, 16]), ALU.mult)
                    link(last)
                    link(pool.tensor_tensor(buf[:, t, 0:512], mem.rope_a, mem.rope_b, ALU.add))
                pool.sem_inc(rope_done, 1)
                pool.wait_ge(qkv_sb, 6 * u + 6)
                pool.dma_start(A["new_cache_k"][0, 0].rearrange("s h d -> s (h d)")[:, 256 * u:256 * u + 256],
                               buf[:, 0, 256:512]).then_inc(kv_stored[u % 2], 16)
                pool.dma_start(A["new_cache_v"][0, 0].rearrange("s h d -> s (h d)")[:, 256 * u:256 * u + 256],
                               buf[:, 0, 512:768]).then_inc(kv_stored[u % 2], 16)

            def value(x):
                return x if isinstance(x, int) else pool.snap(x)

            further[pool] = pool.alloc_register("further")
            pool.reg_mov(further[pool], 0)
            out_bound = pool.snap(pool.to_reg(2 * TOK - 1))
            table_bound = pool.snap(pool.to_reg(PASSES * PAIRS * P - 1))

            def scatter(S, l, col, n, b):
                pool.tensor_copy(mem.sidx[:, b:b + 1], mem.table[:, bass.ds(col, 1)]).then_inc(S["sidx"], 1)
                n1, n2, n16 = value(n + 1), value(n + 2), value(16 * n + 16)
                pool.wait_ge(S["sidx"], n1)
                pool.wait_ge(S["o_act"], n2)
                pool.wait_ge(S["o_dve"], n2)
                pool.sem_inc(turns, 1)
                pool.indirect_dma_start(y_dram[l],
                                        bass.IndirectOffsetOnAxis(ap=mem.sidx[:, b:b + 1].bitcast(U32), axis=0),
                                        mem.O[b], None, bounds_check=out_bound, oob_is_err=False
                                        ).then_inc(S["scattered"], 16)
                pool.wait_ge(S["scattered"], n16)

            for l in range(2):
                S = main[l]
                pool.wait_ge(ints_in, 16)
                pool.wait_ge(table_clear, 32)
                pool.wait_ge(slot_done, l + 1)
                for c in range(6):
                    pool.indirect_dma_start(t_dram[l],
                                            bass.IndirectOffsetOnAxis(ap=mem.slot[:, c:c + 1].bitcast(U32), axis=0),
                                            mem.ints[:, c:c + 1], None, bounds_check=table_bound,
                                            oob_is_err=False).then_inc(ids_out, 16)
                pool.wait_ge(table_in, 16 * (l + 1))
                pool.sem_inc(S["o_free"], 2)

                def first(n, b, it):
                    scatter(S, l, n, n, b)

                def body(n, b, r, k):
                    pool.sem_inc(extra["o_free"], 1)
                    scatter(extra, l, r * PAIRS + n, k, b)

                def after(n, b):
                    pool.sem_inc(S["o_free"], 1)

                passes(pool, l, S, first, body, after)
            for b in range(2):
                pool.wait_ge(kv_stored[b], 64)

        @block.tensor
        def _(pe):
            count = {"ada": 0}

            def ada(n, to):
                wait_unit(pe, n)
                if count["ada"] >= SLOTS:
                    pe.wait_ge(ada_done, count["ada"])
                w = mem.unit(n)[:, 0:KC * 512].rearrange("p (k n) -> p k n", k=KC)
                out = bank[to]
                for k in range(KC):
                    for j in range(4):
                        last = pe.matmul(out[32 * j:32 * j + 32, 0:P], mem.silu[:, k, :],
                                         w[:, k, P * j:P * j + P], start=(k == 0), stop=(k == KC - 1))
                last.then_inc(ada_ps, 1)
                count["ada"] += 1

            def columns(l):
                for u in range(4):
                    last = pe.transpose(bank[3][:, P * u:P * u + P], mem.m[:, l, u, :], ident)
                last.then_inc(col_ps, 1)

            def t8(src):
                for k in range(KC):
                    for t in range(TILES):
                        last = pe.transpose(bank[k][:, P * t:P * t + P], src[:, t, P * k:P * k + P], ident)
                    last.then_inc(t8_ps, 1)

            def turn(t, banks):
                for c in range(KC):
                    last = pe.transpose(bank[banks[c // 4]][:, P * (c % 4):P * (c % 4) + P],
                                        mem.h[:, t, P * c:P * c + P], ident)
                    if c % 4 == 3:
                        last.then_inc(turn_ps, 1)

            def spread(l, vec, i, banks):
                for half in range(2):
                    for j in range(4):
                        last = pe.matmul(banks[half][:, P * j:P * j + P],
                                         mem.const("sel")[:, P * (2 * j + i):P * (2 * j + i) + P],
                                         mem.m[:, l, 2 * vec + half, :], start=True, stop=True)
                return last

            def project(l, srcT, half):
                n = AT["out", l, half]
                wait_unit(pe, n)
                w = mem.unit(n)[:, 0:KC * 512].rearrange("p (k n) -> p k n", k=KC)
                for t in range(TILES):
                    for k in range(KC):
                        last = pe.matmul(bank[3 * half + t], srcT[:, k, P * t:P * t + P], w[:, k, :],
                                         start=(k == 0), stop=(k == KC - 1))
                    last.then_inc(proj_ps, 1)

            pe.wait_ge(cond_in, 32)
            pe.wait_ge(rows_in, 16)
            pe.transpose(bank[0][:, 0:2 * KC], mem.cond[:, :], mem.const("ident")[0:2 * KC, 0:2 * KC]).then_inc(cond_ps, 1)
            pe.wait_ge(silu_done, 2)
            for u in range(4):
                ada(AT["ada", 0, u], 3 + u)
            pe.wait_ge(ada_done, 4)
            columns(0)
            pe.wait_ge(norm_ready, 3)
            pe.wait_ge(col_done, 1)
            t8(mem.h)

            def qkv_group(u, g):
                n = AT["qkv", 0, u]
                i = 6 * u + g
                t, half = (1, 2, 0)[g // 2], g % 2
                if g == 0:
                    wait_unit(pe, n)
                if i >= 2:
                    pe.wait_ge(qkv_sb, i - 1)
                w = mem.unit(n).rearrange("p (k n) -> p k n", k=KC)
                for k in range(KC):
                    last = pe.matmul(bank[i % 2][:, 0:384], mem.hT[:, k, P * t:P * t + P],
                                     w[:, k, 384 * half:384 * half + 384], start=(k == 0), stop=(k == KC - 1))
                last.then_inc(qkv_ps, 1)

            def head_transposes(head):
                w, hh = head // 2, head % 2
                buf = mem.qkv[w % 2]
                pe.wait_ge(rope_done, w + 1)
                pe.wait_ge(qkv_sb, 6 * w + 6)
                pe.wait_ge(ada_done, count["ada"])
                if head >= 1:
                    pe.wait_ge(qT_sb, head)
                    pe.wait_ge(kT_sb, head)
                for t in range(TILES):
                    pe.transpose(bank[3][:, P * t:P * t + P], buf[:, t, P * hh:P * hh + P], ident)
                for t in range(TILES):
                    pe.transpose(bank[4][:, P * t:P * t + P], buf[:, t, 256 + P * hh:256 + P * hh + P], ident)
                pe.transpose(bank[4][:, TOK:TOK + P], mem.ctxk[:, P * head:P * head + P], ident).then_inc(qkT_ps, 1)

            def scores(g):
                head, t = g // 3, g % 3
                pe.wait_ge(qT_sb, head + 1)
                pe.wait_ge(kT_sb, head + 1)
                if g >= 1:
                    pe.wait_ge(exp_done, 2 * g)
                lo, hi = (0, P) if t == 0 else (P, TOK + P)
                for j in range(2):
                    last = pe.matmul(bank[5 + j][:, 0:hi - lo], mem.qT[HD * j:HD * j + HD, P * t:P * t + P],
                                     mem.kT[HD * j:HD * j + HD, lo:hi], start=True, stop=True)
                last.then_inc(score_ps, 1)

            def pd_transposes(g):
                pe.wait_ge(pd_done, g + 1)
                if g >= 1:
                    pe.wait_ge(pdT_sb, g)
                for c in range(1 if g % 3 == 0 else 3):
                    last = pe.transpose(bank[7][:, P * c:P * c + P], mem.p[g % 2][0][:, P * c:P * c + P], ident)
                last.then_inc(pdT_ps, 1)

            def pv(g):
                head, t = g // 3, g % 3
                buf, vc = mem.qkv[(head // 2) % 2], 512 + P * (head % 2)
                pe.wait_ge(pdT_sb, g + 1)
                if g >= 1:
                    pe.wait_ge(o_raw, g)
                out = bank[2][:, 0:P]
                v = [buf[:, 0, vc:vc + P]] if t == 0 else [buf[:, 1, vc:vc + P], buf[:, 2, vc:vc + P],
                                                           mem.ctxv[:, P * head:P * head + P]]
                for c, rhs in enumerate(v):
                    last = pe.matmul(out, mem.pdT[g % 2][:, P * c:P * c + P], rhs, start=(c == 0),
                                     stop=(c == len(v) - 1))
                last.then_inc(pv_ps, 1)

            wait_t8(pe, T8_LN)
            pe.wait_ge(ctx_in, 32)
            for u in range(5):
                between = [AT["qkv", 0, u] + 1 + i for i in range(3)] if u < 4 else []
                for s in range(6):
                    g = 6 * (u - 1) + s
                    if u >= 1 and s % 3 == 0:
                        head_transposes(g // 3)
                    if u < 4:
                        qkv_group(u, s)
                    if u >= 1:
                        scores(g)
                    if g >= 1:
                        pd_transposes(g - 1)
                    if s % 2 == 1 and between:
                        ada(between[s // 2], 3)
                    if g >= 1:
                        pv(g - 1)
            pd_transposes(STEPS - 1)
            pv(STEPS - 1)
            pe.wait_ge(o_done, STEPS)
            pe.wait_ge(ada_done, 16)
            t8(mem.h)

            further[pe] = pe.alloc_register("further")
            pe.reg_mov(further[pe], 0)

            def gt(S, n):
                pe.wait_ge(S["sel"], n + 1)
                for c in range(KC):
                    for t in range(TILES):
                        last = pe.matmul(bank[2 + c // 4][:, P * (c % 4):P * (c % 4) + P],
                                         mem.h[:, t, P * c:P * c + P], mem.sel[:, t, :],
                                         start=(t == 0), stop=(t == TILES - 1))
                last.then_inc(S["gt_ps"], 1)

            def gate_up(S, n, b, slots, landings):
                pe.wait_ge(S["gt_act"], n + 1)
                pe.wait_ge(S["gt_dve"], n + 1)
                for done, value in landings:
                    pe.wait_ge(done, value)
                for c in range(KC):
                    for e in range(2):
                        w = mem.ring[:, slots[e], 0:4 * D].rearrange("p (g k n) -> p g k n", g=2, k=KC)[:, :, c, :]
                        last = pe.matmul(bank[b][64 * e:64 * e + 64, :].rearrange("p (g n) -> p g n", g=2),
                                         mem.GT[b][:, c, 64 * e:64 * e + 64], w,
                                         start=(c == 0), stop=(c == KC - 1))
                last.then_inc(S["u_ps"], 1)

            def act_transposes(S, n, b):
                pe.wait_ge(S["act"], n + 1)
                for f in range(2):
                    last = pe.transpose(bank[4][:, P * f:P * f + P],
                                        mem.act[b].rearrange("p (d f) -> p f d", f=2)[:, f, :], ident)
                last.then_inc(S["at_ps"], 1)

            def down(S, n, b, slots, landings):
                pe.wait_ge(S["at_sb"], n + 1)
                for done, value in landings:
                    pe.wait_ge(done, value)
                pe.wait_ge(S["o_act"], n + 1)
                pe.wait_ge(S["o_dve"], n + 1)
                for half in range(2):
                    for f in range(2):
                        for e in range(2):
                            w = mem.ring[:, slots[e], 4 * D:].rearrange("p (k n) -> p k n", k=2)
                            last = pe.matmul(bank[5 + half][64 * e:64 * e + 64, :],
                                             mem.actT[b][:, f, 64 * e:64 * e + 64],
                                             w[:, f, 512 * half:512 * half + 512], start=(f == 0), stop=(f == 1))
                last.then_inc(S["d_ps"], 1)

            def mlp(l):
                S, base = main[l], MOE_BASE[l]

                def first(n, b, it):
                    units = [base + 2 * b + e for e in range(2)]
                    slots = [x % SLOTS for x in units]
                    gate_up(S, n, b, slots, [(landed[x % SLOTS], 32 * it + LANDED[x]) for x in units])
                    gt(S, n + 1)
                    act_transposes(S, n, b)
                    down(S, n, b, slots, [(down_landed[i], 16 * (it + 1 + l * EXPERTS // SLOTS)) for i in slots])

                def body(n, b, r, k):
                    slots = [(base + 2 * b + e) % SLOTS for e in range(2)]
                    pe.wait_ge(S["gt_act"], n + 2)
                    pe.wait_ge(S["gt_dve"], n + 2)
                    gt(extra, k)
                    gate_up(extra, k, b, slots, [])
                    act_transposes(extra, k, b)
                    pe.wait_ge(S["o_act"], n + 2)
                    pe.wait_ge(S["o_dve"], n + 2)
                    down(extra, k, b, slots, [])

                gt(S, 0)
                passes(pe, l, S, first, body)
                pe.drain().then_inc(mlp_end, 1)

            def mixer_output(l, srcT):
                spread(l, 2, 0, (bank[6], bank[7])).then_inc(gate_ps, 1)
                project(l, srcT, 0)
                pe.wait_ge(gate_sb, 4 * l + 1)
                spread(l, 2, 1, (bank[6], bank[7])).then_inc(gate_ps, 1)
                project(l, srcT, 1)

            def expert_input(l):
                pe.wait_ge(proj_used, 6 * (l + 1))
                pe.wait_ge(gate_sb, 4 * l + 2)
                for i in range(2):
                    spread(l, 4, i, (bank[4 * i], bank[4 * i + 1]))
                    spread(l, 3, i, (bank[4 * i + 2], bank[4 * i + 3])).then_inc(rows_ps, 1)
                def router(t):
                    wait_turn(pe, TURN_ROUTE[l], t)
                    for k in range(KC):
                        last = pe.matmul(bank[0][:, NLOG * t:NLOG * t + NLOG], mem.hT[:, k, P * t:P * t + P],
                                         mem.wr[:, l, k, :], start=(k == 0), stop=(k == KC - 1))
                    return last

                pe.wait_ge(norm_ready, 6 * l + 4)
                turn(0, (0, 1))
                pe.wait_ge(norm_ready, 6 * l + 5)
                turn(1, (2, 3))
                pe.wait_ge(router_in, 64)
                router(0)
                pe.wait_ge(norm_ready, 6 * l + 6)
                turn(2, (4, 5))
                router(1)
                router(2).then_inc(logits_ps, 1)
                spread(l, 5, 0, (bank[6], bank[7])).then_inc(gate_ps, 1)
                spread(l, 5, 1, (bank[2], bank[3])).then_inc(gate_ps, 1)
                pe.wait_ge(msum_done, l + 1)
                for t in range(TILES):
                    for s in range(t + 1):
                        last = pe.matmul(bank[1][:, EXPERTS * t:EXPERTS * t + EXPERTS],
                                         mem.const("tri" if s == t else "ones"), mem.Msum[:, s, :],
                                         start=(s == 0), stop=(s == t))
                for s in range(TILES):
                    last = pe.matmul(bank[1][:, EXPERTS * TILES:EXPERTS * (TILES + 1)], mem.const("ones"),
                                     mem.Msum[:, s, :], start=(s == 0), stop=(s == TILES - 1))
                last.then_inc(pos_ps, 1)
                pe.wait_ge(gate_sb, 4 * l + 4)

            wait_t8(pe, T8_O)
            mixer_output(0, mem.hT)
            expert_input(0)
            mlp(0)

            columns(1)
            pe.wait_ge(col_done, 2)

            def turn_tile(t):
                pe.wait_ge(norm_ready, 7 + t)
                if t >= 1:
                    wait_turn(pe, TURN_LN, t - 1)
                turn(t, (5, 6))

            def over_channels(t):
                wait_turn(pe, TURN_LN, t)
                for gp in range(4):
                    n = 4 * t + gp
                    if n >= 4:
                        pe.wait_ge(chan_act if n % 2 == 0 else chan_dve, (n - 4) // 2 + 1)
                    for i in range(2):
                        last = pe.matmul(bank[(0, 1, 3, 4)[n % 4]][:, 256 * i:256 * i + 256],
                                         mem.hT[:, 2 * gp + i, P * t:P * t + P], mem.dft[:, 0:256],
                                         start=True, stop=True)
                    last.then_inc(chan_ps, 1)
                    if n < 8:
                        ada(AT["ada", 1, 4 + n], 7)

            turn_tile(0)
            turn_tile(1)
            pe.wait_ge(dft_in, 16)
            over_channels(0)
            turn_tile(2)
            over_channels(1)
            over_channels(2)
            pe.wait_ge(chan_act, 2 * TILES)
            pe.wait_ge(chan_dve, 2 * TILES)
            pos_p = mem.dft[:, 256:512].rearrange("p (s n) -> p s n", s=2)
            pos_l = mem.dft[:, 512:].rearrange("p (t s n) -> p t s n", t=2, s=2)
            for g in range(KC):
                out = bank[5 + g % 2]
                if g >= 2:
                    pe.wait_ge(four_act if g % 2 == 0 else four_dve, (g - 2) // 2 + 1)
                for s in range(2):
                    pe.matmul(out[:, 0:P], mem.U[:, 0, g, P * s:P * s + P], pos_p[:, s, :],
                              start=(s == 0), stop=(s == 1))
                for i, (t, s) in enumerate(((0, 0), (0, 1), (1, 0), (1, 1))):
                    last = pe.matmul(out[:, P:TOK], mem.U[:, 1 + t, g, P * s:P * s + P], pos_l[:, t, s, :],
                                     start=(i == 0), stop=(i == 3))
                last.then_inc(four_ps, 1)
            pe.wait_ge(four_act, KC // 2)
            pe.wait_ge(four_dve, KC // 2)
            pe.wait_ge(ada_done, 2 * ADA_UNITS)
            mixer_output(1, mem.fT)
            expert_input(1)
            mlp(1)

        @block.scalar
        def _(act):
            def t8_evict(use, l=None):
                for k in range(0, KC, 2):
                    act.wait_ge(t8_ps, KC * use + k + 1)
                    if l is None:
                        last = nc.scalar.copy(mem.hT[:, k, :], bank[k][:, 0:TOK])
                    else:
                        for i, (lo, hi) in enumerate(((0, P), (P, TOK))):
                            last = nc.scalar.activation(mem.hT[:, k, lo:hi], bank[k][:, lo:hi], ACT.Identity,
                                                        bias=mem.col[:, 0, k // 4, k % 4, i:i + 1],
                                                        scale=mem.col[:, 1, k // 4, k % 4, i:i + 1])
                    last.then_inc(t8_act, 1)

            def turn_evict(t, part):
                act.wait_ge(turn_ps, 2 * (TILES * TURN_LN + t) + part + 1)
                i = 0 if t == 0 else 1
                for j in range(4):
                    last = nc.scalar.activation(mem.hT[:, 4 * part + j, P * t:P * t + P],
                                                bank[5 + part][:, P * j:P * j + P], ACT.Identity,
                                                bias=mem.col[:, 0, part, j, i:i + 1], scale=mem.col[:, 1, part, j, i:i + 1])
                last.then_inc(turn_lo, 1)

            def gate_evict(n, i, banks):
                act.wait_ge(gate_ps, n)
                nc.scalar.copy(mem.gates[:, i, :], mem.psum[:, 512 * banks:512 * banks + D]).then_inc(gate_sb, 1)

            def load_norm(idx):
                if idx >= 1:
                    act.wait_ge(gb_used, idx)
                for i, name in enumerate(("ln_gain", "ln_bias")):
                    act.dma_start(mem.gb[:, i, :], A[name][idx // 2, idx % 2].partition_broadcast(P)).then_inc(gb_in, 16)

            for i, src in enumerate((A["c_ctx"].rearrange("(k p) -> k p", p=P),
                                     A["c"].rearrange("b (k p) -> (b k) p", p=P))):
                act.dma_start(mem.cond[KC * i:KC * i + KC, :], src).then_inc(cond_in, 16)
            act.wait_ge(zeroed, 2)
            for i in range(2):
                act.dma_start(mem.m[i:i + 97:32, :, :, :].rearrange("j l u n -> j (l u) n"),
                              A["b_ada"].rearrange("l (u j n) -> j (l u) n", u=ADA_UNITS, j=4)
                              ).then_inc(bias_in, 16)
            for n, name in enumerate(("lambda_q1", "lambda_k1", "lambda_q2", "lambda_k2")):
                act.dma_start(mem.lam[:, n, :], A[name][0].partition_broadcast(P)).then_inc(lam_in, 16)
            act.dma_start(mem.gain8[:, :], A["subln_gain"][0].partition_broadcast(P)).then_inc(lam_in, 16)
            act.wait_ge(cond_ps, 1)
            for i in range(2):
                nc.scalar.activation(mem.silu[:, :, i], bank[0][:, KC * i:KC * i + KC], ACT.Silu).then_inc(silu_done, 1)
            act.wait_ge(x_in, 16 * TILES)
            act.dma_start(mem.ctxk, A["cache_k"][0, 0].rearrange("s h d -> s (h d)")).then_inc(ctx_in, 16)
            act.dma_start(mem.ctxv, A["cache_v"][0, 0].rearrange("s h d -> s (h d)")).then_inc(ctx_in, 16)
            for l in range(2):
                act.dma_start(mem.wr[:, l, :, 0:GROUPS], A["w_router_group"][l].rearrange("(p k) n -> p k n", p=P)
                              ).then_inc(router_in, 16)
                act.dma_start(mem.wr[:, l, :, GROUPS:], A["w_router_expert"][l].rearrange("(p k) n -> p k n", p=P)
                              ).then_inc(router_in, 16)
            act.wait_ge(col_done, 1)
            t8_evict(T8_LN, 0)
            act.wait_ge(lam_prod, 2)
            nc.scalar.activation(mem.lams[:, 2:4], mem.lams[:, 0:2], ACT.Exp).then_inc(lam_done, 1)

            for u in range(5):
                for s in range(6):
                    g = 6 * (u - 1) + s
                    if u >= 1 and s % 3 == 0:
                        act.wait_ge(qkT_ps, g // 3 + 1)
                        nc.scalar.copy(mem.qT, bank[3][:, 0:TOK]).then_inc(qT_sb, 1)
                    if u >= 1:
                        w = P if g % 3 == 0 else TOK
                        act.wait_ge(nb_done, g + 1)
                        for j in range(2):
                            nc.scalar.activation(mem.p[g % 2][j][:, 0:w], bank[5 + j][:, 0:w], ACT.Exp,
                                                 bias=mem.nb[:, g % 2, j:j + 1], scale=SCALE,
                                                 accum_out=mem.ssum[:, g % 2, j:j + 1]).then_inc(exp_done, 1)
                    if u < 4:
                        i = 6 * u + s
                        t, half = (1, 2, 0)[s // 2], s % 2
                        act.wait_ge(qkv_ps, i + 1)
                        if s == 0 and u >= 2:
                            act.wait_ge(pv_ps, 6 * (u - 1))
                            act.wait_ge(kv_stored[u % 2], 32)
                        nc.scalar.copy(mem.qkv[u % 2][:, t, 384 * half:384 * half + 384],
                                       bank[i % 2][:, 0:384]).then_inc(qkv_sb, 1)
            t8_evict(T8_O)

            def gt_evict(S, n, b):
                act.wait_ge(S["gt_ps"], n + 1)
                nc.scalar.copy(mem.GT[b][:, 0:4, :], bank[2].rearrange("p (c s) -> p c s", c=4)
                               ).then_inc(S["gt_act"], 1)

            def silu(S, n, b):
                act.wait_ge(S["u_ps"], n + 1)
                nc.scalar.activation(mem.sil[b], bank[b][:, 0:FE], ACT.Silu).then_inc(S["sil"], 1)

            def o_evict(S, n, b):
                act.wait_ge(S["d_ps"], n + 1)
                act.wait_ge(S["o_free"], n + 1)
                nc.scalar.copy(mem.O[b][:, 0:512], bank[5]).then_inc(S["o_act"], 1)

            further[act] = act.alloc_register("further")
            act.reg_mov(further[act], 0)
            act.sem_inc(extra["o_act"], 1)

            def expert_input(l):
                for t in range(TILES):
                    for part, done in enumerate((turn_lo, turn_hi)):
                        act.wait_ge(turn_ps, 2 * (TILES * TURN_ROUTE[l] + t) + part + 1)
                        nc.scalar.copy(mem.hT[:, 4 * part:4 * part + 4, P * t:P * t + P],
                                       bank[2 * t + part].rearrange("p (c s) -> p c s", c=4)).then_inc(done, 1)
                act.wait_ge(route_in, 2 * l + 1)
                nc.scalar.activation(mem.r12[1], mem.r12[0], ACT.Exp).then_inc(route_out, 1)
                act.wait_ge(route_in, 2 * l + 2)
                nc.scalar.activation(mem.r3[:, 6], mem.r3[:, 5], ACT.Exp).then_inc(route_out, 1)
                for i in range(2):
                    gate_evict(4 * l + 3 + i, i, (6, 2)[i])
                load_norm(2 * l + 1)
                act.wait_ge(ids_out, 96 * (l + 1))
                act.dma_start(mem.table[:, 0:PASSES * PAIRS].rearrange("p (r n) -> p r n", r=PASSES),
                              t_dram[l].rearrange("(r p n) o -> p r (n o)", r=PASSES, p=P)).then_inc(table_in, 16)

            def mlp(l):
                S = main[l]
                act.sem_inc(S["o_act"], 1)

                def first(n, b, it):
                    silu(S, n, b)
                    gt_evict(S, n + 1, 1 - b)
                    o_evict(S, n, b)

                def body(n, b, r, k):
                    gt_evict(extra, k, b)
                    silu(extra, k, b)
                    o_evict(extra, k, b)

                gt_evict(S, 0, 0)
                passes(act, l, S, first, body)
                act.wait_ge(S["gt_dve"], PAIRS + 1)
                act.wait_ge(S["o_free"], PAIRS + 2)
                for t in range(TILES):
                    act.dma_start(mem.Y[:, t, :, :], y_dram[l].rearrange("(k t p) n -> t p k n", k=2, p=P)[t]
                                  ).then_inc(y_in[t], 16)
                if l == 0:
                    act.dma_start(mem.dft, A["k_dft"]).then_inc(dft_in, 16)
                for t in range(TILES):
                    act.wait_ge(y_in[t], 16 * (l + 1))
                    nc.scalar.activation(mem.Y[:, t, 0, :], mem.Y[:, t, 0, :], ACT.Copy,
                                         scale=mem.w[:, 0, t:t + 1]).then_inc(y_scaled, 1)

            load_norm(0)
            gate_evict(1, 0, 6)
            gate_evict(2, 1, 6)
            expert_input(0)
            mlp(0)
            act.wait_ge(col_done, 2)
            turn_evict(0, 0)
            turn_evict(1, 0)
            for n in range(0, 4 * TILES, 2):
                t, gp = n // 4, n % 4
                if n == 4:
                    turn_evict(2, 0)
                act.wait_ge(chan_ps, n + 1)
                nc.scalar.copy(mem.U[:, t, 2 * gp:2 * gp + 2, :],
                               bank[(0, 1, 3, 4)[n % 4]].rearrange("p (g n) -> p g n", g=2)).then_inc(chan_act, 1)
            for g in range(0, KC, 2):
                act.wait_ge(four_ps, g + 1)
                nc.scalar.copy(mem.fT[:, g, :], bank[5 + g % 2][:, 0:TOK]).then_inc(four_act, 1)
            load_norm(2)
            gate_evict(5, 0, 6)
            gate_evict(6, 1, 6)
            expert_input(1)
            mlp(1)
            for t in range(TILES):
                act.wait_ge(x_done, t + 1)
                dst = A["y_prompt"][0] if t == 0 else A["y_sample"][0][(t - 1) * P:t * P, :]
                act.dma_start(dst, mem.x[:, t, :]).then_inc(out_done, 16)
            act.wait_ge(out_done, 16 * TILES)

        @block.vector
        def _(dve):
            V = nc.vector
            chain = [0]
            ada_count = [0]

            def mark(ins):
                chain[0] += 1
                ins.then_inc(dve_chain, 1)
                return chain[0]

            def link(ins):
                dve.wait_ge(dve_chain, mark(ins))

            def inverse_sqrt(y):
                v, t = mem.rs_v[:, :], mem.rs_t[:, :]
                link(V.tensor_scalar(t.bitcast(I32), v.bitcast(I32), 1, None, ALU.logical_shift_right))
                link(V.tensor_scalar(y.bitcast(I32), t.bitcast(I32), -1.0, float(0x5F3759DF), ALU.mult, ALU.add))
                for _ in range(3):
                    link(V.tensor_tensor(t, y, y, ALU.mult))
                    link(V.scalar_tensor_tensor(out=t, in0=t, scalar=-0.5, in1=v, op0=ALU.mult, op1=ALU.mult))
                    link(V.scalar_tensor_tensor(out=y, in0=t, scalar=1.5, in1=y, op0=ALU.add, op1=ALU.mult))

            def tile_stats(t):
                for i in range(2):
                    last = V.bn_stats(mem.stats[:, t, i, :], mem.x[:, t, 512 * i:512 * i + 512])
                return last

            def finish_stats(last):
                link(last)
                for t in range(TILES):
                    last = V.bn_aggr(mem.mv[:, t, :], mem.stats[:, t, :, :].rearrange("p i n -> p (i n)"))
                link(last)
                link(V.tensor_scalar(mem.rs_v[:, :], mem.mv[:, :, 1], EPS, None, ALU.add))
                inverse_sqrt(mem.rstd[:, :])

            def normalised():
                for t in range(TILES):
                    V.tensor_scalar(mem.h[:, t, :], mem.x[:, t, :], mem.mv[:, t, 0:1], mem.rstd[:, t:t + 1],
                                    ALU.subtract, ALU.mult).then_inc(norm_ready, 1)

            def ada_add(n):
                l, u = UNITS[n][1:]
                src = bank[7 if l == 1 and u >= 4 else 3 + u if l == 0 and u < 4 else 3][:, 0:P]
                ada_count[0] += 1
                dve.wait_ge(ada_ps, ada_count[0])
                V.scalar_tensor_tensor(out=mem.m[:, l, u, :], in0=mem.m[:, l, u, :],
                                       scalar=1.0 if u // 2 in (1, 4) else 0.0, in1=src,
                                       op0=ALU.add, op1=ALU.add).then_inc(ada_done, 1)

            def columns(l):
                dve.wait_ge(col_ps, l + 1)
                V.tensor_copy(mem.col[:, :, :, :, :].rearrange("p s u j i -> p (s u j) i"),
                              bank[3].rearrange("p (c r) -> p c r", r=32)[:, :, 0:2]).then_inc(col_done, 1)

            def t8_evict(use, l=None):
                for k in range(1, KC, 2):
                    dve.wait_ge(t8_ps, KC * use + k + 1)
                    if l is None:
                        last = V.tensor_copy(mem.hT[:, k, :], bank[k][:, 0:TOK])
                    else:
                        for i, (lo, hi) in enumerate(((0, P), (P, TOK))):
                            last = V.tensor_scalar(mem.hT[:, k, lo:hi], bank[k][:, lo:hi],
                                                   mem.col[:, 1, k // 4, k % 4, i:i + 1],
                                                   mem.col[:, 0, k // 4, k % 4, i:i + 1], ALU.mult, ALU.add)
                    last.then_inc(t8_dve, 1)

            dve.wait_ge(x_in, 48)
            for t in range(TILES):
                last = tile_stats(t)
            finish_stats(last)
            normalised()
            dve.wait_ge(bias_in, 16 * 2)
            for u in range(4):
                ada_add(AT["ada", 0, u])
            columns(0)
            dve.wait_ge(col_done, 1)
            t8_evict(T8_LN, 0)

            dve.wait_ge(lam_in, 16 * 5)
            for i in range(2):
                V.tensor_tensor_reduce(out=mem.lamtmp, in0=mem.lam[:, 2 * i, :], in1=mem.lam[:, 2 * i + 1, :],
                                       scale=1.0, scalar=0.0, op0=ALU.mult, op1=ALU.add,
                                       accum_out=mem.lams[:, i:i + 1]).then_inc(lam_prod, 1)
                dve.wait_ge(lam_prod, i + 1)
            link(V.tensor_scalar(mem.gain8[:, :], mem.gain8[:, :], 1.0 - LAM_INIT, None, ALU.mult))
            dve.wait_ge(lam_done, 1)
            link(V.tensor_tensor(mem.lams[:, 4:5], mem.lams[:, 3:4], mem.lams[:, 2:3], ALU.subtract))
            link(V.tensor_scalar(mem.lams[:, 5:6], mem.lams[:, 4:5], -LAM_INIT, None, ALU.add))
            neg_lam = mem.lams[:, 5:6]

            def maximum(g):
                w = P if g % 3 == 0 else TOK
                dve.wait_ge(score_ps, g + 1)
                for j in range(2):
                    last = V.reduce_max(mem.mx[:, g % 2, j:j + 1], bank[5 + j][:, 0:w], AX)
                link(last)
                V.tensor_scalar(mem.nb[:, g % 2, :], mem.mx[:, g % 2, :], -SCALE, None, ALU.mult).then_inc(nb_done, 1)

            def difference(g):
                w = P if g % 3 == 0 else TOK
                dve.wait_ge(exp_done, 2 * g + 2)
                link(V.reciprocal(mem.rsum[:, g % 2, :], mem.ssum[:, g % 2, :]))
                link(V.scalar_tensor_tensor(out=mem.ratio[:, g % 2:g % 2 + 1], in0=mem.rsum[:, g % 2, 1:2],
                                            scalar=mem.ssum[:, g % 2, 0:1], in1=neg_lam, op0=ALU.mult, op1=ALU.mult))
                p0, p1 = mem.p[g % 2]
                V.scalar_tensor_tensor(out=p0[:, 0:w], in0=p1[:, 0:w], scalar=mem.ratio[:, g % 2:g % 2 + 1],
                                       in1=p0[:, 0:w], op0=ALU.mult, op1=ALU.add).then_inc(pd_done, 1)

            def pdT_evict(g):
                w = P if g % 3 == 0 else TOK
                dve.wait_ge(pdT_ps, g + 1)
                V.tensor_copy(mem.pdT[g % 2][:, 0:w], bank[7][:, 0:w]).then_inc(pdT_sb, 1)

            def head_norm(g):
                head, t = g // 3, g % 3
                o = mem.h[:, t, P * head:P * head + P]
                dve.wait_ge(pv_ps, g + 1)
                V.tensor_scalar(o, bank[2][:, 0:P], mem.rsum[:, g % 2, 0:1], None, ALU.mult
                                ).then_inc(o_raw, 1)
                dve.wait_ge(o_raw, g + 1)
                link(V.tensor_tensor_reduce(out=mem.sq[:, :], in0=o, in1=o, scale=1.0 / P, scalar=0.0,
                                            op0=ALU.mult, op1=ALU.add, accum_out=mem.ss[:, t:t + 1]))
                if t == TILES - 1:
                    link(V.tensor_scalar(mem.rs_v[:, :], mem.ss[:, :], EPS, None, ALU.add))
                    inverse_sqrt(mem.rs_y[:, :])
                    for i in range(TILES):
                        oi = mem.h[:, i, P * head:P * head + P]
                        V.scalar_tensor_tensor(out=oi, in0=oi, scalar=mem.rs_y[:, i:i + 1], in1=mem.gain8[:, :],
                                               op0=ALU.mult, op1=ALU.mult).then_inc(o_done, 1)

            for u in range(5):
                between = [AT["qkv", 0, u] + 1 + i for i in range(3)] if u < 4 else []
                for s in range(6):
                    g = 6 * (u - 1) + s
                    if u >= 1:
                        if s % 3 == 0:
                            dve.wait_ge(qkT_ps, g // 3 + 1)
                            V.tensor_copy(mem.kT, bank[4]).then_inc(kT_sb, 1)
                        maximum(g)
                    if g >= 1:
                        pdT_evict(g - 1)
                    if u >= 1:
                        difference(g)
                    if s % 2 == 1 and between:
                        ada_add(between[s // 2])
                    if g >= 1:
                        head_norm(g - 1)
            pdT_evict(STEPS - 1)
            head_norm(STEPS - 1)
            t8_evict(T8_O)

            def post_norm(idx, last):
                finish_stats(last)
                dve.wait_ge(gb_in, 32 * (idx + 1))
                scaled, out = [None] * TILES, [None] * TILES

                def scale(t):
                    scaled[t] = mark(V.scalar_tensor_tensor(out=mem.x[:, t, :], in0=mem.x[:, t, :],
                                                            scalar=mem.mv[:, t, 0:1], in1=mem.gb[:, 0, :],
                                                            op0=ALU.subtract, op1=ALU.mult))

                def shift(t):
                    dve.wait_ge(dve_chain, scaled[t])
                    ins = V.scalar_tensor_tensor(out=mem.x[:, t, :], in0=mem.x[:, t, :],
                                                 scalar=mem.rstd[:, t:t + 1], in1=mem.gb[:, 1, :],
                                                 op0=ALU.mult, op1=ALU.add)
                    if idx == 3:
                        ins.then_inc(x_done, 1)
                    elif t == TILES - 1:
                        ins.then_inc(gb_used, 1)
                    else:
                        out[t] = mark(ins)

                scale(0)
                scale(1)
                shift(0)
                scale(2)
                shift(1)
                if idx == 3:
                    shift(2)
                    return None
                dve.wait_ge(dve_chain, out[0])
                tile_stats(0)
                shift(2)
                dve.wait_ge(dve_chain, out[1])
                tile_stats(1)
                dve.wait_ge(gb_used, idx + 1)
                return tile_stats(2)

            def mixer_output(l):
                for half in range(2):
                    for t in range(TILES):
                        i = 0 if t == 0 else 1
                        part = slice(512 * half, 512 * half + 512)
                        dve.wait_ge(gate_sb, 4 * l + 1 + i)
                        dve.wait_ge(proj_ps, 6 * l + 3 * half + t + 1)
                        V.tensor_tensor(mem.tmp[:, t, part], bank[3 * half + t], mem.gates[:, i, part], ALU.mult
                                        ).then_inc(proj_used, 1)
                        dve.wait_ge(proj_used, 6 * l + 3 * half + t + 1)
                        link(V.scalar_tensor_tensor(out=mem.x[:, t, part], in0=mem.x[:, t, part], scalar=ALPHA,
                                                    in1=mem.tmp[:, t, part], op0=ALU.mult, op1=ALU.add))
                        last = V.bn_stats(mem.stats[:, t, half, :], mem.x[:, t, part])
                return post_norm(2 * l, last)

            def first_true(dst, tmp, eq, n, top):
                shape = [P, TILES, n]
                w = mem.const("descend")[:, 8 - n:8].unsqueeze(1)
                link(V.tensor_tensor(tmp, eq, bc(w, shape), ALU.mult))
                link(V.tensor_reduce(top, tmp, AX, ALU.max))
                link(V.tensor_tensor(dst, tmp, bc(top.unsqueeze(2), shape), ALU.is_equal))

            def select(S, n, place):
                for t in range(TILES):
                    last = V.tensor_scalar(mem.sel[:, t, :], mem.const("rowcode"), place[:, t:t + 1], None, ALU.is_equal)
                last.then_inc(S["sel_first"], 1)
                dve.wait_ge(S["sel_first"], n + 1)
                for t in range(TILES):
                    last = V.scalar_tensor_tensor(out=mem.sel[:, t, :], in0=mem.const("rowcode"),
                                                  scalar=place[:, TILES + t:TILES + t + 1], in1=mem.sel[:, t, :],
                                                  op0=ALU.is_equal, op1=ALU.add)
                last.then_inc(S["sel"], 1)

            def route(l):
                r3, r12, r24 = mem.r3, mem.r12, mem.r24
                s4, s8, s32 = [P, TILES, GROUPS], [P, TILES, PER_GROUP], [P, TILES, GROUPS, PER_GROUP]
                dve.wait_ge(logits_ps, l + 1)
                link(V.tensor_copy(mem.L.rearrange("p t n -> p (t n)"), bank[0][:, 0:TILES * NLOG]))
                lg = mem.L[:, :, 0:GROUPS]
                le = mem.L[:, :, GROUPS:].rearrange("p t (g e) -> p t g e", g=GROUPS)
                link(V.tensor_reduce(r3[:, 0], lg, AX, ALU.max))
                V.tensor_tensor(r12[0], lg, bc(r3[:, 0].unsqueeze(2), s4), ALU.subtract).then_inc(route_in, 1)
                link(V.tensor_tensor(r12[2], lg, bc(r3[:, 0].unsqueeze(2), s4), ALU.is_equal))
                first_true(r12[2], r12[3], r12[2], GROUPS, r3[:, 1])
                group = r12[2]
                link(V.tensor_tensor(mem.r96, le, bc(group.unsqueeze(3), s32), ALU.mult))
                link(V.tensor_reduce(r24[0], mem.r96.rearrange("p t g e -> p t e g"), AX, ALU.add))
                link(V.tensor_reduce(r3[:, 2], r24[0], AX, ALU.max))
                link(V.tensor_tensor(r24[1], r24[0], bc(r3[:, 2].unsqueeze(2), s8), ALU.is_equal))
                first_true(r24[2], r24[3], r24[1], PER_GROUP, r3[:, 3])
                link(V.scalar_tensor_tensor(out=r24[4], in0=r24[2], scalar=-3.0e38, in1=r24[0],
                                            op0=ALU.mult, op1=ALU.add))
                link(V.tensor_reduce(r3[:, 4], r24[4], AX, ALU.max))
                V.tensor_tensor(r3[:, 5], r3[:, 4], r3[:, 2], ALU.subtract).then_inc(route_in, 1)
                link(V.tensor_tensor(r24[5], r24[4], bc(r3[:, 4].unsqueeze(2), s8), ALU.is_equal))
                first_true(r24[6], r24[7], r24[5], PER_GROUP, r3[:, 7])
                for k, one in enumerate((r24[2], r24[6])):
                    for g in range(GROUPS):
                        last = V.tensor_tensor(mem.M[k][:, :, PER_GROUP * g:PER_GROUP * g + PER_GROUP], one,
                                               bc(group[:, :, g:g + 1], s8), ALU.mult)
                link(last)
                V.tensor_tensor(mem.Msum, mem.M[0], mem.M[1], ALU.add).then_inc(msum_done, 1)
                dve.wait_ge(route_out, 2 * l + 2)
                link(V.tensor_reduce(r3[:, 8], r12[1], AX, ALU.add))
                link(V.tensor_scalar(r3[:, 9], r3[:, 6], 1.0, None, ALU.add))
                link(V.tensor_tensor(r3[:, 10], r3[:, 8], r3[:, 9], ALU.mult))
                link(V.reciprocal(mem.w[:, 0, :], r3[:, 10]))
                link(V.tensor_tensor(mem.w[:, 1, :], mem.w[:, 0, :], r3[:, 6], ALU.mult))
                dve.wait_ge(pos_ps, l + 1)
                pos = bank[1][:, 0:TILES * EXPERTS]
                base = bc(mem.const("slotbase").unsqueeze(1), [P, TILES, EXPERTS])
                for i, what in enumerate((pos.rearrange("p (t e) -> p t e", t=TILES), base)):
                    for k in range(2):
                        last = V.tensor_tensor(mem.Mt[:, TILES * k:TILES * k + TILES, :], mem.M[k], what, ALU.mult)
                    link(last)
                    link(V.tensor_reduce(mem.r6[:, i], mem.Mt, AX, ALU.add))
                link(V.tensor_tensor(mem.r30, bc(mem.r6[:, 0].unsqueeze(2), [P, 6, PASSES - 1]),
                                     bc(mem.const("thresholds").unsqueeze(1), [P, 6, PASSES - 1]), ALU.is_ge))
                link(V.tensor_reduce(mem.r6[:, 2], mem.r30, AX, ALU.add))
                link(V.scalar_tensor_tensor(out=mem.r6[:, 3], in0=mem.r6[:, 0], scalar=float(PAIRS), in1=mem.r6[:, 1],
                                            op0=ALU.mult, op1=ALU.add))
                link(V.scalar_tensor_tensor(out=mem.r6[:, 4], in0=mem.r6[:, 2], scalar=float(PAIRS * CAP),
                                            in1=mem.r6[:, 3], op0=ALU.mult, op1=ALU.add))
                V.tensor_copy(mem.slot[:, :], mem.r6[:, 4]).then_inc(slot_done, 1)
                link(V.tensor_copy(mem.place[:, :], mem.r6[:, 4]))
                select(main[l], 0, mem.place)
                counts = bank[1][:, TILES * EXPERTS:(TILES + 1) * EXPERTS].rearrange("p (n e) -> p n e", e=2)
                link(V.tensor_reduce(mem.pairmax, counts, AX, ALU.max))
                s80 = [P, PAIRS, PASSES - 1]
                link(V.tensor_tensor(mem.r80, bc(mem.pairmax.unsqueeze(2), s80), bc(mem.const("thresholds").unsqueeze(1), s80),
                                     ALU.is_gt))
                link(V.tensor_reduce(mem.further, mem.r80, AX, ALU.add))
                link(V.tensor_tensor(mem.further, mem.further, mem.const("octal"), ALU.mult))
                link(V.tensor_reduce(mem.words_f[:, :], mem.further.rearrange("p (h n) -> p h n", h=2), AX, ALU.add))
                V.tensor_copy(mem.words[:, :], mem.words_f[:, :]).then_inc(words_done, 1)

            def expert_input(l, last):
                finish_stats(last)
                scaled = [None] * TILES

                def scale(t):
                    i = 0 if t == 0 else 1
                    dve.wait_ge(rows_ps, 2 * l + 1 + i)
                    scaled[t] = mark(V.scalar_tensor_tensor(
                        out=mem.tmp[:, t, :], in0=mem.x[:, t, :], scalar=mem.mv[:, t, 0:1],
                        in1=mem.psum[:, 2048 * i:2048 * i + D], op0=ALU.subtract, op1=ALU.mult))

                def shift(t):
                    i = 0 if t == 0 else 1
                    dve.wait_ge(dve_chain, scaled[t])
                    V.scalar_tensor_tensor(
                        out=mem.h[:, t, :].rearrange("p (c k) -> p k c", c=KC),
                        in0=mem.tmp[:, t, :].rearrange("p (k c) -> p k c", c=KC), scalar=mem.rstd[:, t:t + 1],
                        in1=mem.psum[:, 2048 * i + D:2048 * i + 2 * D].rearrange("p (k c) -> p k c", c=KC),
                        op0=ALU.mult, op1=ALU.add).then_inc(norm_ready, 1)

                scale(0)
                scale(1)
                shift(0)
                scale(2)
                shift(1)
                shift(2)
                route(l)

            def gt_evict(S, n, b):
                dve.wait_ge(S["gt_ps"], n + 1)
                V.tensor_copy(mem.GT[b][:, 4:8, :], bank[3].rearrange("p (c s) -> p c s", c=4)
                              ).then_inc(S["gt_dve"], 1)

            def up_times(S, n, b):
                dve.wait_ge(S["sil"], n + 1)
                V.tensor_tensor(mem.act[b], mem.sil[b], bank[b][:, FE:2 * FE], ALU.mult).then_inc(S["act"], 1)

            def at_evict(S, n, b):
                dve.wait_ge(S["at_ps"], n + 1)
                V.tensor_copy(mem.actT[b], bank[4][:, 0:2 * P].rearrange("p (f s) -> p f s", f=2)
                              ).then_inc(S["at_sb"], 1)

            def o_evict(S, n, b):
                dve.wait_ge(S["d_ps"], n + 1)
                dve.wait_ge(S["o_free"], n + 1)
                V.tensor_copy(mem.O[b][:, 512:D], bank[6]).then_inc(S["o_dve"], 1)

            further[dve] = dve.alloc_register("further")
            dve.reg_mov(further[dve], 0)
            dve.sem_inc(extra["o_dve"], 1)
            dve.sem_inc(gate_up_through, 1)
            dve.sem_inc(down_through, 1)

            def mlp(l):
                S = main[l]
                dve.sem_inc(S["o_dve"], 1)

                def first(n, b, it):
                    V.tensor_copy(mem.place_x[:, :], mem.place[:, :])
                    V.tensor_scalar(mem.place[:, :], mem.place[:, :], -1.0, None, ALU.add).then_inc(S["place"], 1)
                    dve.wait_ge(S["place"], n + 1)
                    select(S, n + 1, mem.place)
                    up_times(S, n, b)
                    gt_evict(S, n + 1, 1 - b)
                    at_evict(S, n, b)
                    o_evict(S, n, b)

                def body(n, b, r, k):
                    V.tensor_scalar(mem.place_x[:, :], mem.place_x[:, :], -float(PAIRS * P), None, ALU.add
                                    ).then_inc(extra["place"], 1)
                    dve.wait_ge(extra["place"], k + 1)
                    select(extra, k, mem.place_x)
                    gt_evict(extra, k, b)
                    up_times(extra, k, b)
                    dve.sem_inc(gate_up_through, 1)
                    at_evict(extra, k, b)
                    o_evict(extra, k, b)
                    dve.sem_inc(down_through, 1)

                gt_evict(S, 0, 0)
                passes(dve, l, S, first, body)

            def combine(l):
                y = mem.Y
                summed, gated, out = ([None] * TILES for _ in range(3))

                def add_second(t):
                    dve.wait_ge(y_scaled, TILES * l + t + 1)
                    summed[t] = mark(V.scalar_tensor_tensor(out=y[:, t, 0, :], in0=y[:, t, 1, :],
                                                            scalar=mem.w[:, 1, t:t + 1], in1=y[:, t, 0, :],
                                                            op0=ALU.mult, op1=ALU.add))

                def gate(t):
                    dve.wait_ge(dve_chain, summed[t])
                    gated[t] = mark(V.tensor_tensor(y[:, t, 0, :], y[:, t, 0, :],
                                                    mem.gates[:, 0 if t == 0 else 1, :], ALU.mult))

                def onto(t):
                    dve.wait_ge(dve_chain, gated[t])
                    out[t] = mark(V.scalar_tensor_tensor(out=mem.x[:, t, :], in0=mem.x[:, t, :], scalar=ALPHA,
                                                         in1=y[:, t, 0, :], op0=ALU.mult, op1=ALU.add))

                def sums(t):
                    dve.wait_ge(dve_chain, out[t])
                    return tile_stats(t)

                add_second(0)
                gate(0)
                add_second(1)
                onto(0)
                gate(1)
                sums(0)
                add_second(2)
                onto(1)
                gate(2)
                sums(1)
                onto(2)
                return post_norm(2 * l + 1, sums(2))

            def turn_evict(t, part):
                dve.wait_ge(turn_ps, 2 * (TILES * TURN_LN + t) + part + 1)
                i = 0 if t == 0 else 1
                for j in range(4):
                    last = V.tensor_scalar(mem.hT[:, 4 * part + j, P * t:P * t + P], bank[5 + part][:, P * j:P * j + P],
                                           mem.col[:, 1, part, j, i:i + 1], mem.col[:, 0, part, j, i:i + 1],
                                           ALU.mult, ALU.add)
                last.then_inc(turn_hi, 1)

            for b in range(2):
                dve.wait_ge(kv_stored[b], 64)
            expert_input(0, mixer_output(0))
            mlp(0)
            columns(1)
            finish_stats(combine(0))
            normalised()
            dve.wait_ge(col_done, 2)
            turn_evict(0, 1)
            turn_evict(1, 1)
            for n in range(1, 4 * TILES, 2):
                t, gp = n // 4, n % 4
                if n == 5:
                    turn_evict(2, 1)
                dve.wait_ge(chan_ps, n + 1)
                V.tensor_copy(mem.U[:, t, 2 * gp:2 * gp + 2, :],
                              bank[(0, 1, 3, 4)[n % 4]].rearrange("p (g n) -> p g n", g=2)).then_inc(chan_dve, 1)
                for i in range(n - 1, n + 1):
                    if i < 8:
                        ada_add(AT["ada", 1, 4 + i])
            for g in range(1, KC, 2):
                dve.wait_ge(four_ps, g + 1)
                V.tensor_copy(mem.fT[:, g, :], bank[5 + g % 2][:, 0:TOK]).then_inc(four_dve, 1)
            expert_input(1, mixer_output(1))
            mlp(1)
            combine(1)


_INS = ["x_prompt", "x_sample", "cache_k", "cache_v", "c", "c_ctx", "w_ada", "b_ada", "ln_gain", "ln_bias", "w_qkv",
        "w_attn_out", "lambda_q1", "lambda_k1", "lambda_q2", "lambda_k2", "subln_gain", "w_fourier_out",
        "w_router_group", "w_router_expert", "w_expert_gate", "w_expert_up", "w_expert_down"]
_OUTS = [("y_prompt", (1, P, D)), ("y_sample", (1, 2 * P, D)), ("new_cache_k", (1, 1, P, HEADS, 2 * HD)),
         ("new_cache_v", (1, 1, P, HEADS, 2 * HD))]


def kernel(**inputs):
    import concourse.bacc as bacc
    from concourse.bass_utils import run_bass_kernel_spmd

    nc = bacc.Bacc("TRN2", target_bir_lowering=False, num_devices=1)
    arrays = {name: np.ascontiguousarray(inputs[name]) for name in _INS}
    arrays.update(constants())
    aps = {name: nc.dram_tensor(f"in_{name}", a.shape, mybir.dt.from_np(a.dtype), kind="ExternalInput").ap()
           for name, a in arrays.items()}
    for name, shape in _OUTS:
        aps[name] = nc.dram_tensor(f"out_{name}", shape, F32, kind="ExternalOutput").ap()
    build(nc, aps)
    r = run_bass_kernel_spmd(nc, [{f"in_{name}": a for name, a in arrays.items()}], core_ids=[0])
    return tuple(r.results[0][f"out_{name}"] for name, _ in _OUTS)
```

```python
import math
from contextlib import ExitStack

import numpy as np

import concourse.bass as bass
from concourse import mybir

F32 = mybir.dt.float32
I32 = mybir.dt.int32
U32 = mybir.dt.uint32
ALU = mybir.AluOpType
ACT = mybir.ActivationFunctionType
AX = mybir.AxisListType.X

P = 128
D = 1024
KC = D // P
TILES = 3
TOK = TILES * P
HEADS = 8
HD = 64
NMOD = 6
GROUPS, PER_GROUP = 4, 8
EXPERTS = GROUPS * PER_GROUP
FE = 256
CAP = 64
PAIRS = EXPERTS // 2
PASSES = TOK // CAP
NLOG = GROUPS + EXPERTS
SLOTS = 4
SLOT = 6 * D
EPS = 1e-5
ALPHA = (2.0 * 2) ** 0.25
LAM_INIT = 0.8 - 0.6 * math.exp(0.0)
SCALE = HD ** -0.5
INVALID = 4096
ADA_UNITS = NMOD * D // 512
QK_W = 768
STEPS = 3 * HEADS

UNITS = [("ada", 0, u) for u in range(4)]
_rest = [("ada", 0, u) for u in range(4, ADA_UNITS)] + [("ada", 1, u) for u in range(ADA_UNITS - 4)]
BETWEEN = [_rest[0:2], _rest[2:4], _rest[4:6], _rest[6:9], _rest[9:14], _rest[14:16]]
SPOTS = {2: (1, 4), 3: (1, 3, 5), 5: (1, 2, 3, 4, 5)}
for _u in range(4):
    UNITS += [("qkv", 0, _u)] + BETWEEN[_u]
UNITS += BETWEEN[4] + BETWEEN[5] + [("out", 0, 0), ("out", 0, 1)]
MOE_BASE = [len(UNITS)]
UNITS += [("expert", 0, e) for e in range(EXPERTS)]
UNITS += [("ada", 1, 8), ("ada", 1, 9), ("out", 1, 0), ("out", 1, 1), ("ada", 1, 10), ("ada", 1, 11)]
MOE_BASE.append(len(UNITS))
UNITS += [("expert", 1, e) for e in range(EXPERTS)]
AT = {unit: n for n, unit in enumerate(UNITS)}
DMAS = {"ada": 1, "qkv": 3, "out": 1, "expert": 2}
LANDED = []
_sum = [0] * SLOTS
for _n, (_kind, _, _) in enumerate(UNITS):
    _sum[_n % SLOTS] += 16 * DMAS[_kind]
    LANDED.append(_sum[_n % SLOTS])

_C = {}
_at = 0
for _name, _w in (("ident", P), ("tri", P), ("ones", P), ("cos", 2 * HD), ("sin", 2 * HD),
                  ("slotbase", EXPERTS), ("thresholds", PASSES - 1), ("descend", 8), ("octal", PAIRS), ("rowcode", P), ("sel", 8 * P)):
    _C[_name] = (_at, _at + _w)
    _at += _w
NCONST = _at
NDFT = 2 * P + 2 * P + 4 * 2 * P


def constants():
    c = np.zeros((P, NCONST), np.float64)

    def put(name, a):
        c[:, _C[name][0]:_C[name][1]] = np.asarray(a).reshape(np.asarray(a).shape[0], -1)

    put("ident", np.eye(P))
    put("tri", np.triu(np.ones((P, P)), 1))
    put("ones", np.ones((P, P)))
    sel = np.zeros((P, 4, 2, P))
    for j in range(4):
        for i in range(2):
            sel[32 * j + i, j, i, :] = 1.0
    put("sel", sel)
    nf = HD // 4
    inv = np.float32(10000.0) ** (-np.arange(nf, dtype=np.float32) / nf)
    tok = np.arange(2 * P)
    pos = np.stack([tok // 64, tok % 64], 1).astype(np.float32)
    ang = (pos[:, :, None] * inv.astype(np.float32)).astype(np.float32)
    cos, sin = np.cos(ang.astype(np.float64)), np.sin(ang.astype(np.float64))
    full_c = np.concatenate([cos, cos], -1).reshape(2, P, HD).transpose(1, 0, 2)
    full_s = np.concatenate([-sin, sin], -1).reshape(2, P, HD).transpose(1, 0, 2)
    put("cos", full_c)
    put("sin", full_s)
    e = np.arange(EXPERTS)
    put("slotbase", np.tile((e % 2) * (CAP * PAIRS) + e // 2, (P, 1)))
    put("thresholds", np.tile(CAP * np.arange(1, PASSES), (P, 1)))
    put("octal", np.tile(8.0 ** (np.arange(PAIRS) % 8), (P, 1)))
    put("rowcode", np.tile(PAIRS * np.arange(P), (P, 1)))
    put("descend", np.tile(8 - np.arange(8), (P, 1)))

    def dft(n, scale):
        a = 2 * np.pi * (np.outer(np.arange(n), np.arange(n)) % n) / n
        return np.cos(a) * scale, np.sin(a) * scale

    cc, sc = dft(P, 1.0)
    cp, sp = dft(P, 1.0 / P)
    cl, sl = dft(2 * P, (2 * P * P) ** -0.5)
    lat = np.stack([cl, -sl], 1).reshape(2, P, 2, 2 * P).transpose(1, 0, 2, 3)
    table = np.concatenate([cc, sc, cp, -sp, lat.reshape(P, -1)], 1)
    ids = np.arange(P)[:, None, None] + P * np.arange(TILES)[None, None, :] + TOK * np.arange(2)[None, :, None]
    empty = np.full((P, PASSES * PAIRS), INVALID)
    ints = np.concatenate([ids.reshape(P, -1), empty], 1)
    return {"k_rows": c.astype(np.float32), "k_dft": table.astype(np.float32), "k_ints": ints.astype(np.int32)}


class Memory:

    def __init__(self, nc, ctx):
        def sb(name, shape, dt=F32):
            return ctx.enter_context(nc.sbuf_tensor(name, shape, dt))

        self.ring = sb("ring", [P, SLOTS, SLOT])
        self.x = sb("x", [P, TILES, D])
        self.h = sb("h", [P, TILES, D])
        self.hT = sb("hT", [P, KC, TOK])
        self.m = sb("m", [P, 2, ADA_UNITS, P])
        self.rows = sb("k_rows_sb", [P, NCONST])
        self.ints = sb("k_ints_sb", [P, 6 + PASSES * PAIRS], I32)
        self.wr = sb("wr", [P, 2, KC, NLOG])
        self.cond = sb("cond", [2 * KC, P])
        self.silu = sb("silu", [P, KC, 32])
        self.col = sb("col", [P, 2, 2, 4, 2])
        self.lams = sb("lams", [P, 8])
        self.gain8 = sb("gain8", [P, P])
        self.stats = sb("stats", [P, TILES, 2, 6])
        self.mv = sb("mv", [P, TILES, 2])
        self.rstd = sb("rstd", [P, TILES])
        self.mx = sb("mx", [P, 2, 2])
        self.nb = sb("nb", [P, 2, 2])
        self.ssum = sb("ssum", [P, 2, 2])
        self.rsum = sb("rsum", [P, 2, 2])
        self.ratio = sb("ratio", [P, 2])
        self.sq = sb("sq", [P, P])
        self.ss = sb("ss", [P, TILES])
        self.rs_v = sb("rs_v", [P, TILES])
        self.rs_t = sb("rs_t", [P, TILES])
        self.rs_y = sb("rs_y", [P, TILES])
        self.w = sb("w", [P, 2, TILES])
        self.slot = sb("slot", [P, 6], I32)
        self.words_f = sb("words_f", [P, 2])
        self.words = sb("words", [P, 2], I32)
        self.table = sb("table", [P, 8 * PAIRS], I32)
        self.place = sb("place", [P, 6])
        self.place_x = sb("place_x", [P, 6])
        self.sidx = sb("sidx", [P, 2], I32)
        K = 256
        self.arena = a = sb("arena", [P, 50 * K])

        def view(at, size):
            return a[:, int(at * K):int(at * K) + size]

        self.qkv = [view(9 * b, TILES * QK_W).rearrange("p (t n) -> p t n", t=TILES) for b in range(2)]
        self.qT = view(18, TOK)
        self.kT = view(19.5, TOK + P)
        self.rope_a = view(21.5, 512)
        self.rope_b = view(23.5, 512)
        self.ctxk = view(25.5, D)
        self.ctxv = view(29.5, D)
        self.p = [[view(33.5 + 3 * b + 1.5 * j, TOK) for j in range(2)] for b in range(2)]
        self.pdT = [view(39.5 + 1.5 * b, TOK) for b in range(2)]
        self.lam = view(33.5, 4 * HD).rearrange("p (n d) -> p n d", n=4)
        self.lamtmp = view(34.5, HD)
        at = [16 * K]

        def small(*shape):
            n = int(np.prod(shape))
            v = a[:, at[0]:at[0] + n]
            at[0] += n
            names = "abc"[:len(shape)]
            return v.rearrange(f"p ({' '.join(names)}) -> p {' '.join(names)}",
                               **dict(zip(names[1:], shape[1:]))) if len(shape) > 1 else v

        self.L = small(TILES, NLOG)
        self.r3 = small(16, TILES)
        self.r12 = [small(TILES, GROUPS) for _ in range(4)]
        self.r24 = [small(TILES, PER_GROUP) for _ in range(8)]
        self.r96 = small(TILES, GROUPS, PER_GROUP)
        self.M = [small(TILES, EXPERTS) for _ in range(2)]
        self.Msum = small(TILES, EXPERTS)
        self.Mt = small(2 * TILES, EXPERTS)
        self.r6 = small(5, 6)
        self.r30 = small(6, PASSES - 1)
        self.pairmax = small(PAIRS)
        self.r80 = small(PAIRS, PASSES - 1)
        self.further = small(PAIRS)
        self.tmp = view(0, TILES * D).rearrange("p (t n) -> p t n", t=TILES)
        self.U = view(0, TILES * KC * 2 * P).rearrange("p (t g n) -> p t g n", t=TILES, g=KC)
        self.dft = view(24, NDFT)
        self.gates = view(30, 2 * D).rearrange("p (i n) -> p i n", i=2)
        self.gb = view(38, 2 * D).rearrange("p (i n) -> p i n", i=2)
        self.sel = view(0, TOK).rearrange("p (t s) -> p t s", t=TILES)
        self.GT = [view(8 + 4 * b, D).rearrange("p (c s) -> p c s", c=KC) for b in range(2)]
        self.sil = [view(16 + b, FE) for b in range(2)]
        self.act = [view(18 + b, FE) for b in range(2)]
        self.actT = [view(20 + b, 2 * P).rearrange("p (f s) -> p f s", f=2) for b in range(2)]
        self.O = [view(22 + 4 * b, D) for b in range(2)]
        self.Y = view(0, TILES * 2 * D).rearrange("p (t k n) -> p t k n", t=TILES, k=2)
        self.psum = ctx.enter_context(nc.psum_tensor("psum", [P, 8 * 512], F32))
        self.bank = [self.psum[:, 512 * b:512 * b + 512] for b in range(8)]

    def const(self, name):
        return self.rows[:, _C[name][0]:_C[name][1]]

    def unit(self, n):
        return self.ring[:, n % SLOTS, :]


def bc(ap, shape):
    return ap.to_broadcast(shape)


def build(nc, A):
    ctx = ExitStack()
    with ctx:
        mem = Memory(nc, ctx)
        bank = mem.bank
        ident = mem.const("ident")

        sems = {}

        def sem(name):
            if name not in sems:
                sems[name] = ctx.enter_context(nc.semaphore(name))
            return sems[name]

        y_dram = [nc.dram_tensor(f"y_scratch{l}", (2 * TOK, D), F32).ap() for l in range(2)]
        t_dram = [nc.dram_tensor(f"table_scratch{l}", (PASSES * PAIRS * P, 1), I32).ap() for l in range(2)]

        cond_in, rows_in, router_in, x_in, lam_in, ctx_in, ints_in = (
            sem(n) for n in ("cond_in", "rows_in", "router_in", "x_in", "lam_in", "ctx_in", "ints_in"))
        bias_in, zeroed, table_clear = sem("bias_in"), sem("zeroed"), sem("table_clear")
        landed = [sem(f"slot_landed{i}") for i in range(SLOTS)]
        down_landed = [sem(f"down_landed{i}") for i in range(SLOTS)]
        cond_ps, silu_done = sem("cond_ps"), sem("silu_done")
        ada_ps, ada_done = sem("ada_ps"), sem("ada_done")
        col_ps, col_done = sem("col_ps"), sem("col_done")
        norm_ready = sem("norm_ready")
        head_ps, head_sb = sem("head_ps"), sem("head_sb")
        qkv_ps, qkv_sb, rope_done = sem("qkv_ps"), sem("qkv_sb"), sem("rope_done")
        kv_stored = [sem(f"kv_stored{b}") for b in range(2)]
        qkT_ps, qT_sb, kT_sb = sem("qkT_ps"), sem("qT_sb"), sem("kT_sb")
        score_ps, nb_done, exp_done = sem("score_ps"), sem("nb_done"), sem("exp_done")
        pd_done, pdT_ps, pdT_sb, pv_ps, o_done = (sem(n) for n in ("pd_done", "pdT_ps", "pdT_sb", "pv_ps", "o_done"))
        lam_done, o_raw = sem("lam_done"), sem("o_raw")
        gate_ps, gate_sb = sem("gate_ps"), sem("gate_sb")
        proj_ps, proj_used = sem("proj_ps"), sem("proj_used")
        gb_in, gb_used = sem("gb_in"), sem("gb_used")
        rows_ps = sem("rows_ps")
        turn_ps, turn_lo, turn_hi = sem("turn_ps"), sem("turn_lo"), sem("turn_hi")
        y_scaled, count_ps, selectors_in = sem("y_scaled"), sem("count_ps"), sem("selectors_in")
        logits_ps, route_in, route_out, pos_ps, msum_done = (
            sem(n) for n in ("logits_ps", "route_in", "route_out", "pos_ps", "msum_done"))
        slot_done, ids_out, table_in, words_done, mlp_end = (
            sem(n) for n in ("slot_done", "ids_out", "table_in", "words_done", "mlp_end"))
        dft_in, chan_ps, chan_act, chan_dve = sem("dft_in"), sem("chan_ps"), sem("chan_act"), sem("chan_dve")
        four_ps, four_sb = sem("four_ps"), sem("four_sb")
        y_in = [sem(f"y_in{t}") for t in range(TILES)]
        x_done, out_done, lam_prod = sem("x_done"), sem("out_done"), sem("lam_prod")
        turns = sem("turns")
        gate_up_through, down_through = sem("gate_up_through"), sem("down_through")
        dve_chain, act_chain, pool_chain = sem("dve_chain"), sem("act_chain"), sem("pool_chain")

        def moe_sems(tag):
            names = ("place", "sel_first", "sel", "ahead_first", "ahead", "sidx", "gt_ps", "gt_act", "gt_dve", "u_ps", "sil", "act", "at_ps", "at_sb", "d_ps",
                     "o_act", "o_dve", "scattered", "o_free")
            return {n: sem(f"{n}_{tag}") for n in names}

        main = [moe_sems(f"main{l}") for l in range(2)]
        extra = moe_sems("extra")

        def passes(eng, l, S, first, body, start=None):
            eng.wait_ge(words_done, l + 1)
            with eng.Fori(0, 2) as half:
                word = eng.value_load(mem.words[0:1, bass.ds(half, 1)], min_val=0, max_val=(1 << 24) - 1)
                with eng.Fori(0, PAIRS // 4) as it:
                    for b in range(2):
                        n = half * (PAIRS // 2) + it * 2 + b
                        first(n, b, half * (PAIRS // 4) + it)
                        times = eng.snap((word >> (it * 6 + 3 * b)) & 7, min_val=0, max_val=PASSES - 1)
                        with eng.If(times > 0):
                            with eng.Fori(0, times) as r:
                                body(n, b, r + 1, eng.snap(further[eng]))
                                eng.reg_add(further[eng], further[eng], 1)
                        if start is not None:
                            start(n, b)

        further = {}
        block = ctx.enter_context(nc.Block())

        TURN_ROUTE, TURN_LN = [1, 3], [0, 2]
        FIRST_TILES = (1, 2, 0)
        TURN_BANKS = [((0, 1), (2, 5), (6, 7)), ((5, 6), (5, 6), (3, 4))]
        CHAN_BANKS = (0, 1, 3, 4) + (5, 6, 3, 4) * 2

        def wait_unit(eng, n):
            eng.wait_ge(landed[n % SLOTS], LANDED[n])

        ADA_ORDER = [n for n, unit in enumerate(UNITS) if unit[0] == "ada"]

        def ada_bank(n):
            l, u = UNITS[n][1:]
            if (l, u) < (0, 4):
                return 3 + u % 2
            if (l, u) >= (1, 8):
                return (2, 7)[u % 2]
            return 4 if UNITS[n] == BETWEEN[5][1] else 3

        def wait_used(eng, n):
            kind, l, u = UNITS[n]
            if kind == "ada":
                eng.wait_ge(ada_ps, ADA_ORDER.index(n) + 1)
            elif kind == "qkv":
                eng.wait_ge(qkv_ps, 6 * u + 6)
            elif kind == "out":
                eng.wait_ge(proj_ps, 6 * l + 5 + u)
            else:
                eng.wait_ge(mlp_end, l + 1)
                for t in range(TILES):
                    eng.wait_ge(y_in[t], 16 * (l + 1))

        def wait_turn(eng, use, t):
            eng.wait_ge(turn_lo, TILES * use + t + 1)
            eng.wait_ge(turn_hi, TILES * use + t + 1)

        @block.sync
        def _(sp):
            early = _C["sel"][0]
            sp.dma_start(mem.rows[:, 0:early], A["k_rows"][:, 0:early]).then_inc(rows_in, 16)

            def load_gate_up(slot, l, e):
                for part, name in enumerate(("w_expert_gate", "w_expert_up")):
                    sp.dma_start(mem.ring[:, slot, part * 2 * D:(part + 1) * 2 * D],
                                 A[name][l][bass.ds(e, 1)].rearrange("o (p k) n -> p (o k n)", p=P)
                                 ).then_inc(landed[slot], 16)

            def load_down(slot, l, e):
                sp.dma_start(mem.ring[:, slot, 4 * D:], A["w_expert_down"][l][bass.ds(e, 1)].rearrange(
                    "o (p k) n -> p (o k n)", p=P)).then_inc(down_landed[slot], 16)

            def load(n):
                kind, l, u = UNITS[n]
                if n >= SLOTS:
                    wait_used(sp, n - SLOTS)
                dst, done = mem.unit(n), landed[n % SLOTS]
                if kind == "ada":
                    sp.dma_start(dst[:, 0:KC * 512].rearrange("p (k n) -> p k n", k=KC),
                                 A["w_ada"][l].rearrange("(k p) n -> p k n", p=P)[:, :, 512 * u:512 * u + 512]
                                 ).then_inc(done, 16)
                elif kind == "qkv":
                    w = A["w_qkv"][0].rearrange("(k p) n -> p k n", p=P)
                    for part in range(3):
                        sp.dma_start(dst.rearrange("p (k n) -> p k n", k=KC)[:, :, 256 * part:256 * part + 256],
                                     w[:, :, D * part + 256 * u:D * part + 256 * u + 256]).then_inc(done, 16)
                elif kind == "out":
                    w = A["w_attn_out"][0] if l == 0 else A["w_fourier_out"][0]
                    sp.dma_start(dst[:, 0:KC * 512].rearrange("p (k n) -> p k n", k=KC),
                                 w.rearrange("(k p) n -> p k n", p=P)[:, :, 512 * u:512 * u + 512]
                                 ).then_inc(done, 16)
                else:
                    load_gate_up(n % SLOTS, l, u)
                    load_down(n % SLOTS, l, u)

            further[sp] = sp.alloc_register("further")
            sp.reg_mov(further[sp], 1)
            load(0)
            for t in range(TILES):
                src = A["x_prompt"][0] if t == 0 else A["x_sample"][0][(t - 1) * P:t * P, :]
                sp.dma_start(mem.x[:, t, :], src).then_inc(x_in, 16)
            for n in range(1, MOE_BASE[0]):
                load(n)
                if n == AT["qkv", 0, 0]:
                    sp.dma_start(mem.rows[:, early:], A["k_rows"][:, early:]).then_inc(selectors_in, 16)
            for l in range(2):
                base = MOE_BASE[l]
                for n in range(base, base + SLOTS):
                    load(n)
                sp.wait_ge(words_done, l + 1)
                for half in range(2):
                    word = sp.value_load(mem.words[0:1, half:half + 1], min_val=0, max_val=(1 << 24) - 1)
                    with sp.Fori(0, PAIRS // 4 - half) as it:
                        for b in range(2):
                            n = half * (PAIRS // 2) + it * 2 + b
                            times = sp.snap((word >> (it * 6 + 3 * b)) & 7, min_val=0, max_val=PASSES - 1)
                            first_done = sp.snap(n + 1)
                            sp.reg_add(further[sp], further[sp], times)
                            all_done = sp.snap(further[sp])
                            slots = [(base + 2 * b + e) % SLOTS for e in range(2)]
                            experts = [sp.snap(2 * n + 4 + e) for e in range(2)]
                            sp.wait_ge(main[l]["u_ps"], first_done)
                            sp.wait_ge(gate_up_through, all_done)
                            for e in range(2):
                                load_gate_up(slots[e], l, experts[e])
                            sp.wait_ge(main[l]["d_ps"], first_done)
                            sp.wait_ge(down_through, all_done)
                            for e in range(2):
                                load_down(slots[e], l, experts[e])
                if l == 0:
                    for n in range(base + EXPERTS, MOE_BASE[1]):
                        load(n)

        @block.gpsimd
        def _(pool):
            chain = [0]

            def link(ins):
                chain[0] += 1
                ins.then_inc(pool_chain, 1)
                pool.wait_ge(pool_chain, chain[0])

            pool.memset(mem.silu[:, :, :], 0.0).then_inc(zeroed, 1)
            pool.memset(mem.m[:, :, :, :], 0.0).then_inc(zeroed, 1)
            pool.dma_start(mem.ints[:, :], A["k_ints"]).then_inc(ints_in, 16)
            for l in range(2):
                pool.dma_start(t_dram[l].rearrange("(p n) o -> p (n o)", p=P), A["k_ints"][:, 6:]).then_inc(table_clear, 16)
            pool.wait_ge(rows_in, 16)

            cos = mem.const("cos").rearrange("p (t n) -> p t n", t=2)
            sin = mem.const("sin").rearrange("p (t n) -> p t n", t=2)
            for u in range(4):
                buf = mem.qkv[u % 2]
                for t in (1, 2):
                    pool.wait_ge(qkv_sb, 6 * u + 2 * t)
                    x8 = buf[:, t, 0:512].rearrange("p (g n) -> p g n", n=HD)
                    x4 = buf[:, t, 0:512].rearrange("p (g s n) -> p g s n", s=2, n=16)
                    b4 = mem.rope_b.rearrange("p (g s n) -> p g s n", s=2, n=16)
                    sg = sin[:, t - 1, :].rearrange("p (a s n) -> p a s n", a=2, s=2)
                    pool.tensor_tensor(mem.rope_a.rearrange("p (g n) -> p g n", n=HD), x8,
                                       bc(cos[:, t - 1, :].unsqueeze(1), [P, 8, HD]), ALU.mult)
                    for s in range(2):
                        last = pool.tensor_tensor(
                            b4[:, :, s, :].rearrange("p (g a) n -> p g a n", a=2),
                            x4[:, :, 1 - s, :].rearrange("p (g a) n -> p g a n", a=2),
                            bc(sg[:, :, s, :].unsqueeze(1), [P, 8, 2, 16]), ALU.mult)
                    link(last)
                    link(pool.tensor_tensor(buf[:, t, 0:512], mem.rope_a, mem.rope_b, ALU.add))
                pool.sem_inc(rope_done, 1)
                pool.wait_ge(qkv_sb, 6 * u + 6)
                pool.dma_start(A["new_cache_k"][0, 0].rearrange("s h d -> s (h d)")[:, 256 * u:256 * u + 256],
                               buf[:, 0, 256:512]).then_inc(kv_stored[u % 2], 16)
                pool.dma_start(A["new_cache_v"][0, 0].rearrange("s h d -> s (h d)")[:, 256 * u:256 * u + 256],
                               buf[:, 0, 512:768]).then_inc(kv_stored[u % 2], 16)

            def value(x):
                return x if isinstance(x, int) else pool.snap(x)

            further[pool] = pool.alloc_register("further")
            pool.reg_mov(further[pool], 0)
            out_bound = pool.snap(pool.to_reg(2 * TOK - 1))
            table_bound = pool.snap(pool.to_reg(PASSES * PAIRS * P - 1))

            def scatter(S, l, col, n, b):
                pool.tensor_copy(mem.sidx[:, b:b + 1], mem.table[:, bass.ds(col, 1)]).then_inc(S["sidx"], 1)
                n1, n2, n16 = value(n + 1), value(n + 2), value(16 * n + 16)
                pool.wait_ge(S["sidx"], n1)
                pool.wait_ge(S["o_act"], n2)
                pool.wait_ge(S["o_dve"], n2)
                pool.sem_inc(turns, 1)
                pool.indirect_dma_start(y_dram[l],
                                        bass.IndirectOffsetOnAxis(ap=mem.sidx[:, b:b + 1].bitcast(U32), axis=0),
                                        mem.O[b], None, bounds_check=out_bound, oob_is_err=False
                                        ).then_inc(S["scattered"], 16)
                pool.wait_ge(S["scattered"], n16)

            for l in range(2):
                S = main[l]
                pool.wait_ge(ints_in, 16)
                pool.wait_ge(table_clear, 32)
                pool.wait_ge(slot_done, l + 1)
                for c in range(6):
                    pool.indirect_dma_start(t_dram[l],
                                            bass.IndirectOffsetOnAxis(ap=mem.slot[:, c:c + 1].bitcast(U32), axis=0),
                                            mem.ints[:, c:c + 1], None, bounds_check=table_bound,
                                            oob_is_err=False).then_inc(ids_out, 16)
                pool.wait_ge(table_in, 16 * (l + 1))
                pool.sem_inc(S["o_free"], 2)

                def first(n, b, it):
                    scatter(S, l, n, n, b)

                def body(n, b, r, k):
                    pool.sem_inc(extra["o_free"], 1)
                    scatter(extra, l, r * PAIRS + n, k, b)

                def after(n, b):
                    pool.sem_inc(S["o_free"], 1)

                passes(pool, l, S, first, body, after)
            for b in range(2):
                pool.wait_ge(kv_stored[b], 64)

        @block.tensor
        def _(pe):
            count = {"ada": 0}

            def ada(n):
                wait_unit(pe, n)
                if count["ada"] >= 2:
                    pe.wait_ge(ada_done, count["ada"] - (1 if count["ada"] < 4 or ada_bank(n) != 3 else 0))
                w = mem.unit(n)[:, 0:KC * 512].rearrange("p (k n) -> p k n", k=KC)
                out = bank[ada_bank(n)]
                for k in range(KC):
                    for j in range(4):
                        last = pe.matmul(out[32 * j:32 * j + 32, 0:P], mem.silu[:, k, :],
                                         w[:, k, P * j:P * j + P], start=(k == 0), stop=(k == KC - 1))
                last.then_inc(ada_ps, 1)
                count["ada"] += 1

            def columns(l):
                for u in range(4):
                    last = pe.transpose(bank[3][:, P * u:P * u + P], mem.m[:, l, u, :], ident)
                last.then_inc(col_ps, 1)

            def turn_head(k):
                pe.wait_ge(o_done, TILES * (k + 1))
                if k >= 2:
                    pe.wait_ge(head_sb, k - 1)
                for t in range(TILES):
                    last = pe.transpose(bank[k % 2][:, P * t:P * t + P], mem.h[:, t, P * k:P * k + P], ident)
                last.then_inc(head_ps, 1)

            def turn(t, banks):
                for c in range(KC):
                    last = pe.transpose(bank[banks[c // 4]][:, P * (c % 4):P * (c % 4) + P],
                                        mem.h[:, t, P * c:P * c + P], ident)
                    if c % 4 == 3:
                        last.then_inc(turn_ps, 1)

            def spread(l, vec, i, banks):
                for half in range(2):
                    for j in range(4):
                        last = pe.matmul(banks[half][:, P * j:P * j + P],
                                         mem.const("sel")[:, P * (2 * j + i):P * (2 * j + i) + P],
                                         mem.m[:, l, 2 * vec + half, :], start=True, stop=True)
                return last

            def project(l, t, banks, halves=(0, 1)):
                for half in halves:
                    n = AT["out", l, half]
                    wait_unit(pe, n)
                    w = mem.unit(n)[:, 0:KC * 512].rearrange("p (k n) -> p k n", k=KC)
                    for k in range(KC):
                        last = pe.matmul(bank[banks[half]], mem.hT[:, k, P * t:P * t + P], w[:, k, :],
                                         start=(k == 0), stop=(k == KC - 1))
                    last.then_inc(proj_ps, 1)

            pe.wait_ge(cond_in, 32)
            pe.wait_ge(rows_in, 16)
            pe.transpose(bank[0][:, 0:2 * KC], mem.cond[:, :], mem.const("ident")[0:2 * KC, 0:2 * KC]).then_inc(cond_ps, 1)
            pe.wait_ge(silu_done, 2)
            for u in range(2):
                ada(AT["ada", 0, u])
            for j, t in enumerate(FIRST_TILES):
                pe.wait_ge(norm_ready, t + 1)
                turn(t, TURN_BANKS[0][j])
            for u in range(2, 4):
                ada(AT["ada", 0, u])
            pe.wait_ge(ada_done, 4)
            columns(0)

            def qkv_group(u, g):
                n = AT["qkv", 0, u]
                i = 6 * u + g
                t, half = FIRST_TILES[g // 2], g % 2
                if g == 0:
                    wait_unit(pe, n)
                if u == 0:
                    wait_turn(pe, TURN_LN[0], g // 2)
                if i >= 2:
                    pe.wait_ge(qkv_sb, i - 1)
                w = mem.unit(n).rearrange("p (k n) -> p k n", k=KC)
                for k in range(KC):
                    last = pe.matmul(bank[i % 2][:, 0:384], mem.hT[:, k, P * t:P * t + P],
                                     w[:, k, 384 * half:384 * half + 384], start=(k == 0), stop=(k == KC - 1))
                last.then_inc(qkv_ps, 1)

            def head_transposes(head):
                w, hh = head // 2, head % 2
                buf = mem.qkv[w % 2]
                pe.wait_ge(rope_done, w + 1)
                pe.wait_ge(qkv_sb, 6 * w + 6)
                pe.wait_ge(ada_done, count["ada"])
                if head >= 1:
                    pe.wait_ge(qT_sb, head)
                    pe.wait_ge(kT_sb, head)
                for t in range(TILES):
                    pe.transpose(bank[3][:, P * t:P * t + P], buf[:, t, P * hh:P * hh + P], ident)
                for t in range(TILES):
                    pe.transpose(bank[4][:, P * t:P * t + P], buf[:, t, 256 + P * hh:256 + P * hh + P], ident)
                pe.transpose(bank[4][:, TOK:TOK + P], mem.ctxk[:, P * head:P * head + P], ident).then_inc(qkT_ps, 1)

            def scores(g):
                head, t = g // 3, g % 3
                pe.wait_ge(qT_sb, head + 1)
                pe.wait_ge(kT_sb, head + 1)
                if g >= 1:
                    pe.wait_ge(exp_done, 2 * g)
                lo, hi = (0, P) if t == 0 else (P, TOK + P)
                for j in range(2):
                    last = pe.matmul(bank[5 + j][:, 0:hi - lo], mem.qT[HD * j:HD * j + HD, P * t:P * t + P],
                                     mem.kT[HD * j:HD * j + HD, lo:hi], start=True, stop=True)
                last.then_inc(score_ps, 1)

            def pd_transposes(g):
                pe.wait_ge(pd_done, g + 1)
                if g >= 1:
                    pe.wait_ge(pdT_sb, g)
                for c in range(1 if g % 3 == 0 else 3):
                    last = pe.transpose(bank[7][:, P * c:P * c + P], mem.p[g % 2][0][:, P * c:P * c + P], ident)
                last.then_inc(pdT_ps, 1)

            def pv(g):
                head, t = g // 3, g % 3
                buf, vc = mem.qkv[(head // 2) % 2], 512 + P * (head % 2)
                pe.wait_ge(pdT_sb, g + 1)
                if g >= 1:
                    pe.wait_ge(o_raw, g)
                out = bank[2][:, 0:P]
                v = [buf[:, 0, vc:vc + P]] if t == 0 else [buf[:, 1, vc:vc + P], buf[:, 2, vc:vc + P],
                                                           mem.ctxv[:, P * head:P * head + P]]
                for c, rhs in enumerate(v):
                    last = pe.matmul(out, mem.pdT[g % 2][:, P * c:P * c + P], rhs, start=(c == 0),
                                     stop=(c == len(v) - 1))
                last.then_inc(pv_ps, 1)

            for u in range(5):
                between = [AT[unit] for unit in BETWEEN[u]]
                if u == 1:
                    pe.wait_ge(ctx_in, 32)
                for s in range(6):
                    g = 6 * (u - 1) + s
                    if u >= 1 and s % 3 == 0:
                        head_transposes(g // 3)
                        if g >= 1:
                            pd_transposes(g - 1)
                    if u >= 1:
                        scores(g)
                        if s % 3 != 0:
                            pd_transposes(g - 1)
                    if u < 4:
                        qkv_group(u, s)
                    if s in SPOTS[len(between)]:
                        ada(between[SPOTS[len(between)].index(s)])
                    if g >= 1:
                        pv(g - 1)
                    if u == 4:
                        turn_head(s)
            pd_transposes(STEPS - 1)
            pv(STEPS - 1)
            for unit in BETWEEN[5]:
                ada(AT[unit])
            turn_head(6)
            turn_head(7)
            pe.wait_ge(ada_done, 20)

            further[pe] = pe.alloc_register("further")
            pe.reg_mov(further[pe], 0)

            def gt(S, n):
                pe.wait_ge(S["sel"], n + 1)
                for c in range(KC):
                    for t in range(TILES):
                        last = pe.matmul(bank[2 + c // 4][:, P * (c % 4):P * (c % 4) + P],
                                         mem.h[:, t, P * c:P * c + P], mem.sel[:, t, :],
                                         start=(t == 0), stop=(t == TILES - 1))
                last.then_inc(S["gt_ps"], 1)

            def gate_up(S, n, b, slots, landings):
                pe.wait_ge(S["gt_act"], n + 1)
                pe.wait_ge(S["gt_dve"], n + 1)
                for done, value in landings:
                    pe.wait_ge(done, value)
                for c in range(KC):
                    for e in range(2):
                        w = mem.ring[:, slots[e], 0:4 * D].rearrange("p (g k n) -> p g k n", g=2, k=KC)[:, :, c, :]
                        last = pe.matmul(bank[b][64 * e:64 * e + 64, :].rearrange("p (g n) -> p g n", g=2),
                                         mem.GT[b][:, c, 64 * e:64 * e + 64], w,
                                         start=(c == 0), stop=(c == KC - 1))
                last.then_inc(S["u_ps"], 1)

            def act_transposes(S, n, b):
                pe.wait_ge(S["act"], n + 1)
                for f in range(2):
                    last = pe.transpose(bank[4][:, P * f:P * f + P],
                                        mem.act[b].rearrange("p (d f) -> p f d", f=2)[:, f, :], ident)
                last.then_inc(S["at_ps"], 1)

            def down(S, n, b, slots, landings):
                pe.wait_ge(S["at_sb"], n + 1)
                for done, value in landings:
                    pe.wait_ge(done, value)
                pe.wait_ge(S["o_act"], n + 1)
                pe.wait_ge(S["o_dve"], n + 1)
                for half in range(2):
                    for f in range(2):
                        for e in range(2):
                            w = mem.ring[:, slots[e], 4 * D:].rearrange("p (k n) -> p k n", k=2)
                            last = pe.matmul(bank[5 + half][64 * e:64 * e + 64, :],
                                             mem.actT[b][:, f, 64 * e:64 * e + 64],
                                             w[:, f, 512 * half:512 * half + 512], start=(f == 0), stop=(f == 1))
                last.then_inc(S["d_ps"], 1)

            def mlp(l):
                S, base = main[l], MOE_BASE[l]

                def first(n, b, it):
                    units = [base + 2 * b + e for e in range(2)]
                    slots = [x % SLOTS for x in units]
                    gate_up(S, n, b, slots, [(landed[x % SLOTS], 32 * it + LANDED[x]) for x in units])
                    gt(S, n + 1)
                    act_transposes(S, n, b)
                    down(S, n, b, slots, [(down_landed[i], 16 * (it + 1 + l * EXPERTS // SLOTS)) for i in slots])

                def body(n, b, r, k):
                    slots = [(base + 2 * b + e) % SLOTS for e in range(2)]
                    pe.wait_ge(S["gt_act"], n + 2)
                    pe.wait_ge(S["gt_dve"], n + 2)
                    pe.wait_ge(S["ahead"], n + 1)
                    gt(extra, k)
                    gate_up(extra, k, b, slots, [])
                    act_transposes(extra, k, b)
                    pe.wait_ge(S["o_act"], n + 2)
                    pe.wait_ge(S["o_dve"], n + 2)
                    down(extra, k, b, slots, [])

                gt(S, 0)
                passes(pe, l, S, first, body)
                pe.drain().then_inc(mlp_end, 1)

            def router(l, t):
                for k in range(KC):
                    last = pe.matmul(bank[0][:, NLOG * t:NLOG * t + NLOG], mem.hT[:, k, P * t:P * t + P],
                                     mem.wr[:, l, k, :], start=(k == 0), stop=(k == KC - 1))
                return last

            def mixer_to_experts(l):
                if l == 0:
                    pe.wait_ge(selectors_in, 16)
                    spread(l, 2, 0, (bank[6], bank[7])).then_inc(gate_ps, 1)
                    project(l, 0, (0, 1), (0,))
                    spread(l, 2, 1, (bank[4], bank[5])).then_inc(gate_ps, 1)
                    project(l, 0, (0, 1), (1,))
                pe.wait_ge(gate_sb, 4 * l + 2)
                spread(l, 4, 0, (bank[4], bank[5]))
                spread(l, 3, 0, (bank[6], bank[7])).then_inc(rows_ps, 1)
                project(l, 1, (2, 3))
                pe.wait_ge(proj_used, 6 * l + 2)
                project(l, 2, (0, 1), (0,))
                pe.wait_ge(norm_ready, 6 * l + 4)
                spread(l, 4, 1, (bank[4], bank[5]))
                spread(l, 3, 1, (bank[6], bank[7])).then_inc(rows_ps, 1)
                pe.wait_ge(proj_used, 6 * l + 4)
                turn(0, (2, 3))
                project(l, 2, (0, 1), (1,))
                pe.wait_ge(norm_ready, 6 * l + 5)
                wait_turn(pe, TURN_ROUTE[l], 0)
                turn(1, (2, 3))
                pe.wait_ge(router_in, 64)
                pe.wait_ge(proj_used, 6 * (l + 1))
                router(l, 0)
                wait_turn(pe, TURN_ROUTE[l], 1)
                router(l, 1)
                pe.wait_ge(norm_ready, 6 * l + 6)
                turn(2, (2, 3))
                spread(l, 5, 0, (bank[6], bank[7])).then_inc(gate_ps, 1)
                wait_turn(pe, TURN_ROUTE[l], 2)
                router(l, 2).then_inc(logits_ps, 1)
                spread(l, 5, 1, (bank[4], bank[5])).then_inc(gate_ps, 1)
                pe.wait_ge(msum_done, l + 1)
                for t in range(TILES):
                    for s in range(t + 1):
                        last = pe.matmul(bank[1][:, EXPERTS * t:EXPERTS * t + EXPERTS],
                                         mem.const("tri" if s == t else "ones"), mem.Msum[:, s, :],
                                         start=(s == 0), stop=(s == t))
                last.then_inc(pos_ps, 1)
                pe.wait_ge(gate_sb, 4 * l + 4)
                for s in range(TILES):
                    last = pe.matmul(bank[5][:, 0:EXPERTS], mem.const("ones"), mem.Msum[:, s, :],
                                     start=(s == 0), stop=(s == TILES - 1))
                last.then_inc(count_ps, 1)

            pe.wait_ge(head_sb, HEADS)
            mixer_to_experts(0)
            mlp(0)

            columns(1)
            pe.wait_ge(col_done, 2)

            def turn_tile(t):
                pe.wait_ge(norm_ready, 7 + t)
                turn(t, TURN_BANKS[1][t])

            def over_channels(t):
                wait_turn(pe, TURN_LN[1], t)
                for n in range(4 * t, 4 * t + 4):
                    if n >= 8:
                        pe.wait_ge(chan_act if n % 2 == 0 else chan_dve, (n - 8) // 2 + (5 if n % 2 == 0 else 1))
                    for i in range(2):
                        last = pe.matmul(bank[CHAN_BANKS[n]][:, 256 * i:256 * i + 256],
                                         mem.hT[:, 2 * (n % 4) + i, P * t:P * t + P], mem.dft[:, 0:256],
                                         start=True, stop=True)
                    last.then_inc(chan_ps, 1)

            pos_p = mem.dft[:, 256:512].rearrange("p (s n) -> p s n", s=2)
            pos_l = mem.dft[:, 512:].rearrange("p (t s n) -> p t s n", t=2, s=2)

            turn_tile(0)
            ada(AT["ada", 1, 8])
            pe.wait_ge(dft_in, 16)
            over_channels(0)
            ada(AT["ada", 1, 9])
            pe.wait_ge(chan_act, 4)
            for g in range(KC):
                for s in range(2):
                    last = pe.matmul(bank[(3, 4)[g // 4]][:, P * (g % 4):P * (g % 4) + P],
                                     mem.U[:, 0, g, P * s:P * s + P], pos_p[:, s, :], start=(s == 0), stop=(s == 1))
                if g % 4 == 3:
                    last.then_inc(four_ps, 1)
            spread(1, 2, 0, (bank[5], bank[6])).then_inc(gate_ps, 1)
            pe.wait_ge(four_sb, 2)
            project(1, 0, (0, 1), (0,))
            pe.wait_ge(gate_sb, 5)
            turn_tile(1)
            turn_tile(2)
            project(1, 0, (0, 1), (1,))
            for u in (10, 11):
                ada(AT["ada", 1, u])
            wait_turn(pe, TURN_LN[1], 2)
            over_channels(1)
            over_channels(2)
            pe.wait_ge(chan_act, 8)
            pe.wait_ge(chan_dve, 4)
            spread(1, 2, 1, (bank[4], bank[5])).then_inc(gate_ps, 1)
            pe.wait_ge(ada_done, 2 * ADA_UNITS)
            for g in range(KC):
                if g >= 2:
                    pe.wait_ge(four_sb, g + 1)
                for i, (t, s) in enumerate(((0, 0), (0, 1), (1, 0), (1, 1))):
                    last = pe.matmul(bank[(2, 7)[g % 2]][:, 0:2 * P], mem.U[:, 1 + t, g, P * s:P * s + P],
                                     pos_l[:, t, s, :], start=(i == 0), stop=(i == 3))
                last.then_inc(four_ps, 1)
            pe.wait_ge(four_sb, KC + 2)
            mixer_to_experts(1)
            mlp(1)

        @block.scalar
        def _(act):
            def head_evict(k):
                act.wait_ge(head_ps, k + 1)
                nc.scalar.copy(mem.hT[:, k, :], bank[k % 2][:, 0:TOK]).then_inc(head_sb, 1)

            def turn_evict(l, j, part=0):
                t = FIRST_TILES[j] if l == 0 else j
                i = 0 if t == 0 else 1
                src = bank[TURN_BANKS[l][j][part]]
                act.wait_ge(turn_ps, 2 * (TILES * TURN_LN[l] + j) + part + 1)
                for c in range(4):
                    last = nc.scalar.activation(mem.hT[:, 4 * part + c, P * t:P * t + P], src[:, P * c:P * c + P],
                                                ACT.Identity, bias=mem.col[:, 0, part, c, i:i + 1],
                                                scale=mem.col[:, 1, part, c, i:i + 1])
                last.then_inc((turn_lo, turn_hi)[part], 1)

            def gate_evict(n, i, banks):
                act.wait_ge(gate_ps, n)
                nc.scalar.copy(mem.gates[:, i, :], mem.psum[:, 512 * banks:512 * banks + D]).then_inc(gate_sb, 1)

            def load_norm(idx):
                if idx >= 1:
                    act.wait_ge(gb_used, idx)
                for i, name in enumerate(("ln_gain", "ln_bias")):
                    act.dma_start(mem.gb[:, i, :], A[name][idx // 2, idx % 2].partition_broadcast(P)).then_inc(gb_in, 16)

            for i, src in enumerate((A["c_ctx"].rearrange("(k p) -> k p", p=P),
                                     A["c"].rearrange("b (k p) -> (b k) p", p=P))):
                act.dma_start(mem.cond[KC * i:KC * i + KC, :], src).then_inc(cond_in, 16)
            act.wait_ge(zeroed, 2)
            for i in range(2):
                act.dma_start(mem.m[i:i + 97:32, :, :, :].rearrange("j l u n -> j (l u) n"),
                              A["b_ada"].rearrange("l (u j n) -> j (l u) n", u=ADA_UNITS, j=4)
                              ).then_inc(bias_in, 16)
            for n, name in enumerate(("lambda_q1", "lambda_k1", "lambda_q2", "lambda_k2")):
                act.dma_start(mem.lam[:, n, :], A[name][0].partition_broadcast(P)).then_inc(lam_in, 16)
            act.dma_start(mem.gain8[:, :], A["subln_gain"][0].partition_broadcast(P)).then_inc(lam_in, 16)
            act.wait_ge(cond_ps, 1)
            for i in range(2):
                nc.scalar.activation(mem.silu[:, :, i], bank[0][:, KC * i:KC * i + KC], ACT.Silu).then_inc(silu_done, 1)
            act.wait_ge(col_done, 1)
            for j in range(TILES):
                turn_evict(0, j)
            act.dma_start(mem.ctxk, A["cache_k"][0, 0].rearrange("s h d -> s (h d)")).then_inc(ctx_in, 16)
            act.dma_start(mem.ctxv, A["cache_v"][0, 0].rearrange("s h d -> s (h d)")).then_inc(ctx_in, 16)
            for l in range(2):
                act.dma_start(mem.wr[:, l, :, 0:GROUPS], A["w_router_group"][l].rearrange("(p k) n -> p k n", p=P)
                              ).then_inc(router_in, 16)
                act.dma_start(mem.wr[:, l, :, GROUPS:], A["w_router_expert"][l].rearrange("(p k) n -> p k n", p=P)
                              ).then_inc(router_in, 16)
            act.wait_ge(lam_prod, 2)
            nc.scalar.activation(mem.lams[:, 2:4], mem.lams[:, 0:2], ACT.Exp).then_inc(lam_done, 1)

            for u in range(5):
                for s in range(6):
                    g = 6 * (u - 1) + s
                    if u >= 1 and s % 3 == 0:
                        act.wait_ge(qkT_ps, g // 3 + 1)
                        nc.scalar.copy(mem.qT, bank[3][:, 0:TOK]).then_inc(qT_sb, 1)
                    if u >= 1:
                        w = P if g % 3 == 0 else TOK
                        act.wait_ge(nb_done, g + 1)
                        for j in range(2):
                            nc.scalar.activation(mem.p[g % 2][j][:, 0:w], bank[5 + j][:, 0:w], ACT.Exp,
                                                 bias=mem.nb[:, g % 2, j:j + 1], scale=SCALE,
                                                 accum_out=mem.ssum[:, g % 2, j:j + 1]).then_inc(exp_done, 1)
                    if u < 4:
                        i = 6 * u + s
                        t, half = FIRST_TILES[s // 2], s % 2
                        act.wait_ge(qkv_ps, i + 1)
                        if s == 0 and u >= 2:
                            act.wait_ge(pv_ps, 6 * (u - 1))
                            act.wait_ge(kv_stored[u % 2], 32)
                        nc.scalar.copy(mem.qkv[u % 2][:, t, 384 * half:384 * half + 384],
                                       bank[i % 2][:, 0:384]).then_inc(qkv_sb, 1)
                    else:
                        head_evict(s)
            head_evict(6)
            head_evict(7)

            def gt_evict(S, n, b):
                act.wait_ge(S["gt_ps"], n + 1)
                nc.scalar.copy(mem.GT[b][:, 0:4, :], bank[2].rearrange("p (c s) -> p c s", c=4)
                               ).then_inc(S["gt_act"], 1)

            def silu(S, n, b):
                act.wait_ge(S["u_ps"], n + 1)
                nc.scalar.activation(mem.sil[b], bank[b][:, 0:FE], ACT.Silu).then_inc(S["sil"], 1)

            def o_evict(S, n, b):
                act.wait_ge(S["d_ps"], n + 1)
                act.wait_ge(S["o_free"], n + 1)
                nc.scalar.copy(mem.O[b][:, 0:512], bank[5]).then_inc(S["o_act"], 1)

            further[act] = act.alloc_register("further")
            act.reg_mov(further[act], 0)
            act.sem_inc(extra["o_act"], 1)

            def expert_input(l):
                for t in range(TILES):
                    for part, done in enumerate((turn_lo, turn_hi)):
                        act.wait_ge(turn_ps, 2 * (TILES * TURN_ROUTE[l] + t) + part + 1)
                        nc.scalar.copy(mem.hT[:, 4 * part:4 * part + 4, P * t:P * t + P],
                                       bank[2 + part].rearrange("p (c s) -> p c s", c=4)).then_inc(done, 1)
                act.wait_ge(route_in, 2 * l + 1)
                nc.scalar.activation(mem.r12[1], mem.r12[0], ACT.Exp).then_inc(route_out, 1)
                act.wait_ge(route_in, 2 * l + 2)
                nc.scalar.activation(mem.r3[:, 6], mem.r3[:, 5], ACT.Exp).then_inc(route_out, 1)
                for i in range(2):
                    gate_evict(4 * l + 3 + i, i, (6, 4)[i])
                load_norm(2 * l + 1)
                act.wait_ge(ids_out, 96 * (l + 1))
                act.dma_start(mem.table[:, 0:PASSES * PAIRS].rearrange("p (r n) -> p r n", r=PASSES),
                              t_dram[l].rearrange("(r p n) o -> p r (n o)", r=PASSES, p=P)).then_inc(table_in, 16)

            def mlp(l):
                S = main[l]
                act.sem_inc(S["o_act"], 1)

                def first(n, b, it):
                    silu(S, n, b)
                    gt_evict(S, n + 1, 1 - b)
                    o_evict(S, n, b)

                def body(n, b, r, k):
                    gt_evict(extra, k, b)
                    silu(extra, k, b)
                    o_evict(extra, k, b)

                gt_evict(S, 0, 0)
                passes(act, l, S, first, body)
                act.wait_ge(S["gt_dve"], PAIRS + 1)
                act.wait_ge(S["o_free"], PAIRS + 2)
                for t in range(TILES):
                    act.dma_start(mem.Y[:, t, :, :], y_dram[l].rearrange("(k t p) n -> t p k n", k=2, p=P)[t]
                                  ).then_inc(y_in[t], 16)
                if l == 0:
                    act.dma_start(mem.dft, A["k_dft"]).then_inc(dft_in, 16)
                for t in range(TILES):
                    act.wait_ge(y_in[t], 16 * (l + 1))
                    nc.scalar.activation(mem.Y[:, t, 0, :], mem.Y[:, t, 0, :], ACT.Copy,
                                         scale=mem.w[:, 0, t:t + 1]).then_inc(y_scaled, 1)

            load_norm(0)
            gate_evict(1, 0, 6)
            gate_evict(2, 1, 4)
            expert_input(0)
            mlp(0)
            act.wait_ge(col_done, 2)
            def chan_evict(n):
                act.wait_ge(chan_ps, n + 1)
                nc.scalar.copy(mem.U[:, n // 4, 2 * (n % 4):2 * (n % 4) + 2, :],
                               bank[CHAN_BANKS[n]].rearrange("p (g n) -> p g n", g=2)).then_inc(chan_act, 1)

            for part in range(2):
                turn_evict(1, 0, part)
            for n in range(4):
                chan_evict(n)
            for part in range(2):
                act.wait_ge(four_ps, part + 1)
                nc.scalar.copy(mem.hT[:, 4 * part:4 * part + 4, 0:P],
                               bank[(3, 4)[part]].rearrange("p (g n) -> p g n", g=4)).then_inc(four_sb, 1)
            gate_evict(5, 0, 5)
            turn_evict(1, 1)
            turn_evict(1, 2)
            for n in range(4, 4 * TILES, 2):
                chan_evict(n)
            load_norm(2)
            gate_evict(6, 1, 4)
            for g in range(KC):
                act.wait_ge(four_ps, g + 3)
                nc.scalar.copy(mem.hT[:, g, P:TOK], bank[(2, 7)[g % 2]][:, 0:2 * P]).then_inc(four_sb, 1)
            expert_input(1)
            mlp(1)
            for t in range(TILES):
                act.wait_ge(x_done, t + 1)
                dst = A["y_prompt"][0] if t == 0 else A["y_sample"][0][(t - 1) * P:t * P, :]
                act.dma_start(dst, mem.x[:, t, :]).then_inc(out_done, 16)
            act.wait_ge(out_done, 16 * TILES)

        @block.vector
        def _(dve):
            V = nc.vector
            chain = [0]
            ada_count = [0]

            def mark(ins):
                chain[0] += 1
                ins.then_inc(dve_chain, 1)
                return chain[0]

            def link(ins):
                dve.wait_ge(dve_chain, mark(ins))

            def inverse_sqrt(y, tiles=slice(0, TILES)):
                v, t = mem.rs_v[:, tiles], mem.rs_t[:, tiles]
                link(V.tensor_scalar(t.bitcast(I32), v.bitcast(I32), 1, None, ALU.logical_shift_right))
                link(V.tensor_scalar(y.bitcast(I32), t.bitcast(I32), -1.0, float(0x5F3759DF), ALU.mult, ALU.add))
                for _ in range(3):
                    link(V.tensor_tensor(t, y, y, ALU.mult))
                    link(V.scalar_tensor_tensor(out=t, in0=t, scalar=-0.5, in1=v, op0=ALU.mult, op1=ALU.mult))
                    link(V.scalar_tensor_tensor(out=y, in0=t, scalar=1.5, in1=y, op0=ALU.add, op1=ALU.mult))

            def tile_stats(t):
                for i in range(2):
                    last = V.bn_stats(mem.stats[:, t, i, :], mem.x[:, t, 512 * i:512 * i + 512])
                return last

            def finish_stats(last, tiles=range(TILES)):
                part = slice(tiles[0], tiles[-1] + 1)
                link(last)
                for t in tiles:
                    last = V.bn_aggr(mem.mv[:, t, :], mem.stats[:, t, :, :].rearrange("p i n -> p (i n)"))
                link(last)
                link(V.tensor_scalar(mem.rs_v[:, part], mem.mv[:, part, 1], EPS, None, ALU.add))
                inverse_sqrt(mem.rstd[:, part], part)

            def normalised(tiles=range(TILES)):
                for t in tiles:
                    V.tensor_scalar(mem.h[:, t, :], mem.x[:, t, :], mem.mv[:, t, 0:1], mem.rstd[:, t:t + 1],
                                    ALU.subtract, ALU.mult).then_inc(norm_ready, 1)

            def ada_add(n):
                l, u = UNITS[n][1:]
                src = bank[ada_bank(n)][:, 0:P]
                ada_count[0] += 1
                dve.wait_ge(ada_ps, ada_count[0])
                V.scalar_tensor_tensor(out=mem.m[:, l, u, :], in0=mem.m[:, l, u, :],
                                       scalar=1.0 if u // 2 in (1, 4) else 0.0, in1=src,
                                       op0=ALU.add, op1=ALU.add).then_inc(ada_done, 1)

            def columns(l):
                dve.wait_ge(col_ps, l + 1)
                V.tensor_copy(mem.col[:, :, :, :, :].rearrange("p s u j i -> p (s u j) i"),
                              bank[3].rearrange("p (c r) -> p c r", r=32)[:, :, 0:2]).then_inc(col_done, 1)

            def turn_evict(l, j):
                t = FIRST_TILES[j] if l == 0 else j
                i = 0 if t == 0 else 1
                src = bank[TURN_BANKS[l][j][1]]
                dve.wait_ge(turn_ps, 2 * (TILES * TURN_LN[l] + j) + 2)
                for c in range(4):
                    last = V.tensor_scalar(mem.hT[:, 4 + c, P * t:P * t + P], src[:, P * c:P * c + P],
                                           mem.col[:, 1, 1, c, i:i + 1], mem.col[:, 0, 1, c, i:i + 1],
                                           ALU.mult, ALU.add)
                last.then_inc(turn_hi, 1)

            dve.wait_ge(x_in, 48)
            for t in range(TILES):
                last = tile_stats(t)
            finish_stats(last)
            normalised()
            dve.wait_ge(bias_in, 16 * 2)
            for u in range(4):
                ada_add(AT["ada", 0, u])
            columns(0)
            dve.wait_ge(col_done, 1)
            for j in range(TILES):
                turn_evict(0, j)

            dve.wait_ge(lam_in, 16 * 5)
            for i in range(2):
                V.tensor_tensor_reduce(out=mem.lamtmp, in0=mem.lam[:, 2 * i, :], in1=mem.lam[:, 2 * i + 1, :],
                                       scale=1.0, scalar=0.0, op0=ALU.mult, op1=ALU.add,
                                       accum_out=mem.lams[:, i:i + 1]).then_inc(lam_prod, 1)
                dve.wait_ge(lam_prod, i + 1)
            link(V.tensor_scalar(mem.gain8[:, :], mem.gain8[:, :], 1.0 - LAM_INIT, None, ALU.mult))
            dve.wait_ge(lam_done, 1)
            link(V.tensor_tensor(mem.lams[:, 4:5], mem.lams[:, 3:4], mem.lams[:, 2:3], ALU.subtract))
            link(V.tensor_scalar(mem.lams[:, 5:6], mem.lams[:, 4:5], -LAM_INIT, None, ALU.add))
            neg_lam = mem.lams[:, 5:6]

            def maximum(g):
                w = P if g % 3 == 0 else TOK
                dve.wait_ge(score_ps, g + 1)
                for j in range(2):
                    last = V.reduce_max(mem.mx[:, g % 2, j:j + 1], bank[5 + j][:, 0:w], AX)
                link(last)
                V.tensor_scalar(mem.nb[:, g % 2, :], mem.mx[:, g % 2, :], -SCALE, None, ALU.mult).then_inc(nb_done, 1)

            def difference(g):
                w = P if g % 3 == 0 else TOK
                dve.wait_ge(exp_done, 2 * g + 2)
                link(V.reciprocal(mem.rsum[:, g % 2, :], mem.ssum[:, g % 2, :]))
                link(V.scalar_tensor_tensor(out=mem.ratio[:, g % 2:g % 2 + 1], in0=mem.rsum[:, g % 2, 1:2],
                                            scalar=mem.ssum[:, g % 2, 0:1], in1=neg_lam, op0=ALU.mult, op1=ALU.mult))
                p0, p1 = mem.p[g % 2]
                V.scalar_tensor_tensor(out=p0[:, 0:w], in0=p1[:, 0:w], scalar=mem.ratio[:, g % 2:g % 2 + 1],
                                       in1=p0[:, 0:w], op0=ALU.mult, op1=ALU.add).then_inc(pd_done, 1)

            def pdT_evict(g):
                w = P if g % 3 == 0 else TOK
                dve.wait_ge(pdT_ps, g + 1)
                V.tensor_copy(mem.pdT[g % 2][:, 0:w], bank[7][:, 0:w]).then_inc(pdT_sb, 1)

            def head_norm(g):
                head, t = g // 3, g % 3
                o = mem.h[:, t, P * head:P * head + P]
                dve.wait_ge(pv_ps, g + 1)
                V.tensor_scalar(o, bank[2][:, 0:P], mem.rsum[:, g % 2, 0:1], None, ALU.mult
                                ).then_inc(o_raw, 1)
                dve.wait_ge(o_raw, g + 1)
                link(V.tensor_tensor_reduce(out=mem.sq[:, :], in0=o, in1=o, scale=1.0 / P, scalar=0.0,
                                            op0=ALU.mult, op1=ALU.add, accum_out=mem.ss[:, t:t + 1]))
                if t == TILES - 1:
                    link(V.tensor_scalar(mem.rs_v[:, :], mem.ss[:, :], EPS, None, ALU.add))
                    inverse_sqrt(mem.rs_y[:, :])
                    for i in range(TILES):
                        oi = mem.h[:, i, P * head:P * head + P]
                        V.scalar_tensor_tensor(out=oi, in0=oi, scalar=mem.rs_y[:, i:i + 1], in1=mem.gain8[:, :],
                                               op0=ALU.mult, op1=ALU.mult).then_inc(o_done, 1)

            for u in range(5):
                between = [AT[unit] for unit in BETWEEN[u]]
                for s in range(6):
                    g = 6 * (u - 1) + s
                    if u >= 1:
                        if s % 3 == 0:
                            dve.wait_ge(qkT_ps, g // 3 + 1)
                            V.tensor_copy(mem.kT, bank[4]).then_inc(kT_sb, 1)
                        maximum(g)
                    if g >= 1:
                        pdT_evict(g - 1)
                    if u >= 1:
                        difference(g)
                    if s in SPOTS[len(between)]:
                        ada_add(between[SPOTS[len(between)].index(s)])
                    if g >= 1:
                        head_norm(g - 1)
            pdT_evict(STEPS - 1)
            head_norm(STEPS - 1)
            for unit in BETWEEN[5]:
                ada_add(AT[unit])

            def post_norm(idx, last, tiles):
                finish_stats(last, tiles)
                dve.wait_ge(gb_in, 32 * (idx + 1))
                for t in tiles:
                    last = mark(V.scalar_tensor_tensor(out=mem.x[:, t, :], in0=mem.x[:, t, :],
                                                       scalar=mem.mv[:, t, 0:1], in1=mem.gb[:, 0, :],
                                                       op0=ALU.subtract, op1=ALU.mult))
                shifted = {}
                for j, t in enumerate(tiles):
                    dve.wait_ge(dve_chain, last - len(tiles) + 1 + j)
                    ins = V.scalar_tensor_tensor(out=mem.x[:, t, :], in0=mem.x[:, t, :],
                                                 scalar=mem.rstd[:, t:t + 1], in1=mem.gb[:, 1, :],
                                                 op0=ALU.mult, op1=ALU.add)
                    if idx == 3:
                        ins.then_inc(x_done, 1)
                    elif t == TILES - 1:
                        ins.then_inc(gb_used, 1)
                    else:
                        shifted[t] = mark(ins)
                if idx == 3:
                    return None
                for t in tiles:
                    if t in shifted:
                        dve.wait_ge(dve_chain, shifted[t])
                    else:
                        dve.wait_ge(gb_used, idx + 1)
                    last = tile_stats(t)
                return last

            def mixer_to_experts(l):
                for t in range(TILES):
                    i = 0 if t == 0 else 1
                    x, tmp = mem.x[:, t, :], mem.tmp[:, t, :]
                    mean, rstd = mem.mv[:, t, 0:1], mem.rstd[:, t:t + 1]
                    dve.wait_ge(gate_sb, 4 * l + 1 + i)
                    for half in range(2):
                        n, part = 6 * l + 2 * t + half + 1, slice(512 * half, 512 * half + 512)
                        dve.wait_ge(proj_ps, n)
                        V.tensor_tensor(tmp[:, part], bank[(2 if t == 1 else 0) + half],
                                        mem.gates[:, i, part], ALU.mult).then_inc(proj_used, 1)
                        dve.wait_ge(proj_used, n)
                        link(V.scalar_tensor_tensor(out=x[:, part], in0=x[:, part], scalar=ALPHA,
                                                    in1=tmp[:, part], op0=ALU.mult, op1=ALU.add))
                        last = V.bn_stats(mem.stats[:, t, half, :], x[:, part])
                    finish_stats(last, [t])
                    if t == 0:
                        dve.wait_ge(gb_in, 32 * (2 * l + 1))
                    link(V.scalar_tensor_tensor(out=x, in0=x, scalar=mean, in1=mem.gb[:, 0, :],
                                                op0=ALU.subtract, op1=ALU.mult))
                    shifted = V.scalar_tensor_tensor(out=x, in0=x, scalar=rstd, in1=mem.gb[:, 1, :],
                                                     op0=ALU.mult, op1=ALU.add)
                    if t < TILES - 1:
                        link(shifted)
                    else:
                        shifted.then_inc(gb_used, 1)
                        dve.wait_ge(gb_used, 2 * l + 1)
                    finish_stats(tile_stats(t), [t])
                    dve.wait_ge(rows_ps, 2 * l + 1 + i)
                    link(V.scalar_tensor_tensor(out=tmp, in0=x, scalar=mean, in1=mem.psum[:, 2048:2048 + D],
                                                op0=ALU.subtract, op1=ALU.mult))
                    V.scalar_tensor_tensor(
                        out=mem.h[:, t, :].rearrange("p (c k) -> p k c", c=KC),
                        in0=tmp.rearrange("p (k c) -> p k c", c=KC), scalar=rstd,
                        in1=mem.psum[:, 2048 + D:2048 + 2 * D].rearrange("p (k c) -> p k c", c=KC),
                        op0=ALU.mult, op1=ALU.add).then_inc(norm_ready, 1)
                route(l)

            def first_true(dst, tmp, eq, n, top):
                shape = [P, TILES, n]
                w = mem.const("descend")[:, 8 - n:8].unsqueeze(1)
                link(V.tensor_tensor(tmp, eq, bc(w, shape), ALU.mult))
                link(V.tensor_reduce(top, tmp, AX, ALU.max))
                link(V.tensor_tensor(dst, tmp, bc(top.unsqueeze(2), shape), ALU.is_equal))

            def select(S, n, place, signals=("sel_first", "sel")):
                for t in range(TILES):
                    last = V.tensor_scalar(mem.sel[:, t, :], mem.const("rowcode"), place[:, t:t + 1], None, ALU.is_equal)
                last.then_inc(S[signals[0]], 1)
                dve.wait_ge(S[signals[0]], n + 1)
                for t in range(TILES):
                    last = V.scalar_tensor_tensor(out=mem.sel[:, t, :], in0=mem.const("rowcode"),
                                                  scalar=place[:, TILES + t:TILES + t + 1], in1=mem.sel[:, t, :],
                                                  op0=ALU.is_equal, op1=ALU.add)
                last.then_inc(S[signals[1]], 1)

            def route(l):
                r3, r12, r24 = mem.r3, mem.r12, mem.r24
                s4, s8, s32 = [P, TILES, GROUPS], [P, TILES, PER_GROUP], [P, TILES, GROUPS, PER_GROUP]
                dve.wait_ge(logits_ps, l + 1)
                link(V.tensor_copy(mem.L.rearrange("p t n -> p (t n)"), bank[0][:, 0:TILES * NLOG]))
                lg = mem.L[:, :, 0:GROUPS]
                le = mem.L[:, :, GROUPS:].rearrange("p t (g e) -> p t g e", g=GROUPS)
                link(V.tensor_reduce(r3[:, 0], lg, AX, ALU.max))
                V.tensor_tensor(r12[0], lg, bc(r3[:, 0].unsqueeze(2), s4), ALU.subtract).then_inc(route_in, 1)
                link(V.tensor_tensor(r12[2], lg, bc(r3[:, 0].unsqueeze(2), s4), ALU.is_equal))
                first_true(r12[2], r12[3], r12[2], GROUPS, r3[:, 1])
                group = r12[2]
                link(V.tensor_tensor(mem.r96, le, bc(group.unsqueeze(3), s32), ALU.mult))
                link(V.tensor_reduce(r24[0], mem.r96.rearrange("p t g e -> p t e g"), AX, ALU.add))
                link(V.tensor_reduce(r3[:, 2], r24[0], AX, ALU.max))
                link(V.tensor_tensor(r24[1], r24[0], bc(r3[:, 2].unsqueeze(2), s8), ALU.is_equal))
                first_true(r24[2], r24[3], r24[1], PER_GROUP, r3[:, 3])
                link(V.scalar_tensor_tensor(out=r24[4], in0=r24[2], scalar=-3.0e38, in1=r24[0],
                                            op0=ALU.mult, op1=ALU.add))
                link(V.tensor_reduce(r3[:, 4], r24[4], AX, ALU.max))
                V.tensor_tensor(r3[:, 5], r3[:, 4], r3[:, 2], ALU.subtract).then_inc(route_in, 1)
                link(V.tensor_tensor(r24[5], r24[4], bc(r3[:, 4].unsqueeze(2), s8), ALU.is_equal))
                first_true(r24[6], r24[7], r24[5], PER_GROUP, r3[:, 7])
                for k, one in enumerate((r24[2], r24[6])):
                    for g in range(GROUPS):
                        last = V.tensor_tensor(mem.M[k][:, :, PER_GROUP * g:PER_GROUP * g + PER_GROUP], one,
                                               bc(group[:, :, g:g + 1], s8), ALU.mult)
                link(last)
                V.tensor_tensor(mem.Msum, mem.M[0], mem.M[1], ALU.add).then_inc(msum_done, 1)
                dve.wait_ge(route_out, 2 * l + 2)
                link(V.tensor_reduce(r3[:, 8], r12[1], AX, ALU.add))
                link(V.tensor_scalar(r3[:, 9], r3[:, 6], 1.0, None, ALU.add))
                link(V.tensor_tensor(r3[:, 10], r3[:, 8], r3[:, 9], ALU.mult))
                link(V.reciprocal(mem.w[:, 0, :], r3[:, 10]))
                link(V.tensor_tensor(mem.w[:, 1, :], mem.w[:, 0, :], r3[:, 6], ALU.mult))
                dve.wait_ge(pos_ps, l + 1)
                pos = bank[1][:, 0:TILES * EXPERTS]
                base = bc(mem.const("slotbase").unsqueeze(1), [P, TILES, EXPERTS])
                for i, what in enumerate((pos.rearrange("p (t e) -> p t e", t=TILES), base)):
                    for k in range(2):
                        last = V.tensor_tensor(mem.Mt[:, TILES * k:TILES * k + TILES, :], mem.M[k], what, ALU.mult)
                    link(last)
                    link(V.tensor_reduce(mem.r6[:, i], mem.Mt, AX, ALU.add))
                link(V.tensor_tensor(mem.r30, bc(mem.r6[:, 0].unsqueeze(2), [P, 6, PASSES - 1]),
                                     bc(mem.const("thresholds").unsqueeze(1), [P, 6, PASSES - 1]), ALU.is_ge))
                link(V.tensor_reduce(mem.r6[:, 2], mem.r30, AX, ALU.add))
                link(V.scalar_tensor_tensor(out=mem.r6[:, 3], in0=mem.r6[:, 0], scalar=float(PAIRS), in1=mem.r6[:, 1],
                                            op0=ALU.mult, op1=ALU.add))
                link(V.scalar_tensor_tensor(out=mem.r6[:, 4], in0=mem.r6[:, 2], scalar=float(PAIRS * CAP),
                                            in1=mem.r6[:, 3], op0=ALU.mult, op1=ALU.add))
                V.tensor_copy(mem.slot[:, :], mem.r6[:, 4]).then_inc(slot_done, 1)
                link(V.tensor_copy(mem.place[:, :], mem.r6[:, 4]))
                select(main[l], 0, mem.place)
                dve.wait_ge(count_ps, l + 1)
                counts = bank[5][:, 0:EXPERTS].rearrange("p (n e) -> p n e", e=2)
                link(V.tensor_reduce(mem.pairmax, counts, AX, ALU.max))
                s80 = [P, PAIRS, PASSES - 1]
                link(V.tensor_tensor(mem.r80, bc(mem.pairmax.unsqueeze(2), s80), bc(mem.const("thresholds").unsqueeze(1), s80),
                                     ALU.is_gt))
                link(V.tensor_reduce(mem.further, mem.r80, AX, ALU.add))
                link(V.tensor_tensor(mem.further, mem.further, mem.const("octal"), ALU.mult))
                link(V.tensor_reduce(mem.words_f[:, :], mem.further.rearrange("p (h n) -> p h n", h=2), AX, ALU.add))
                V.tensor_copy(mem.words[:, :], mem.words_f[:, :]).then_inc(words_done, 1)

            def gt_evict(S, n, b):
                dve.wait_ge(S["gt_ps"], n + 1)
                V.tensor_copy(mem.GT[b][:, 4:8, :], bank[3].rearrange("p (c s) -> p c s", c=4)
                              ).then_inc(S["gt_dve"], 1)

            def up_times(S, n, b):
                dve.wait_ge(S["sil"], n + 1)
                V.tensor_tensor(mem.act[b], mem.sil[b], bank[b][:, FE:2 * FE], ALU.mult).then_inc(S["act"], 1)

            def at_evict(S, n, b):
                dve.wait_ge(S["at_ps"], n + 1)
                V.tensor_copy(mem.actT[b], bank[4][:, 0:2 * P].rearrange("p (f s) -> p f s", f=2)
                              ).then_inc(S["at_sb"], 1)

            def o_evict(S, n, b):
                dve.wait_ge(S["d_ps"], n + 1)
                dve.wait_ge(S["o_free"], n + 1)
                V.tensor_copy(mem.O[b][:, 512:D], bank[6]).then_inc(S["o_dve"], 1)

            further[dve] = dve.alloc_register("further")
            dve.reg_mov(further[dve], 0)
            dve.sem_inc(extra["o_dve"], 1)
            dve.sem_inc(extra["sel"], 1)
            dve.sem_inc(gate_up_through, 1)
            dve.sem_inc(down_through, 1)

            def mlp(l):
                S = main[l]
                dve.sem_inc(S["o_dve"], 1)

                def first(n, b, it):
                    V.tensor_scalar(mem.place_x[:, :], mem.place[:, :], -float(PAIRS * P), None, ALU.add)
                    V.tensor_scalar(mem.place[:, :], mem.place[:, :], -1.0, None, ALU.add).then_inc(S["place"], 1)
                    dve.wait_ge(S["place"], n + 1)
                    select(S, n + 1, mem.place)
                    up_times(S, n, b)
                    gt_evict(S, n + 1, 1 - b)
                    at_evict(S, n, b)
                    select(S, n, mem.place_x, ("ahead_first", "ahead"))
                    dve.wait_ge(S["ahead"], n + 1)
                    o_evict(S, n, b)

                def body(n, b, r, k):
                    gt_evict(extra, k, b)
                    up_times(extra, k, b)
                    dve.sem_inc(gate_up_through, 1)
                    at_evict(extra, k, b)
                    V.tensor_scalar(mem.place_x[:, :], mem.place_x[:, :], -float(PAIRS * P), None, ALU.add
                                    ).then_inc(extra["place"], 1)
                    dve.wait_ge(extra["place"], k + 1)
                    select(extra, k, mem.place_x)
                    dve.wait_ge(extra["sel"], k + 2)
                    o_evict(extra, k, b)
                    dve.sem_inc(down_through, 1)

                gt_evict(S, 0, 0)
                passes(dve, l, S, first, body)

            def combine(l, tiles):
                y = mem.Y
                summed, gated, out = ([None] * TILES for _ in range(3))

                def add_second(t):
                    dve.wait_ge(y_scaled, TILES * l + t + 1)
                    summed[t] = mark(V.scalar_tensor_tensor(out=y[:, t, 0, :], in0=y[:, t, 1, :],
                                                            scalar=mem.w[:, 1, t:t + 1], in1=y[:, t, 0, :],
                                                            op0=ALU.mult, op1=ALU.add))

                def gate(t):
                    dve.wait_ge(dve_chain, summed[t])
                    gated[t] = mark(V.tensor_tensor(y[:, t, 0, :], y[:, t, 0, :],
                                                    mem.gates[:, 0 if t == 0 else 1, :], ALU.mult))

                def onto(t):
                    dve.wait_ge(dve_chain, gated[t])
                    out[t] = mark(V.scalar_tensor_tensor(out=mem.x[:, t, :], in0=mem.x[:, t, :], scalar=ALPHA,
                                                         in1=y[:, t, 0, :], op0=ALU.mult, op1=ALU.add))

                def sums(t):
                    dve.wait_ge(dve_chain, out[t])
                    return tile_stats(t)

                for step in (add_second, gate, onto):
                    for t in tiles:
                        step(t)
                for t in tiles:
                    last = sums(t)
                return post_norm(2 * l + 1, last, tiles)

            for b in range(2):
                dve.wait_ge(kv_stored[b], 64)
            mixer_to_experts(0)
            mlp(0)
            columns(1)
            for tiles in ([0], [1, 2]):
                finish_stats(combine(0, tiles), tiles)
                normalised(tiles)
            for u in (8, 9):
                ada_add(AT["ada", 1, u])
            dve.wait_ge(col_done, 2)
            turn_evict(1, 1)
            turn_evict(1, 2)
            for u in (10, 11):
                ada_add(AT["ada", 1, u])
            for n in range(5, 4 * TILES, 2):
                dve.wait_ge(chan_ps, n + 1)
                V.tensor_copy(mem.U[:, n // 4, 2 * (n % 4):2 * (n % 4) + 2, :],
                              bank[CHAN_BANKS[n]].rearrange("p (g n) -> p g n", g=2)).then_inc(chan_dve, 1)
            mixer_to_experts(1)
            mlp(1)
            for tiles in ([0], [1, 2]):
                combine(1, tiles)


_INS = ["x_prompt", "x_sample", "cache_k", "cache_v", "c", "c_ctx", "w_ada", "b_ada", "ln_gain", "ln_bias", "w_qkv",
        "w_attn_out", "lambda_q1", "lambda_k1", "lambda_q2", "lambda_k2", "subln_gain", "w_fourier_out",
        "w_router_group", "w_router_expert", "w_expert_gate", "w_expert_up", "w_expert_down"]
_OUTS = [("y_prompt", (1, P, D)), ("y_sample", (1, 2 * P, D)), ("new_cache_k", (1, 1, P, HEADS, 2 * HD)),
         ("new_cache_v", (1, 1, P, HEADS, 2 * HD))]


def kernel(**inputs):
    import concourse.bacc as bacc
    from concourse.bass_utils import run_bass_kernel_spmd

    nc = bacc.Bacc("TRN2", target_bir_lowering=False, num_devices=1)
    arrays = {name: np.ascontiguousarray(inputs[name]) for name in _INS}
    arrays.update(constants())
    aps = {name: nc.dram_tensor(f"in_{name}", a.shape, mybir.dt.from_np(a.dtype), kind="ExternalInput").ap()
           for name, a in arrays.items()}
    for name, shape in _OUTS:
        aps[name] = nc.dram_tensor(f"out_{name}", shape, F32, kind="ExternalOutput").ap()
    build(nc, aps)
    r = run_bass_kernel_spmd(nc, [{f"in_{name}": a for name, a in arrays.items()}], core_ids=[0])
    return tuple(r.results[0][f"out_{name}"] for name, _ in _OUTS)
```
